# Optimizing a Trainium2 kernel written in Bass

```python
import math, functools
import jax, jax.numpy as jnp
from jax import lax
import numpy as np

D_MODEL = 1024
BATCH = 1
SEQ = 512
DEPTH = 2
DEC_BATCH = 8
DEC_SEQ = 1
PAST_LEN = 256
PAGE_SIZE = 128

N_EVEN = (DEPTH + 1) // 2
N_ODD = DEPTH // 2
H_A = 4
DK_A = 64
DV_A = 2 * DK_A
Q_BLOCK = 128
H_B = 4
DK_B = 64
DV_B = 128
MLSTM_CHUNK = 128
GATE_CAP = 15.0
D_RNN = 1280
N_BLK = 5
BW = D_RNN // N_BLK
CONV_W = 4
LRU_C = 8.0
D_FF = -(-8 * D_MODEL // (3 * 256)) * 256
ALPHA = (2.0 * DEPTH) ** 0.25
BETA = (8.0 * DEPTH) ** -0.25
ALIBI_SLOPES = np.array([2.0 ** (-8.0 * (h + 1) / H_A) for h in range(H_A)], np.float32)
EVEN_SIZES = [H_A * 2 * DK_A, H_A * 2 * DK_A, H_A * DV_A, H_B * DK_B, H_B * DK_B, H_B * DV_B, H_B * DV_B, H_B, H_B]
EVEN_SPLITS = np.cumsum(EVEN_SIZES)[:-1].tolist()
P_EVEN = sum(EVEN_SIZES)
D_MIX_EVEN = H_A * DV_A + H_B * DV_B

kernel_name = "hybrid_diffattn_mlstm_rglru_decoder_step"

def layer_norm(x, g, b, eps=1e-5):
    xf = x.astype(jnp.float32)
    mu = xf.mean(-1, keepdims=True)
    var = jnp.square(xf - mu).mean(-1, keepdims=True)
    return ((xf - mu) * lax.rsqrt(var + eps) * g + b).astype(x.dtype)

def rms_norm(x, g, eps=1e-5):
    xf = x.astype(jnp.float32)
    return (xf * lax.rsqrt(jnp.mean(xf * xf, -1, keepdims=True) + eps) * g).astype(x.dtype)

def diff_attn_prompt(q, k, v, lam):
    bsz, t_len = q.shape[:2]
    n_qb = t_len // Q_BLOCK
    qf = q.astype(jnp.float32) * (DK_A ** -0.5)
    kf = k.astype(jnp.float32)
    vf = v.astype(jnp.float32)
    q_blocks = qf.reshape(bsz, n_qb, Q_BLOCK, H_A, 2, DK_A).transpose(1, 0, 2, 3, 4, 5)
    k_pos = jnp.arange(t_len)
    slopes = jnp.asarray(ALIBI_SLOPES)[:, None, None, None]

    def one_block(args):
        q_blk, blk = args
        q_pos = blk * Q_BLOCK + jnp.arange(Q_BLOCK)
        dist = q_pos[:, None] - k_pos[None, :]
        s = jnp.einsum('bqhjd,bshjd->bhjqs', q_blk, kf)
        s = s - slopes * dist.astype(jnp.float32)
        s = jnp.where(dist >= 0, s, -jnp.inf)
        p = jax.nn.softmax(s, axis=-1)
        w = p[:, :, 0] - lam * p[:, :, 1]
        return jnp.einsum('bhqs,bshv->bqhv', w, vf)

    out = lax.map(one_block, (q_blocks, jnp.arange(n_qb)))
    return out.transpose(1, 0, 2, 3, 4).reshape(bsz, t_len, H_A, DV_A)

def diff_attn_sample(q, k_new, v_new, lam, k_past, v_past):
    past = k_past.shape[1]
    t_len = q.shape[1]
    qf = q.astype(jnp.float32) * (DK_A ** -0.5)
    slopes = jnp.asarray(ALIBI_SLOPES)[:, None, None, None]
    q_pos = past + jnp.arange(t_len)
    dist_past = (q_pos[:, None] - jnp.arange(past)[None, :]).astype(jnp.float32)
    dist_new = q_pos[:, None] - q_pos[None, :]
    s_past = jnp.einsum('bthjd,bshjd->bhjts', qf, k_past.astype(jnp.float32)) - slopes * dist_past
    s_new = jnp.einsum('bthjd,bshjd->bhjts', qf, k_new.astype(jnp.float32)) - slopes * dist_new.astype(jnp.float32)
    s_new = jnp.where(dist_new >= 0, s_new, -jnp.inf)
    p = jax.nn.softmax(jnp.concatenate([s_past, s_new], axis=-1), axis=-1)
    w = p[:, :, 0] - lam * p[:, :, 1]
    return (jnp.einsum('bhts,bshv->bthv', w[..., :past], v_past.astype(jnp.float32))
            + jnp.einsum('bhts,bshv->bthv', w[..., past:], v_new.astype(jnp.float32)))

def mlstm_chunk(carry, xs):
    c_prev, n_prev, m_prev = carry
    q, k, v, ig, lf = xs
    length = q.shape[2]
    b = jnp.cumsum(lf, axis=-1)
    causal = jnp.tril(jnp.ones((length, length), bool))
    d = jnp.where(causal, b[..., :, None] - b[..., None, :] + ig[..., None, :], -jnp.inf)
    inter = b + m_prev[..., None]
    m_t = jnp.maximum(inter, d.max(-1))
    w = jnp.exp(d - m_t[..., None])
    g_inter = jnp.exp(inter - m_t)
    s = jnp.einsum('bhtk,bhsk->bhts', q, k) * w
    num = jnp.einsum('bhts,bhsv->bhtv', s, v) + g_inter[..., None] * jnp.einsum('bhtk,bhvk->bhtv', q, c_prev)
    den = s.sum(-1) + g_inter * jnp.einsum('bhtk,bhk->bht', q, n_prev)
    h = num / jnp.maximum(jnp.abs(den), jnp.exp(-m_t))[..., None]
    g_tot = b[..., -1]
    dl = g_tot[..., None] - b + ig
    m_new = jnp.maximum(g_tot + m_prev, dl.max(-1))
    wl = jnp.exp(dl - m_new[..., None])
    decay = jnp.exp(g_tot + m_prev - m_new)
    c_new = decay[..., None, None] * c_prev + jnp.einsum('bhs,bhsv,bhsk->bhvk', wl, v, k)
    n_new = decay[..., None] * n_prev + jnp.einsum('bhs,bhsk->bhk', wl, k)
    return (c_new, n_new, m_new), h

def mlstm_sequence(q, k, v, ig, lf, c0, n0, m0, chunk):
    bsz, t_len = q.shape[:2]
    n_chunks = t_len // chunk

    def to_chunks(t):
        t = t.reshape((bsz, n_chunks, chunk) + t.shape[2:])
        return jnp.swapaxes(jnp.moveaxis(t, 1, 0), 2, 3)

    init = (c0.astype(jnp.float32), n0.astype(jnp.float32), m0.astype(jnp.float32))
    xs = (to_chunks(q), to_chunks(k), to_chunks(v), to_chunks(ig), to_chunks(lf))
    final, hs = lax.scan(mlstm_chunk, init, xs)
    hs = jnp.moveaxis(jnp.swapaxes(hs, 2, 3), 0, 1).reshape(bsz, t_len, H_B, DV_B)
    return hs, final

def causal_conv(x_ext, w, b):
    t_len = x_ext.shape[1] - (CONV_W - 1)
    y = b
    for j in range(CONV_W):
        y = y + w[j] * x_ext[:, j:j + t_len]
    return y

def linear_scan(a, b, h0):
    def combine(left, right):
        return left[0] * right[0], right[0] * left[1] + right[1]
    a_cum, b_cum = lax.associative_scan(combine, (a, b), axis=1)
    return a_cum * h0[:, None] + b_cum

def setup_inputs(seed: int = 0) -> dict:
    key = jax.random.key(seed)
    ks = iter(jax.random.split(key, 48))

    def nrm(shape, scale=1.0):
        return scale * jax.random.normal(next(ks), shape, jnp.float32)

    n_pages = PAST_LEN // PAGE_SIZE
    n_used = DEC_BATCH * n_pages
    n_pool = n_used + n_used // 4
    perm = jax.random.permutation(next(ks), n_pool)
    page_table = perm[:n_used].reshape(DEC_BATCH, n_pages).astype(jnp.int32)

    u_lru = jax.random.uniform(next(ks), (N_ODD, D_RNN), jnp.float32, 0.9, 0.999)
    a0 = u_lru ** (1.0 / LRU_C)
    lru_lambda = jnp.log(a0) - jnp.log1p(-a0)

    return {
        "x_prompt": nrm((BATCH, SEQ, D_MODEL)),
        "x_sample": nrm((DEC_BATCH, DEC_SEQ, D_MODEL)),
        "cache_k": nrm((N_EVEN, n_pool, PAGE_SIZE, H_A, 2, DK_A)),
        "cache_v": nrm((N_EVEN, n_pool, PAGE_SIZE, H_A, DV_A)),
        "state_C": nrm((N_EVEN, DEC_BATCH, H_B, DV_B, DK_B)),
        "state_n": nrm((N_EVEN, DEC_BATCH, H_B, DK_B)),
        "state_m": nrm((N_EVEN, DEC_BATCH, H_B)),
        "state_h": nrm((N_ODD, DEC_BATCH, D_RNN), 0.5),
        "state_conv": nrm((N_ODD, DEC_BATCH, CONV_W - 1, D_RNN)),
        "page_table": page_table,
        "c_prompt": nrm((BATCH, D_MODEL)),
        "c_sample": nrm((DEC_BATCH, D_MODEL)),
        "w_ada": nrm((DEPTH, D_MODEL, 6 * D_MODEL), 0.5 * D_MODEL ** -0.5),
        "b_ada": nrm((DEPTH, 6 * D_MODEL), 0.01),
        "ln_g": 1.0 + nrm((DEPTH, 2, D_MODEL), 0.01),
        "ln_b": nrm((DEPTH, 2, D_MODEL), 0.01),
        "w_in_even": nrm((N_EVEN, D_MODEL, P_EVEN), D_MODEL ** -0.5),
        "w_out_even": nrm((N_EVEN, D_MIX_EVEN, D_MODEL), BETA * D_MIX_EVEN ** -0.5),
        "lam": nrm((N_EVEN, 4, DK_A), 0.1),
        "attn_norm_g": 1.0 + nrm((N_EVEN, DV_A), 0.01),
        "mlstm_norm_g": 1.0 + nrm((N_EVEN, H_B, DV_B), 0.01),
        "b_i": nrm((N_EVEN, H_B), 0.1),
        "b_f": jax.random.uniform(next(ks), (N_EVEN, H_B), jnp.float32, 3.0, 6.0),
        "w_in_odd": nrm((N_ODD, D_MODEL, 2 * D_RNN), D_MODEL ** -0.5),
        "w_out_odd": nrm((N_ODD, D_RNN, D_MODEL), BETA * D_RNN ** -0.5),
        "conv_w": nrm((N_ODD, CONV_W, D_RNN), CONV_W ** -0.5),
        "conv_b": nrm((N_ODD, D_RNN), 0.01),
        "w_a": nrm((N_ODD, N_BLK, BW, BW), BW ** -0.5),
        "b_a": nrm((N_ODD, D_RNN), 0.01),
        "w_x": nrm((N_ODD, N_BLK, BW, BW), BW ** -0.5),
        "b_x": nrm((N_ODD, D_RNN), 0.01),
        "lru_lambda": lru_lambda,
        "w_ffn_in": nrm((DEPTH, D_MODEL, 2 * D_FF), D_MODEL ** -0.5),
        "w_ffn_out": nrm((DEPTH, D_FF, D_MODEL), BETA * D_FF ** -0.5),
    }

def reference(x_prompt, x_sample, cache_k, cache_v, state_C, state_n, state_m, state_h, state_conv, page_table,
              c_prompt, c_sample, w_ada, b_ada, ln_g, ln_b, w_in_even, w_out_even, lam, attn_norm_g, mlstm_norm_g,
              b_i, b_f, w_in_odd, w_out_odd, conv_w, conv_b, w_a, b_a, w_x, b_x, lru_lambda, w_ffn_in, w_ffn_out):
    f32 = jnp.float32

    def modulations(c, li):
        mod = jax.nn.silu(c) @ w_ada[li] + b_ada[li]
        return jnp.split(mod[:, None, :], 6, axis=-1)

    def post_norm(x, sub, gate, li, j):
        return layer_norm(ALPHA * x + (1.0 + gate) * sub, ln_g[li, j], ln_b[li, j])

    def even_mixer(u, li, attend, c0, n0, m0, chunk):
        e = li // 2
        bsz, t_len, _ = u.shape
        aq, ak, av, bq, bk, bv, bo, bi, bf = jnp.split(u @ w_in_even[e], EVEN_SPLITS, axis=-1)
        aq = aq.reshape(bsz, t_len, H_A, 2, DK_A)
        ak = ak.reshape(bsz, t_len, H_A, 2, DK_A)
        av = av.reshape(bsz, t_len, H_A, DV_A)
        lam_init = 0.8 - 0.6 * math.exp(-0.3 * li)
        lp = lam[e].astype(f32)
        lam_val = jnp.exp(jnp.sum(lp[0] * lp[1])) - jnp.exp(jnp.sum(lp[2] * lp[3])) + lam_init
        a_out = attend(aq, ak, av, lam_val)
        a_out = rms_norm(a_out, attn_norm_g[e]) * (1.0 - lam_init)
        q = bq.reshape(bsz, t_len, H_B, DK_B).astype(f32) * (DK_B ** -0.5)
        k = bk.reshape(bsz, t_len, H_B, DK_B).astype(f32)
        v = bv.reshape(bsz, t_len, H_B, DV_B).astype(f32)
        ig = GATE_CAP * jnp.tanh((bi + b_i[e]).astype(f32) / GATE_CAP)
        lf = jax.nn.log_sigmoid((bf + b_f[e]).astype(f32))
        h, (c_n, n_n, m_n) = mlstm_sequence(q, k, v, ig, lf, c0, n0, m0, chunk)
        h = rms_norm(h, mlstm_norm_g[e]) * jax.nn.sigmoid(bo.astype(f32)).reshape(bsz, t_len, H_B, DV_B)
        mixed = jnp.concatenate([a_out.reshape(bsz, t_len, -1), h.reshape(bsz, t_len, -1)], axis=-1).astype(u.dtype)
        return mixed @ w_out_even[e], ak, av, c_n, n_n, m_n

    def odd_mixer(u, li, h0, conv0):
        o = li // 2
        bsz, t_len, _ = u.shape
        g, xr = jnp.split(u @ w_in_odd[o], 2, axis=-1)
        x_ext = jnp.concatenate([conv0.astype(xr.dtype), xr], axis=1)
        xc = causal_conv(x_ext, conv_w[o], conv_b[o]).astype(f32)
        xb = xc.reshape(bsz, t_len, N_BLK, BW)
        r = jax.nn.sigmoid(jnp.einsum('btnc,ncd->btnd', xb, w_a[o].astype(f32)).reshape(bsz, t_len, D_RNN) + b_a[o])
        i = jax.nn.sigmoid(jnp.einsum('btnc,ncd->btnd', xb, w_x[o].astype(f32)).reshape(bsz, t_len, D_RNN) + b_x[o])
        log_a = -LRU_C * r * jax.nn.softplus(-lru_lambda[o].astype(f32))
        a = jnp.exp(log_a)
        b = jnp.sqrt(-jnp.expm1(2.0 * log_a)) * (i * xc)
        h = linear_scan(a, b, h0.astype(f32))
        y = (h.astype(u.dtype) * jax.nn.gelu(g)) @ w_out_odd[o]
        return y, h[:, -1], x_ext[:, -(CONV_W - 1):]

    def ffn(u, li):
        gate, up = jnp.split(u @ w_ffn_in[li], 2, axis=-1)
        return (jax.nn.silu(gate) * up) @ w_ffn_out[li]

    xp, xs = x_prompt, x_sample
    bp, bs = xp.shape[0], xs.shape[0]
    k_p, v_p, k_s, v_s = [], [], [], []
    cp_l, np_l, mp_l, cs_l, ns_l, ms_l = [], [], [], [], [], []
    hp_l, convp_l, hs_l, convs_l = [], [], [], []

    for li in range(DEPTH):
        mod_p = modulations(c_prompt, li)
        mod_s = modulations(c_sample, li)
        up = xp * (1.0 + mod_p[1]) + mod_p[0]
        us = xs * (1.0 + mod_s[1]) + mod_s[0]
        if li % 2 == 0:
            e = li // 2
            yp, akp, avp, c_n, n_n, m_n = even_mixer(
                up, li, diff_attn_prompt,
                jnp.zeros((bp, H_B, DV_B, DK_B), f32), jnp.zeros((bp, H_B, DK_B), f32), jnp.zeros((bp, H_B), f32),
                MLSTM_CHUNK)
            k_p.append(akp.reshape(bp, -1, PAGE_SIZE, H_A, 2, DK_A))
            v_p.append(avp.reshape(bp, -1, PAGE_SIZE, H_A, DV_A))
            cp_l.append(c_n); np_l.append(n_n); mp_l.append(m_n)
            k_past = cache_k[e, page_table].reshape(bs, -1, H_A, 2, DK_A)
            v_past = cache_v[e, page_table].reshape(bs, -1, H_A, DV_A)
            attend_s = functools.partial(diff_attn_sample, k_past=k_past, v_past=v_past)
            ys, aks, avs, c_n, n_n, m_n = even_mixer(us, li, attend_s, state_C[e], state_n[e], state_m[e], xs.shape[1])
            k_s.append(aks); v_s.append(avs)
            cs_l.append(c_n); ns_l.append(n_n); ms_l.append(m_n)
        else:
            o = li // 2
            yp, h_n, conv_n = odd_mixer(up, li, jnp.zeros((bp, D_RNN), f32), jnp.zeros((bp, CONV_W - 1, D_RNN), xp.dtype))
            hp_l.append(h_n); convp_l.append(conv_n)
            ys, h_n, conv_n = odd_mixer(us, li, state_h[o], state_conv[o])
            hs_l.append(h_n); convs_l.append(conv_n)
        xp = post_norm(xp, yp, mod_p[2], li, 0)
        xs = post_norm(xs, ys, mod_s[2], li, 0)
        up = xp * (1.0 + mod_p[4]) + mod_p[3]
        us = xs * (1.0 + mod_s[4]) + mod_s[3]
        xp = post_norm(xp, ffn(up, li), mod_p[5], li, 1)
        xs = post_norm(xs, ffn(us, li), mod_s[5], li, 1)

    k_prompt = jnp.stack(k_p)
    v_prompt = jnp.stack(v_p)
    k_sample = jnp.stack(k_s)
    v_sample = jnp.stack(v_s)
    C_prompt, n_prompt, m_prompt = jnp.stack(cp_l), jnp.stack(np_l), jnp.stack(mp_l)
    C_sample, n_sample, m_sample = jnp.stack(cs_l), jnp.stack(ns_l), jnp.stack(ms_l)
    h_prompt, conv_prompt = jnp.stack(hp_l), jnp.stack(convp_l)
    h_sample, conv_sample = jnp.stack(hs_l), jnp.stack(convs_l)
    return (xp, xs, k_prompt, v_prompt, k_sample, v_sample, C_prompt, n_prompt, m_prompt,
            C_sample, n_sample, m_sample, h_prompt, conv_prompt, h_sample, conv_sample)


_drawn_inputs = setup_inputs


def setup_inputs(seed=0):
    import zlib

    import numpy as np

    out = dict(_drawn_inputs(seed))
    spreads = {}
    factors = {'ln_g': 2.728,
     'lam': 2.701,
     'attn_norm_g': 32.105,
     'mlstm_norm_g': 64.0,
     'b_a': 52.602,
     'b_x': 23.423,
     'ln_b': 4.361,
     'conv_b': 8.0}
    for name, (base, spread) in spreads.items():
        noise = np.random.default_rng([zlib.crc32(name.encode()), seed]).standard_normal(out[name].shape)
        drawn = base * np.exp(spread * noise) if base else spread * noise
        out[name] = __import__('jax').numpy.asarray(drawn.astype(out[name].dtype))
    for name, factor in factors.items():
        out[name] = (out[name] * factor).astype(out[name].dtype)
    return out
```

```python
from contextlib import ExitStack
import math

import numpy as np
import concourse.bass as bass
from concourse import mybir

F32 = mybir.dt.float32
F32R = mybir.dt.float32r
I32 = mybir.dt.int32
ACT = mybir.ActivationFunctionType
ALU = mybir.AluOpType
AX = mybir.AxisListType

P = 128
D = 1024
KD = D // P
SEQ = 512
NS = 8
HALF = 256
HS = NS // 2
HT = HALF + HS
H = 4
DK = 64
DV = 128
DR = 1280
KR = DR // P
DFF = 2816
KF = DFF // P
KH = KF // 2
PAGE = 128
NPG = 2
NPOOL = 20
E_COLS = 3072
ALPHA = 4.0 ** 0.25
LAM_INIT = 0.2
BIG = 1e30
EPS = 1e-5
NRAW, NSPLIT, NGRP = 4, 2, 4
SLOT = 2048

C_ID, C_MASK, C_DIST, C_SEL, C_COMB, C_SLOPE, C_DROW, C_ADA = 0, 128, 640, 1152, 2176, 2240, 2241, 2498
C_END = 2507


def constants():
    c = np.zeros((P, C_END), np.float32)
    i = np.arange(P)
    c[:, C_ID:C_ID + P] = np.eye(P)
    c[:, C_MASK:C_MASK + P] = np.where(i[:, None] > i[None, :], BIG, 0.0)
    d = i[:, None] - np.arange(512)[None, :] + 384
    c[:, C_DIST:C_DIST + 512] = np.where(d >= 0, d, BIG)
    for b in range(8):
        c[b, C_SEL + b * P:C_SEL + (b + 1) * P] = 1.0
    for r in range(64):
        b, h, j = r // 8, (r // 2) % 4, r % 2
        c[r, C_COMB + (0 if j == 0 else 32) + b * 4 + h] = 1.0
        c[r, C_SLOPE] = -(2.0 ** (-2.0 * (h + 1)))
    c[:, C_DROW:C_DROW + 256] = (256 - np.arange(256))[None, :]
    for r in range(9):
        c[r, C_ADA + r] = 1.0
        c[r + 9, C_ADA + r] = 1.0
    return c


class Stage:

    def __init__(self, name, n, k, m, uses):
        self.name, self.n, self.k, self.m, self.uses = name, n, k, m, uses


def plan():
    st, use, order = {}, {}, []

    def one(*keys):
        for key in keys:
            use[key] = one.g
            one.g += 1
    one.g = 0

    def stage(name, n, k, m, uses):
        s = Stage(name, n, k, m, uses)
        s.c0, s.g0 = stage.c, one.g
        stage.c += n
        one.g += n * uses
        st[name] = s
        order.append(s)
    stage.c = 0

    one(*[("tx", i) for i in range(4)], "ra", "tc", "tb", "to", "lam")
    for l in range(2):
        stage(f"ada{l}", 24, 8, 256, 1)
        one(("sel", l))
    stage("ein", 12, 8, 256, 2)
    stage("gate", 1, 8, 128, 1)
    one(*[("kv", i) for i in range(4)], *[("bkv", i) for i in range(4)], "stokA", "stokB", "acol", "gs")
    for h in range(H):
        one(("bc", h))
        for sb in range(4):
            one(("mS", h, sb))
        one(("mN", h), ("mC", h))
    for s in range(18):
        if s < 16:
            one(("S", s))
        if 1 <= s < 17:
            one(("T", s - 1))
        if s >= 2:
            one(("PV", s - 2))
    for b in range(NS):
        one(("qb", b))
    one("st", "wT", "pvs", "pk")
    for t in range(8):
        one(("rms", t))
    stage("eout", 4, 8, 256, 2)
    one(("lnm", 0), ("lnq", 0))

    def ffn(l):
        for hf in range(2):
            stage(f"fi{l}{hf}", 11, 8, 256, 2)
            stage(f"fo{l}{hf}", 8, 11, 128, 1)
        one(("lnm", 2 * l + 1), ("lnq", 2 * l + 1))
    ffn(0)
    stage("oin", 10, 8, 256, 2)
    stage("wa", 2, 10, 128, 5)
    stage("wx", 2, 10, 128, 5)
    one("osA", "osB")
    stage("oout", 8, 10, 128, 1)
    one(("lnm", 2), ("lnq", 2))
    ffn(1)
    one(*[("ty", i) for i in range(4)], "tys")
    return st, use, order


def trunk(nc, a, o):
    st, use, order = plan()
    chunk_stage = {}
    for s in order:
        for c in range(s.c0, s.c0 + s.n):
            chunk_stage[c] = s
    n_chunks = len(chunk_stage)

    def chunk_last_use(c):
        s = chunk_stage[c]
        return s.g0 + (c - s.c0 + 1) * s.uses - 1

    def chunk_floats(c):
        s = chunk_stage[c]
        return s.k * s.m

    with ExitStack() as ctx:
        def sb(name, shape, dt=F32):
            return ctx.enter_context(nc.sbuf_tensor(name, shape, dt))

        def sem(name):
            return ctx.enter_context(nc.semaphore(name))

        raw = [sb(f"raw{i}", [P, SLOT]) for i in range(NRAW)]
        whi = [sb(f"whi{i}", [P, SLOT], F32R) for i in range(NSPLIT)]
        wlo = [sb(f"wlo{i}", [P, SLOT], F32R) for i in range(NSPLIT)]
        xT = sb("xT", [P, KD, 2, HT])
        cn = sb("cn", [P, C_END])
        modT = [sb(f"modT{l}", [P, 48, 9]) for l in range(2)]
        G9 = sb("G9", [P, 4, KD, 9])
        B9 = sb("B9", [P, 4, KD, 9])
        lnT = sb("lnT", [P, KD, 8])
        lnA = sb("lnA", [P, KD, 8])
        OT = sb("OT", [P, KR, 40])
        sp8 = sb("sp8", [P, 4, KR])
        bT = sb("bT", [P, 101])
        gA = sb("gA", [P, 1])
        neglam = sb("neglam", [P, 1])
        ones = sb("ones", [P, P])
        onesD = sb("onesD", [P, P])
        onesV = sb("onesV", [P, P])
        epsc = sb("epsc", [P, 1])
        stmp = sb("stmp", [P, 2, HS])
        sml = sb("sml", [P, 64])
        psig = sb("psig", [P, 1])
        xrS = sb("xrS", [P, KR, NS])
        tS = sb("tS", [P, 2, KR, NS])
        OS = sb("OS", [P, KR, 20])
        pgt = sb("pgt", [P, 16], I32)
        mpv = sb("mpv", [P, H])
        bgi = sb("bgi", [P, 2])
        ident = cn[:, C_ID:C_ID + P]

        base = (nc.sbuf_base + 31) // 32 * 32 if not callable(nc.sbuf_base) else None
        HTB = 2 * HT * 4

        def at(name, shape, off, dt=F32):
            return nc.alloc_sbuf_tensor_at(name, shape, dt, offset=base + off)

        O_U = 24 * HTB
        O_L = 40 * HTB
        accS, accQ = at("accS", [P, 2, HT], O_L), at("accQ", [P, 2, HT], O_L + HTB)
        sqb = [at(f"sqb{i}", [P, 2, HT], O_L + (2 + i) * HTB) for i in range(2)]
        mu, tv, rstd = (at(n, [P, 2, HT], O_L + (2 + i) * HTB) for i, n in enumerate(["mu", "tv", "rstd"]))
        db = [at(f"db{i}", [P, 2, HT], O_L + (5 + i) * HTB) for i in range(2)]
        nb = [at(f"nb{i}", [P, 2, HT], O_L + (7 + i) * HTB) for i in range(2)]
        ub = [at(f"ub{i}", [P, 2, HT], O_L + (9 + i) * HTB) for i in range(2)]
        UH, UL = at("UH", [P, KD, 2, HT], O_U, F32R), at("UL", [P, KD, 2, HT], O_U + 8 * HTB, F32R)
        xtok = at("xtok", [P, 4, D], 0)
        RA, CR = at("RA", [P, D], 16384), at("CR", [P, D], 20480)
        RO = at("RO", [P, DR], 24576)
        BR, NR = at("BR", [P, P], 29696), at("NR", [P, P], 30208)
        lamr = at("lamr", [P, 272], 30720)
        cH = at("cH", [P, KD, P], O_L, F32R)
        modrow = at("modrow", [P, 6 * D], 32768 + 512)
        assert 32768 + 512 + 24576 <= O_L
        proj = at("proj", [P, 24, 2, HT], 0)
        O_M = O_U
        def am(name, shape, off, dt=F32):
            n = 4
            for x in shape[1:]:
                n *= x
            assert O_M + off + n <= O_L + 12 * HTB, name
            return at(name, shape, O_M + off, dt)

        vtok = am("vtok", [P, 4, 512], 0)
        bkv = am("bkv", [P, 4, 768], 8192)
        stok = am("stok", [P, 2048], 20480)
        smp = am("smp", [P, 24, NS], 28672)
        rowc = am("rowc", [P, 2, SEQ], 29440)
        acol = am("acol", [P, 4, H], 33536)
        gst = sml[:, 16:24]
        ncT = am("ncT", [P, 1], 33632)
        wl = am("wl", [P, 4], 33664)
        kw = am("kw", [P, 4, DK], 33696)
        Cst = am("Cst", [P, H, DK], 34720)
        nst = am("nst", [P, H, DK], 35744)
        cmB = [am(f"cmB{i}", [P, 2, 512], 36768 + i * 4096) for i in range(2)]
        Ex = [am(f"Ex{i}", [P, 512], 44960 + i * 2048) for i in range(2)]
        PTall = am("PT", [P, 1280], 49056)
        pt_off = [0, 512, 896, 1152]
        PT = [PTall[:, pt_off[i]:pt_off[i] + 512 - i * P] for i in range(4)]
        rows = am("rows", [P, 6, 2, HT], 36768)
        ktok = am("ktok", [P, 4, 512], 49280)
        Sb = [am(f"Sb{i}", [P, 2, 512], 36768 + i * 4096) for i in range(2)]
        Wb = [am(f"Wb{i}", [P, 512], 44960 + i * 2048) for i in range(2)]
        wTb = [am(f"wTb{i}", [P, 512], 49056 + i * 2048) for i in range(2)]
        st8 = [am(f"st8{i}", [P, 8], 53152 + i * 32) for i in range(2)]
        Kp = [am(f"Kp{i}", [P, NPG, 512], i * 4096) for i in range(2)]
        Vp = [am(f"Vp{i}", [P, NPG, 512], 8192 + i * 4096) for i in range(3)]
        kbc = am("kbc", [P, NS, 256], 29440)
        prod = am("prod", [P, NPG, 512], 37632)
        Sc = am("Sc", [P, NPG, 64], 41728)
        Pq = am("Pq", [P, 257], 42240)
        s8 = am("s8", [P, 256], 43296)
        CqS = am("CqS", [P, NS, H], 44320)
        wTs = am("wTs", [P, 3, 32], 44448)
        pks = am("pks", [P, NS, 16], 44832)
        Comb = am("Comb", [P, 32], 45344)
        sm8 = am("sm8", [P, 96], 45472)
        np8 = am("np8", [P, 512], 45856)
        t32 = am("t32", [P, 2, 32], 47904)
        Cs = am("Cs", [P, NS, 256], 48160)
        MH, ML = at("MH", [P, 8, 2, HT], O_U, F32R), at("ML", [P, 8, 2, HT], O_U + 8 * HTB, F32R)
        rmb = [at(f"rmb{i}", [P, 2, HT], O_L + (4 + i) * HTB) for i in range(2)]
        rsq = [at(f"rsq{i}", [P, 2, HT], O_L + (6 + i) * HTB) for i in range(2)]
        mxb = [at(f"mxb{i}", [P, 2, HT], O_L + (8 + i) * HTB) for i in range(2)]
        HH, HL = at("HH", [P, KH, 2, HT], 0, F32R), at("HL", [P, KH, 2, HT], 11 * HTB, F32R)
        silb = [at(f"silb{i}", [P, 2, HT], O_L + (5 + i) * HTB) for i in range(2)]
        hb = [at(f"hb{i}", [P, 2, HT], O_L + (7 + i) * HTB) for i in range(2)]
        gT = at("gT", [P, KR, 2, HT], 0)
        rT = at("rT", [P, KR, 2, HT], 10 * HTB)
        xr = at("xr", [P, KR, 3 + SEQ], 10 * HTB)
        XH, XL = at("XH", [P, KR, 2, HT], 20 * HTB, F32R), at("XL", [P, KR, 2, HT], 30 * HTB, F32R)
        aT, qT = at("aT", [P, KR, 2, HT], 20 * HTB), at("qT", [P, KR, 2, HT], 30 * HTB)
        YH, YL = at("YH", [P, KR, 2, HT], 20 * HTB, F32R), at("YL", [P, KR, 2, HT], 30 * HTB, F32R)
        xc = at("xc", [P, KR, 2, HT], 40 * HTB)
        xc_end = 50
        isb = [at(f"isb{i}", [P, 2, HT], (xc_end + i) * HTB) for i in range(2)]
        ysb = [at(f"ysb{i}", [P, 2, HT], (xc_end + i) * HTB) for i in range(2)]
        OST = at("OST", [P, DR], 0)
        ytok = [at(f"ytok{i}", [P, D], i * 4096) for i in range(2)]
        ysamp = at("ysamp", [P, D], 8192)
        xsm = at("xsm", [P, KD, NS], 12288)

        psum = [ctx.enter_context(nc.psum_tensor(f"ps{i}", [P, 2, 512], F32)) for i in range(NGRP)]

        raw_loaded = [sem(f"raw_loaded{i}") for i in range(NRAW)]
        hi_done, lo_done = sem("hi_done"), sem("lo_done")
        filled = sem("psum_filled")
        freed = [sem(f"psum_freed{i}") for i in range(NGRP)]
        consts_loaded, x_loaded, small_loaded = sem("consts_loaded"), sem("x_loaded"), sem("small_loaded")
        memset_done = sem("memset_done")
        silu_c, c_hi, c_lo = sem("silu_c"), sem("c_hi"), sem("c_lo")
        dve_step, act_step, pool_step = sem("dve_step"), sem("act_step"), sem("pool_step")
        modrow_done = sem("modrow_done")
        d_ready, n_ready, u_ready = sem("d_ready"), sem("n_ready"), sem("u_ready")
        uhi_ready, ulo_ready, x_ready = sem("uhi_ready"), sem("ulo_ready"), sem("x_ready")
        z_ready, sq_ready, acc_step = sem("z_ready"), sem("sq_ready"), sem("acc_step")
        mu_ready, var_ready, sd_ready = sem("mu_ready"), sem("var_ready"), sem("sd_ready")
        sil_ready, h_ready, hhi_ready, hlo_ready = sem("sil_ready"), sem("h_ready"), sem("hhi_ready"), sem("hlo_ready")
        evac, tok_ready = sem("proj_evacuated"), sem("tok_ready")
        act_q, dve_q = sem("act_answer"), sem("dve_ask")
        exq, pxq = sem("score_arg_ready"), sem("score_exp_ready")
        pt_ready, cm_ready = sem("pt_ready"), sem("cm_ready")
        for_pe = sem("dve_for_pe")
        pb_ready, w_ready, wT_ready = sem("p_ready"), sem("w_ready"), sem("wT_ready")
        smax_ready = sem("smax_ready")
        past_k = [sem(f"past_k{i}") for i in range(2)]
        past_v = [sem(f"past_v{i}") for i in range(3)]
        k_used, v_used = sem("past_k_used"), sem("past_v_used")
        state_loaded, region_q = sem("state_loaded"), sem("region_free")
        state_n_loaded = sem("state_n_loaded")
        region_p, keys_stored = sem("prompt_states_stored"), sem("keys_stored")
        for_store = sem("dve_for_store")
        stored = sem("stored")
        rm_sq, rm_sd, rm_in, mix_hi, mix_lo = sem("rms_sq"), sem("rms_sd"), sem("rms_in"), sem("mix_hi"), sem("mix_lo")
        mx_ready = sem("mixed_ready")
        xr_ready, cv0, cv_ready, xch, xcl = sem("xr_ready"), sem("conv_first"), sem("conv_ready"), sem("xc_hi"), sem("xc_lo")
        i_ready, ix_ready, a_ready, q_ready, sqrt_ready = sem("i_ready"), sem("ix_ready"), sem("a_ready"), sem("q_ready"), sem("sqrt_ready")
        y_ready, yhi_ready, ylo_ready = sem("y_ready"), sem("yhi_ready"), sem("ylo_ready")
        pool_store, ytok_stored = sem("pool_store"), [sem(f"ytok_stored{i}") for i in range(2)]
        out_ready = sem("out_ready")
        zero_ready = sem("history_zero")

        block = ctx.enter_context(nc.Block())

        def ps(g):
            return psum[g % NGRP]

        def wait_filled(eng, g):
            eng.wait_ge(filled, g + 1)

        def free(ins, g):
            ins.then_inc(freed[g % NGRP], 1)

        def chain(eng, s):
            n = [0]

            def link(ins):
                n[0] += 1
                ins.then_inc(s, 1)
                eng.wait_ge(s, n[0])
            return link

        landed = {}

        def settled(eng, s, n=1):
            landed[s] = landed.get(s, 0) + n
            eng.wait_ge(s, landed[s])

        def tok(t):
            return t[:, :, 0:HALF]

        def smpl(t):
            return t[:, :, HALF:HT]

        def pT(g):
            return ps(g)[:, :, 0:HT]

        def weight_view(s):
            n = s.name
            if n[:3] == "ada":
                return a["w_ada"][int(n[3])].rearrange("(k p) (c m) -> c p k m", p=P, m=256)
            if n == "ein":
                return a["w_in_even"][0][:, 0:E_COLS].rearrange("(k p) (c m) -> c p k m", p=P, m=256)
            if n == "eout":
                return a["w_out_even"][0].rearrange("(k p) (c m) -> c p k m", p=P, m=256)
            if n[:2] == "fi":
                l, hf = int(n[2]), int(n[3])
                v = a["w_ffn_in"][l].rearrange("(k p) (g c m) -> c p k g m", p=P, g=2, m=P)
                return v[hf * KH:(hf + 1) * KH]
            if n[:2] == "fo":
                l, hf = int(n[2]), int(n[3])
                return a["w_ffn_out"][l][hf * KH * P:(hf + 1) * KH * P].rearrange("(k p) (c m) -> c p k m", p=P, m=P)
            if n == "oin":
                return a["w_in_odd"][0].rearrange("(k p) (c m) -> c p k m", p=P, m=256)
            if n in ("wa", "wx"):
                w = a["w_a" if n == "wa" else "w_x"][0].rearrange("n r m -> (n r) m")
                return w.rearrange("(k p) (c m) -> c p k m", p=P, m=P)
            return a["w_out_odd"][0].rearrange("(k p) (c m) -> c p k m", p=P, m=P)

        def past(sp):
            sp.wait_ge(small_loaded, 16 * N_SMALL)
            sp.wait_ge(region_q, 1)
            sp.dma_start(Cs[:], a["state_C"][0].rearrange("b h v k -> v (b h) k")).then_inc(state_loaded, 16)
            pages = [None] * 16

            def page(b, g):
                return sp.value_load(pgt[0:1, 2 * b + g:2 * b + g + 1], min_val=0, max_val=NPOOL - 1)

            def load_k(b):
                if b >= 2:
                    sp.wait_ge(k_used, b - 1)
                for g in range(NPG):
                    pg = page(b, g)
                    src = a["cache_k"][0][bass.ds(pg, 1)].rearrange("a p h j d -> (a p) (h j d)")
                    sp.dma_start(Kp[b % 2][:, g], src).then_inc(past_k[b % 2], 16)

            def load_v(b):
                if b >= 3:
                    sp.wait_ge(v_used, b - 2)
                for g in range(NPG):
                    pg = page(b, g)
                    src = a["cache_v"][0][bass.ds(pg, 1)].rearrange("a p h d -> (a p) (h d)")
                    sp.dma_start(Vp[b % 3][:, g], src).then_inc(past_v[b % 3], 16)
            for b in range(NS):
                load_k(b)
                if b < 3:
                    load_v(b)
            for b in range(3, NS):
                load_v(b)

        N_SMALL = 20
        count = {}

        @block.sync
        def _(sp):
            def load(s, c, it=None):
                gc = s.c0 + c
                slot = gc % NRAW
                if gc >= NRAW:
                    sp.wait_ge(lo_done, gc - NRAW + 1 + (0 if it is None else it * NRAW))
                v = weight_view(s)
                if s.name[:2] == "fi":
                    src = v[bass.ds(c + it * NRAW, 1)].rearrange("a p k g m -> (a p) k g m") if it is not None else v[c]
                    dst = raw[slot][:].rearrange("p (k g m) -> p k g m", k=8, g=2)
                    for g in range(2):
                        sp.dma_start(dst[:, :, g], src[:, :, g]).then_inc(raw_loaded[slot], 16)
                else:
                    src = v[bass.ds(c + it * NRAW, 1)].rearrange("a p k m -> (a p) k m") if it is not None else v[c]
                    dst = raw[slot][:, 0:s.k * s.m].rearrange("p (k m) -> p k m", m=s.m)
                    kh = s.k // 2
                    sp.dma_start(dst[:, 0:kh], src[:, 0:kh]).then_inc(raw_loaded[slot], 16)
                    sp.dma_start(dst[:, kh:], src[:, kh:]).then_inc(raw_loaded[slot], 16)

            sp.dma_start(cn[:], a["consts"]).then_inc(consts_loaded, 16)
            sp.dma_start(xtok[:], a["x_prompt"][0].rearrange("(b p) d -> p b d", p=P)).then_inc(x_loaded, 16)
            for s in order:
                if s.name == "gate":
                    gc = s.c0
                    sp.wait_ge(lo_done, gc - NRAW + 1)
                    dst = raw[gc % NRAW][:, 0:64].rearrange("p (k g m) -> p k g m", k=8, g=2)
                    src = a["w_in_even"][0][:, E_COLS:E_COLS + 8].rearrange("(k p) (g m) -> p k g m", p=P, g=2)
                    for g in range(2):
                        sp.dma_start(dst[:, :, g], src[:, :, g]).then_inc(raw_loaded[gc % NRAW], 16)
                    continue
                peel = NRAW if s.c0 == 0 else 0
                for c in range(peel):
                    load(s, c)
                bodies = (s.n - peel) // NRAW
                if bodies > 1:
                    with sp.Fori(0, bodies) as it:
                        for c in range(NRAW):
                            load(s, peel + c, it=it)
                    peel += bodies * NRAW
                for c in range(peel, s.n):
                    load(s, c)
                if s.name == "eout":
                    past(sp)

        @block.gpsimd
        def _(pool):
            link = chain(pool, pool_step)

            pool.memset(ones[:], 1.0).then_inc(memset_done, 1)
            settled(pool, memset_done)
            pool.memset(onesD[:], 1.0 / D).then_inc(memset_done, 1)
            settled(pool, memset_done)
            pool.memset(onesV[:], 1.0 / DV).then_inc(memset_done, 1)
            settled(pool, memset_done)
            pool.memset(epsc[:], EPS).then_inc(memset_done, 1)
            settled(pool, memset_done)
            pool.memset(cH[:].bitcast(F32), 0.0).then_inc(memset_done, 1)
            settled(pool, memset_done)

            n = [0]

            def small(dst, src):
                pool.dma_start(dst, src).then_inc(small_loaded, 16)
                n[0] += 1
            small(CR[0:1], a["c_prompt"])
            small(CR[1:9], a["c_sample"])
            small(RA[0:8], a["x_sample"].rearrange("b t d -> (b t) d"))
            small(RA[8:12], a["ln_g"].rearrange("l j d -> (l j) d"))
            small(RA[12:16], a["ln_b"].rearrange("l j d -> (l j) d"))
            small(BR[0:96], a["b_ada"].rearrange("l (r m) -> (l r) m", m=P))
            small(NR[0:1], a["attn_norm_g"])
            small(NR[1:5], a["mlstm_norm_g"][0])
            small(RO[0:24], a["state_conv"][0].rearrange("b j d -> (b j) d"))
            small(RO[24:32], a["state_h"][0])
            small(RO[32:36], a["conv_w"][0])
            small(RO[36:37], a["conv_b"])
            small(RO[37:38], a["b_a"])
            small(RO[38:39], a["b_x"])
            small(RO[39:40], a["lru_lambda"])
            small(lamr[0:1, 0:256], a["lam"].rearrange("e r d -> e (r d)"))
            small(pgt[0:1, :], a["page_table"].rearrange("(e b) g -> e (b g)", e=1))
            small(mpv[0:NS], a["state_m"][0])
            small(bgi[0:4, 0:1], a["b_i"].rearrange("e h -> h e"))
            small(bgi[32:36, 1:2], a["b_f"].rearrange("e h -> h e"))
            assert n[0] == N_SMALL

            stores = [0]

            def store(dst, src):
                pool.dma_start(dst, src).then_inc(stored, 16)
                stores[0] += 1

            store(o["conv_sample"][0][:, 0:2, :], a["state_conv"][0][:, 1:3, :])

            for tb in range(4):
                pool.wait_ge(tok_ready, 2 * tb + 1)
                store(o["k_prompt"][0, 0, tb].rearrange("t h j d -> t (h j d)"), ktok[:, tb])
                store(o["v_prompt"][0, 0, tb].rearrange("t h d -> t (h d)"), vtok[:, tb])
            pool.wait_ge(stored, 16 * stores[0])
            pool.memset(psig[:], 0.0).then_inc(keys_stored, 1)
            settled(pool, keys_stored)
            pool.wait_ge(for_store, 2)
            store(o["k_sample"][0].rearrange("b t h j d -> (b t) (h j d)"), stok[0:NS, 512:1024])
            store(o["v_sample"][0].rearrange("b t h d -> (b t) (h d)"), stok[0:NS, 1024:1536])
            pool.wait_ge(for_store, 3)
            store(o["m_prompt"][0, 0].rearrange("(h e) -> h e", e=1), rowc[0:4, 1, SEQ - 1:SEQ])
            pool.wait_ge(for_store, 4)
            store(o["C_prompt"][0, 0].rearrange("h v k -> v h k"), Cst[:])
            store(o["n_prompt"][0].rearrange("a h k -> a (h k)"), nst[0:1].rearrange("p h k -> p (h k)"))
            pool.wait_ge(stored, 16 * stores[0])
            pool.wait_ge(for_store, 5)
            pool.memset(np8[:], 0.0).then_inc(region_p, 1)
            settled(pool, region_p)
            pool.wait_ge(region_p, 1)
            pool.dma_start(np8[0:NS, 0:256], a["state_n"][0].rearrange("b h k -> b (h k)")).then_inc(state_n_loaded, 16)
            pool.wait_ge(for_store, 6)
            store(o["m_sample"][0], sm8[0:NS, 0:4])
            store(o["n_sample"][0].rearrange("b h k -> b (h k)"), np8[0:NS, 256:512])
            pool.wait_ge(for_store, 7)
            store(o["C_sample"][0].rearrange("b h v k -> v (b h) k"), Cs[:].rearrange("p b (h k) -> p (b h) k", h=H))
            mid_stores = count["middle"] = stores[0]

            def ln_sums(r):
                if r == 0:
                    pool.wait_ge(stored, 16 * mid_stores)
                for t in range(KD):
                    pool.wait_ge(z_ready, 8 * r + t + 1)
                    k = 16 * r + 2 * t
                    if t == 0:
                        pool.tensor_copy(accS[:], xT[:, t]).then_inc(acc_step, 1)
                        settled(pool, acc_step)
                    else:
                        pool.wait_ge(acc_step, k)
                        pool.tensor_tensor(accS[:], accS[:], xT[:, t], ALU.add).then_inc(acc_step, 1)
                        settled(pool, acc_step)
                    pool.wait_ge(sq_ready, 8 * r + t + 1)
                    if t == 0:
                        pool.tensor_copy(accQ[:], sqb[t % 2][:]).then_inc(acc_step, 1)
                        settled(pool, acc_step)
                    else:
                        pool.tensor_tensor(accQ[:], accQ[:], sqb[t % 2][:], ALU.add).then_inc(acc_step, 1)
                        settled(pool, acc_step)

            def ln_center(r):
                pool.wait_ge(mu_ready, r + 1)
                for t in range(KD):
                    if t >= 2:
                        pool.wait_ge(n_ready, 8 * r + t - 1)
                    pool.tensor_tensor(db[t % 2][:], xT[:, t], mu[:], ALU.subtract).then_inc(d_ready, 1)
                    settled(pool, d_ready)

            for r in range(4):
                ln_sums(r)
                ln_center(r)
                if r == 1:
                    pool.wait_ge(ulo_ready, 8 * 3)
                    pool.memset(xr[:, :, 0:3], 0.0).then_inc(zero_ready, 1)
                    settled(pool, zero_ready)
                    pool.wait_ge(out_ready, 2)
                    store(o["conv_prompt"][0, 0], OST[0:3])
                    store(o["conv_sample"][0][:, 2, :], OST[3:11])
                    store(o["h_prompt"][0], OST[11:12])
                    store(o["h_sample"][0], OST[12:20])
                    count["rows_stored"] = stores[0]
            for tb in range(4):
                pool.wait_ge(out_ready, 3 + tb)
                pool.dma_start(o["y_prompt"][0][tb * P:(tb + 1) * P], ytok[tb % 2][:]).then_inc(ytok_stored[tb % 2], 16)
            pool.wait_ge(out_ready, 7)
            store(o["y_sample"].rearrange("b t d -> (b t) d"), ysamp[0:NS])
            pool.wait_ge(stored, 16 * stores[0])
            pool.wait_ge(ytok_stored[0], 32)
            pool.wait_ge(ytok_stored[1], 32)

        def middle_act(act, link):
            act.wait_ge(evac, 24)
            nc.scalar.activation(proj[:, 20:24], proj[:, 20:24], ACT.Sigmoid).then_inc(act_q, 1)
            settled(act, act_q)
            act.wait_ge(act_q, 4)
            g = use_gate
            wait_filled(act, g)
            act.wait_ge(dve_q, 3)
            nc.scalar.activation(rows[0:4, 0], ps(g)[0:4, :, 0:HT], ACT.Tanh, scale=1.0 / 15.0,
                                 bias=sml[0:4, 8:9]).then_inc(act_q, 1)
            settled(act, act_q)
            act.wait_ge(dve_q, 4)
            nc.scalar.activation(rows[0:4, 2], rows[0:4, 2], ACT.Exp, scale=-1.0).then_inc(act_q, 1)
            settled(act, act_q)
            act.wait_ge(act_q, 6)
            nc.scalar.activation(rows[0:4, 2], rows[0:4, 2], ACT.Ln, bias=1.0).then_inc(act_q, 1)
            settled(act, act_q)
            for tb in range(4):
                g = use[("kv", tb)]
                wait_filled(act, g)
                nc.scalar.activation(ktok[:, tb], ps(g)[:, 0], ACT.Identity)
                nc.scalar.activation(vtok[:, tb], ps(g)[:, 1], ACT.Identity).then_inc(tok_ready, 1)
                settled(act, tok_ready)
                act.wait_ge(tok_ready, 2 * tb + 1)
                free(nc.scalar.activation(sml[0:1, 0:1], ps(g)[0:1, 0, 0:1], ACT.Identity), g)
                act.wait_ge(freed[g % NGRP], g // NGRP + 1)
                g = use[("bkv", tb)]
                wait_filled(act, g)
                nc.scalar.activation(bkv[:, tb], ps(g)[:].rearrange("p a b -> p (a b)")[:, 0:768],
                                     ACT.Identity).then_inc(tok_ready, 1)
                settled(act, tok_ready)
                act.wait_ge(tok_ready, 2 * tb + 2)
                free(nc.scalar.activation(sml[0:1, 0:1], ps(g)[0:1, 0, 0:1], ACT.Identity), g)
                act.wait_ge(freed[g % NGRP], g // NGRP + 1)
            for h in range(H):
                g = use[("bc", h)]
                wait_filled(act, g)
                cm = cmB[h % 2]
                if h >= 2:
                    act.wait_ge(for_pe, h + 2)
                link(nc.scalar.activation(cm[:, 0], ps(g)[:, 0], ACT.Identity))
                free(nc.scalar.activation(cm[:, 1], ps(g)[:, 1], ACT.Exp, scale=-1.0), g)
                act.wait_ge(freed[g % NGRP], g // NGRP + 1)
                act.wait_ge(freed[g % NGRP], g // NGRP + 1)
                cm_sem(nc.scalar.activation(ncT[:], cm[:, 0, SEQ - 1:SEQ], ACT.Copy, scale=-1.0))
                act.wait_ge(cm_ready, 2 * h + 1)
                act.wait_ge(for_store, 3)
                if h >= 1:
                    act.wait_ge(for_pe, h + 3)
                cm_sem(nc.scalar.activation(wl[:], acol[:, :, h], ACT.Exp, bias=ncT[:]))
                for sb_ in range(4):
                    n = SEQ - sb_ * P
                    k = 4 * h + sb_
                    act.wait_ge(exq, k + 1)
                    nc.scalar.activation(Ex[k % 2][:, 0:n], Ex[k % 2][:, 0:n], ACT.Exp, scale=-1.0,
                                         bias=acol[:, sb_, h:h + 1]).then_inc(pxq, 1)
                    settled(act, pxq)
            def unit_exp(u):
                n = (u % 4 + 1) * P
                act.wait_ge(pb_ready, u + 1)
                for j in range(2):
                    ins = nc.scalar.activation(Sb[u % 2][:, j, 0:n], Sb[u % 2][:, j, 0:n], ACT.Exp,
                                               bias=st8[u % 2][:, j:j + 1], accum_out=st8[u % 2][:, 2 + j:3 + j])
                    ins.then_inc(smax_ready, 1)
                    settled(act, smax_ready)

            def unit_wT(u):
                n = (u % 4 + 1) * P
                g = use[("T", u)]
                wait_filled(act, g)
                if u >= 2:
                    wait_filled(act, use[("PV", u - 2)])
                nc.scalar.activation(wTb[u % 2][:, 0:n], ps(g)[:, 0, 0:n], ACT.Identity).then_inc(wT_ready, 1)
                settled(act, wT_ready)
                act.wait_ge(wT_ready, u + 1)
                free(nc.scalar.activation(sml[0:1, 0:1], ps(g)[0:1, 0, 0:1], ACT.Identity), g)
                act.wait_ge(freed[g % NGRP], g // NGRP + 1)
            for s_ in range(17):
                if s_ < 16:
                    unit_exp(s_)
                if s_ >= 1:
                    unit_wT(s_ - 1)
            act.wait_ge(dve_q, 5)
            nc.scalar.activation(sm8[0:NS, 16:24], sm8[0:NS, 16:24], ACT.Exp).then_inc(act_q, 1)
            settled(act, act_q)
            nc.scalar.activation(sm8[0:NS, 24:28], sm8[0:NS, 0:4], ACT.Exp, scale=-1.0).then_inc(act_q, 1)
            settled(act, act_q)
            act.wait_ge(dve_q, 6)
            nc.scalar.activation(Pq[0:64], Pq[0:64], ACT.Exp, bias=t32[0:64, 0, 0:1],
                                 accum_out=t32[0:64, 0, 1:2]).then_inc(act_q, 1)
            settled(act, act_q)
            act.wait_ge(for_pe, 12)
            act.wait_ge(stored, 16 * count["middle"])
            for t in range(8):
                src = proj[:, t] if t < 4 else proj[:, 12 + t]
                if t >= 2:
                    wait_filled(act, use[("rms", t - 2)])
                nc.scalar.activation(rsq[t % 2][:], src, ACT.Square).then_inc(rm_sq, 1)
                settled(act, rm_sq)
                if t >= 1:
                    rms_tail(act, t - 1)
            rms_tail(act, 7)

        def cm_sem(ins):
            ins.then_inc(cm_ready, 1)
            settled(nc.scalar, cm_ready)

        def rms_tail(act, t):
            g = use[("rms", t)]
            wait_filled(act, g)
            if t >= 2:
                act.wait_ge(mx_ready, t - 1)
            ins = nc.scalar.activation(rmb[t % 2][:], pT(g), ACT.Sqrt, bias=epsc[:])
            free(ins, g)
            act.wait_ge(freed[g % NGRP], g // NGRP + 1)
            act.wait_ge(mx_ready, t + 1)
            nc.scalar.activation(MH[:, t], mxb[t % 2][:], ACT.Identity).then_inc(mix_hi, 1)
            settled(act, mix_hi)

        use_gate = st["gate"].g0

        @block.scalar
        def _(act):
            link = chain(act, act_step)

            def hi(c):
                if c >= n_chunks:
                    return
                s = chunk_stage[c]
                act.wait_ge(raw_loaded[c % NRAW], 32 * (c // NRAW + 1))
                if c >= NSPLIT:
                    wait_filled(act, chunk_last_use(c - NSPLIT))
                if s.name == "gate":
                    src = raw[c % NRAW][:, 0:64].rearrange("p (k g m) -> p k g m", k=8, g=2)
                    dst = whi[c % 2][:, 0:1024].rearrange("p (k g m) -> p k g m", k=8, m=32)[:, :, 0:2, 0:4]
                    ins = nc.scalar.activation(dst, src, ACT.Identity)
                else:
                    f = chunk_floats(c)
                    ins = nc.scalar.activation(whi[c % 2][:, 0:f], raw[c % NRAW][:, 0:f], ACT.Identity)
                ins.then_inc(hi_done, 1)
                settled(act, hi_done)

            act.wait_ge(small_loaded, 16 * N_SMALL)
            nc.scalar.activation(CR[0:9], CR[0:9], ACT.Silu).then_inc(silu_c, 1)
            settled(act, silu_c)
            hi(0)
            hi(1)
            act.wait_ge(memset_done, 5)
            wait_filled(act, use["tc"])
            nc.scalar.activation(cH[:, :, 0:9], ps(use["tc"])[:, 0, 0:72].rearrange("p (k c) -> p k c", c=9),
                                 ACT.Identity).then_inc(c_hi, 1)
            settled(act, c_hi)
            act.wait_ge(dve_q, 1)
            nc.scalar.activation(sp8[:, 1], sp8[:, 1], ACT.Exp, scale=-1.0).then_inc(act_q, 1)
            settled(act, act_q)
            act.wait_ge(dve_q, 2)
            nc.scalar.activation(lamr[0:1, 258:260], lamr[0:1, 256:258], ACT.Exp).then_inc(act_q, 1)
            settled(act, act_q)
            act.wait_ge(act_q, 2)
            nc.scalar.activation(sp8[:, 1], sp8[:, 1], ACT.Ln, bias=1.0).then_inc(act_q, 1)
            settled(act, act_q)
            for l in range(2):
                s = st[f"ada{l}"]
                for c in range(s.n):
                    hi(s.c0 + c + 2)

            def split_u(q):
                r = q - 1
                for t in range(KD):
                    if r >= 0:
                        act.wait_ge(n_ready, 8 * r + t + 1)
                        lt = lnT if r == 3 else lnA
                        nc.scalar.activation(xT[:, t], nb[t % 2][:], ACT.Identity, scale=lt[:, t, r:r + 1],
                                             bias=lt[:, t, 4 + r:5 + r]).then_inc(x_ready, 1)
                        settled(act, x_ready)
                    if q < 4:
                        act.wait_ge(u_ready, 8 * q + t + 1)
                        nc.scalar.activation(UH[:, t], ub[t % 2][:], ACT.Identity).then_inc(uhi_ready, 1)
                        settled(act, uhi_ready)

            def squares(r, t):
                act.wait_ge(z_ready, 8 * r + t + 1)
                if t >= 2:
                    act.wait_ge(acc_step, 16 * r + 2 * (t - 2) + 2)
                nc.scalar.activation(sqb[t % 2][:], xT[:, t], ACT.Square).then_inc(sq_ready, 1)
                settled(act, sq_ready)

            def ln_sqrt(r):
                act.wait_ge(var_ready, r + 1)
                nc.scalar.activation(tv[:], tv[:], ACT.Sqrt).then_inc(sd_ready, 1)
                settled(act, sd_ready)

            def ffn(l):
                for hf in range(2):
                    s = st[f"fi{l}{hf}"]
                    for c in range(s.n):
                        k = (2 * l + hf) * KH + c
                        g = s.g0 + 2 * c
                        wait_filled(act, g)
                        if k >= 2:
                            act.wait_ge(h_ready, k - 1)
                        ins = nc.scalar.activation(silb[c % 2][:], pT(g), ACT.Silu)
                        free(ins, g)
                        act.wait_ge(freed[g % NGRP], g // NGRP + 1)
                        hi(s.c0 + c + 2)
                        act.wait_ge(h_ready, k + 1)
                        if l == 1 and hf == 0 and c == 0:
                            act.wait_ge(stored, 16 * count["rows_stored"])
                        nc.scalar.activation(HH[:, c], hb[c % 2][:], ACT.Identity).then_inc(hhi_ready, 1)
                        settled(act, hhi_ready)
                    s = st[f"fo{l}{hf}"]
                    for c in range(s.n):
                        hi(s.c0 + c + 2)
                        if hf == 1 and c >= 1:
                            squares(2 * l + 1, c - 1)
                squares(2 * l + 1, KD - 1)
                ln_sqrt(2 * l + 1)

            split_u(0)
            for c in range(12):
                hi(st["ein"].c0 + c + 2)
            hi(st["gate"].c0 + 2)
            middle_act(act, link)
            for c in range(4):
                hi(st["eout"].c0 + c + 2)
                if c >= 1:
                    squares(0, 2 * c - 2)
                    squares(0, 2 * c - 1)
            squares(0, 6)
            squares(0, 7)
            ln_sqrt(0)
            split_u(1)
            ffn(0)
            split_u(2)
            s = st["oin"]
            for c in range(s.n):
                hi(s.c0 + c + 2)
                for m in range(2):
                    t = 2 * c + m
                    g = s.g0 + t
                    if t < KR:
                        wait_filled(act, g)
                        free(nc.scalar.activation(gT[:, t], pT(g), ACT.Gelu_apprx_tanh), g)
                        act.wait_ge(freed[g % NGRP], g // NGRP + 1)
                    else:
                        t -= KR
                        act.wait_ge(xr_ready, t + 1)
                        nc.scalar.activation(tok(xc[:, t]), xr[:, t, 0:SEQ].rearrange("p (a b) -> p a b", a=2),
                                             ACT.Identity, scale=OT[:, t, 32:33],
                                             bias=OT[:, t, 36:37]).then_inc(cv0, 1)
                        settled(act, cv0)
            for t in range(KR):
                act.wait_ge(cv_ready, 1)
                nc.scalar.activation(XH[:, t], xc[:, t], ACT.Identity).then_inc(xch, 1)
                settled(act, xch)
            for w, col in (("wa", 37), ("wx", 38)):
                s = st[w]
                for c in range(2):
                    for b in range(5):
                        g = s.g0 + 5 * c + b
                        t = 2 * b + c
                        wait_filled(act, g)
                        if w == "wa":
                            if g == s.g0:
                                act.wait_ge(for_store, 8)
                            ins = nc.scalar.activation(rT[:, t], pT(g), ACT.Sigmoid, bias=OT[:, t, col:col + 1])
                            free(ins, g)
                            act.wait_ge(freed[g % NGRP], g // NGRP + 1)
                        else:
                            k = 5 * c + b
                            if k >= 2:
                                act.wait_ge(ix_ready, k - 1)
                            ins = nc.scalar.activation(isb[k % 2][:], pT(g), ACT.Sigmoid, bias=OT[:, t, col:col + 1])
                            free(ins, g)
                            act.wait_ge(freed[g % NGRP], g // NGRP + 1)
                    hi(s.c0 + c + 2)
            act.wait_ge(xcl, KR)
            act.wait_ge(ix_ready, KR)
            act.wait_ge(freed[(st["wx"].g0 + 9) % NGRP], (st["wx"].g0 + 9) // NGRP + 1)
            for t in range(KR):
                link(nc.scalar.activation(aT[:, t], rT[:, t], ACT.Exp, scale=sp8[:, 3, t:t + 1]))
                nc.scalar.activation(qT[:, t], rT[:, t], ACT.Tanh, scale=sp8[:, 2, t:t + 1])
                if t >= 2:
                    act.wait_ge(q_ready, t - 1)
                nc.scalar.activation(isb[t % 2][:], aT[:, t], ACT.Square).then_inc(a_ready, 1)
                settled(act, a_ready)
            for t in range(KR):
                act.wait_ge(q_ready, t + 1)
                nc.scalar.activation(qT[:, t], qT[:, t], ACT.Sqrt).then_inc(sqrt_ready, 1)
                settled(act, sqrt_ready)
            for t in range(KR):
                act.wait_ge(y_ready, t + 1)
                nc.scalar.activation(YH[:, t], ysb[t % 2][:], ACT.Identity).then_inc(yhi_ready, 1)
                settled(act, yhi_ready)
            s = st["oout"]
            for c in range(s.n):
                hi(s.c0 + c + 2)
                if c >= 1:
                    squares(2, c - 1)
            squares(2, KD - 1)
            ln_sqrt(2)
            split_u(3)
            ffn(1)
            split_u(4)

        def middle_dve(dve, link):
            v = nc.vector
            v.tensor_copy(smp[:, 0:20].rearrange("p t (a b) -> p t a b", a=2), proj[:, 0:20, :, HALF:HT]).then_inc(for_pe, 1)
            settled(dve, for_pe)
            v.tensor_scalar(sml[0:4, 8:9], bgi[0:4, 0:1], 1.0 / 15.0, None, ALU.mult).then_inc(dve_q, 1)
            settled(dve, dve_q)
            g = use_gate
            wait_filled(dve, g)
            x_f = rows[0:4, 1]
            link(v.tensor_scalar(x_f, ps(g)[32:36, :, 0:HT], bgi[32:36, 1:2], None, ALU.add))
            link(v.tensor_scalar(rows[0:4, 2], x_f, -1.0, None, ALU.mult))
            v.tensor_tensor(rows[0:4, 2], rows[0:4, 2], x_f, ALU.max).then_inc(dve_q, 1)
            settled(dve, dve_q)
            dve.wait_ge(dve_q, 4)
            link(v.tensor_scalar(x_f, x_f, 0.0, None, ALU.min))
            dve.wait_ge(act_q, 7)
            free(v.tensor_scalar(rows[0:4, 0], rows[0:4, 0], 15.0, None, ALU.mult), g)
            dve.wait_ge(freed[g % NGRP], g // NGRP + 1)
            link(v.tensor_tensor(x_f, x_f, rows[0:4, 2], ALU.subtract))
            one_row = ones[0:4, 0:1].broadcast_to([4, HALF])
            for hf in range(2):
                ini = 0.0 if hf == 0 else rows[0:4, 3, 0, HALF - 1:HALF]
                link(v.tensor_tensor_scan(rows[0:4, 3, hf, 0:HALF], one_row, x_f[:, hf, 0:HALF], ini, ALU.mult, ALU.add))
            link(v.tensor_tensor(tok(rows[0:4, 4]), tok(rows[0:4, 0]), tok(rows[0:4, 3]), ALU.subtract))
            for hf in range(2):
                ini = 0.0 if hf == 0 else rowc[0:4, 0, HALF - 1:HALF]
                link(v.tensor_tensor_scan(rowc[0:4, 0, hf * HALF:(hf + 1) * HALF], one_row, rows[0:4, 4, hf, 0:HALF], ini,
                                          ALU.mult, ALU.max))
            link(v.tensor_tensor(rowc[0:4, 1].rearrange("p (a b) -> p a b", a=2), tok(rows[0:4, 3]),
                                 rowc[0:4, 0].rearrange("p (a b) -> p a b", a=2), ALU.add))
            link(v.tensor_copy(rows[0:4, 5, 0, 0:8].rearrange("p (a b) -> p a b", a=2), smpl(rows[0:4, 0])))
            v.tensor_copy(rows[0:4, 5, 0, 8:16].rearrange("p (a b) -> p a b", a=2), smpl(x_f)).then_inc(for_pe, 1)
            settled(dve, for_pe)
            for i, key in enumerate(("stokA", "stokB")):
                g = use[key]
                wait_filled(dve, g)
                v.tensor_copy(stok[0:NS, i * 1024:(i + 1) * 1024], ps(g)[0:NS].rearrange("p a b -> p (a b)")).then_inc(for_store, 1)
                settled(dve, for_store)
                dve.wait_ge(for_store, i + 1)
                free(v.tensor_copy(sml[0:1, 9:10], ps(g)[0:1, 0, 0:1]), g)
                dve.wait_ge(freed[g % NGRP], g // NGRP + 1)
            g = use["acol"]
            wait_filled(dve, g)
            free(v.tensor_copy(acol[:], ps(g)[:, 0, 0:16].rearrange("p (a b) -> p a b", a=4)), g)
            dve.wait_ge(freed[g % NGRP], g // NGRP + 1)
            g = use["gs"]
            wait_filled(dve, g)
            free(v.tensor_copy(gst[0:NS], ps(g)[0:NS, 0, 0:8]), g)
            dve.wait_ge(freed[g % NGRP], g // NGRP + 1)
            dve.wait_ge(freed[g % NGRP], g // NGRP + 1)
            v.memset(sml[:, 10:11], 0.0).then_inc(for_store, 1)
            settled(dve, for_store)
            for h in range(H):
                cm = cmB[h % 2]
                dve.wait_ge(cm_ready, 2 * h + 2)
                for s_ in range(4):
                    n = SEQ - s_ * P
                    k = 4 * h + s_
                    v.tensor_tensor(Ex[k % 2][:, 0:n], cm[:, 0, s_ * P:SEQ], cn[:, C_MASK:C_MASK + n], ALU.add).then_inc(exq, 1)
                    settled(dve, exq)
                    g = use[("mS", h, s_)]
                    dve.wait_ge(pxq, k + 1)
                    wait_filled(dve, g)
                    if h == 0 and s_ == 0:
                        dve.wait_ge(keys_stored, 1)
                    if h >= 1 and s_ == 0:
                        wait_filled(dve, use[("mN", h - 1)])
                    v.tensor_tensor(PT[s_][:, 0:n], ps(g)[:, 0, 0:n], Ex[k % 2][:, 0:n], ALU.mult).then_inc(pt_ready, 1)
                    settled(dve, pt_ready)
                    dve.wait_ge(pt_ready, 5 * h + s_ + 1)
                    free(v.tensor_copy(sml[0:1, 11:12], ps(g)[0:1, 0, 0:1]), g)
                    dve.wait_ge(freed[g % NGRP], g // NGRP + 1)
                if h >= 1:
                    wait_filled(dve, use[("mC", h - 1)])
                v.tensor_tensor(kw[:], bkv[:, :, 512 + h * DK:512 + (h + 1) * DK],
                                wl[:].unsqueeze(2).broadcast_to([P, 4, DK]), ALU.mult).then_inc(pt_ready, 1)
                settled(dve, pt_ready)
                g = use[("mN", h)]
                wait_filled(dve, g)
                link(v.scalar_tensor_tensor(cm[:, 1], ps(g)[:, 1], -1.0, cm[:, 1], ALU.mult, ALU.max))
                link(v.tensor_tensor(cm[:, 1], ps(g)[:, 1], cm[:, 1], ALU.max))
                link(v.reciprocal(cm[:, 1], cm[:, 1]))
                free(v.tensor_tensor(tok(proj[:, 16 + h]), ps(g)[:, 0].rearrange("p (a b) -> p a b", a=2),
                                     cm[:, 1].rearrange("p (a b) -> p a b", a=2), ALU.mult), g)
                dve.wait_ge(freed[g % NGRP], g // NGRP + 1)
                g = use[("mC", h)]
                wait_filled(dve, g)
                link(v.tensor_copy(nst[0:1, h], ps(g)[0:1, 1, 0:DK]))
                free(v.tensor_copy(Cst[:, h], ps(g)[:, 0, 0:DK]), g)
                dve.wait_ge(freed[g % NGRP], g // NGRP + 1)
                dve.wait_ge(freed[g % NGRP], g // NGRP + 1)
                v.memset(sml[:, 10:11], 0.0).then_inc(for_pe, 1)
                settled(dve, for_pe)
            v.memset(sml[:, 10:11], 0.0).then_inc(for_store, 1)
            settled(dve, for_store)
            dve.wait_ge(for_store, 4)
            def scores(u):
                h, i = u // 4, u % 4
                n = (i + 1) * P
                g = use[("S", u)]
                S, s8_ = Sb[u % 2], st8[u % 2]
                wait_filled(dve, g)
                dist = cn[:, C_DIST + 512 - n:C_DIST + 512].unsqueeze(1).broadcast_to([P, 2, n])
                free(v.scalar_tensor_tensor(S[:, :, 0:n], dist, -(2.0 ** (-2.0 * (h + 1))), ps(g)[:, :, 0:n], ALU.mult, ALU.add), g)
                dve.wait_ge(freed[g % NGRP], g // NGRP + 1)
                dve.wait_ge(freed[g % NGRP], g // NGRP + 1)
                link(v.tensor_reduce(s8_[:, 4:6], S[:, :, 0:n], AX.X, ALU.max))
                v.tensor_scalar(s8_[:, 0:2], s8_[:, 4:6], -1.0, None, ALU.mult).then_inc(pb_ready, 1)
                settled(dve, pb_ready)

            def weights(u):
                n = (u % 4 + 1) * P
                S, s8_ = Sb[u % 2], st8[u % 2]
                dve.wait_ge(smax_ready, 2 * u + 2)
                link(v.reciprocal(s8_[:, 2:4], s8_[:, 2:4]))
                link(v.tensor_scalar(s8_[:, 3:4], s8_[:, 3:4], neglam[:, 0:1], None, ALU.mult))
                link(v.tensor_scalar(S[:, 1, 0:n], S[:, 1, 0:n], s8_[:, 3:4], None, ALU.mult))
                if u >= 2:
                    wait_filled(dve, use[("T", u - 2)])
                v.scalar_tensor_tensor(Wb[u % 2][:, 0:n], S[:, 0, 0:n], s8_[:, 2:3], S[:, 1, 0:n], ALU.mult, ALU.add).then_inc(w_ready, 1)
                settled(dve, w_ready)
                dve.wait_ge(w_ready, u + 1)

            def outputs(u):
                h, i = u // 4, u % 4
                g = use[("PV", u)]
                wait_filled(dve, g)
                free(v.tensor_copy(proj[:, h, i // 2, (i % 2) * P:(i % 2 + 1) * P], ps(g)[:, 0, 0:P]), g)
                dve.wait_ge(freed[g % NGRP], g // NGRP + 1)
            for s_ in range(18):
                if s_ < 16:
                    scores(s_)
                if 1 <= s_ < 17:
                    weights(s_ - 1)
                if s_ >= 2:
                    outputs(s_ - 2)
            g = use[("PV", 15)]
            dve.wait_ge(freed[g % NGRP], g // NGRP + 1)
            v.memset(sml[:, 10:11], 0.0).then_inc(region_q, 1)
            settled(dve, region_q)
            v.memset(sml[:, 10:11], 0.0).then_inc(for_store, 1)
            settled(dve, for_store)
            dve.wait_ge(region_p, 1)
            dve.wait_ge(state_loaded, 16)
            dve.wait_ge(state_n_loaded, 16)
            for b in range(NS):
                g = use[("qb", b)]
                wait_filled(dve, g)
                dve.wait_ge(past_k[b % 2], 32 * (b // 2 + 1))
                link(v.tensor_tensor(prod[:], Kp[b % 2][:], ps(g)[:, 0:1, :].broadcast_to([P, NPG, 512]), ALU.mult))
                v.tensor_reduce(Sc[:, :, b * 8:(b + 1) * 8], prod[:].rearrange("p g (r d) -> p g r d", d=DK), AX.X,
                                ALU.add).then_inc(k_used, 1)
                settled(dve, k_used)
                dve.wait_ge(k_used, b + 1)
                link(v.tensor_tensor(prod[:, 0, 0:256], Cs[:, b], ps(g)[:, 1, 0:256], ALU.mult))
                link(v.tensor_reduce(CqS[:, b], prod[:, 0, 0:256].rearrange("p (h k) -> p h k", h=H), AX.X, ALU.add))
                free(v.tensor_copy(kbc[:, b], ps(g)[:, 1, 256:512]), g)
                dve.wait_ge(freed[g % NGRP], g // NGRP + 1)
            link(v.tensor_tensor(np8[0:NS, 256:512], stok[0:NS, 0:256], stok[0:NS, 512:768], ALU.mult))
            link(v.tensor_reduce(sm8[0:NS, 40:44], np8[0:NS, 256:512].rearrange("p (r d) -> p r d", d=DK), AX.X, ALU.add))
            link(v.tensor_tensor(np8[0:NS, 256:512], stok[0:NS, 256:512], stok[0:NS, 768:1024], ALU.mult))
            link(v.tensor_reduce(sm8[0:NS, 44:48], np8[0:NS, 256:512].rearrange("p (r d) -> p r d", d=DK), AX.X, ALU.add))
            sel8 = cn[0:NS, C_SEL:C_SEL + 1024].rearrange("p (b m) -> p b m", b=8)
            link(v.tensor_tensor(s8[0:NS, 0:64].rearrange("p (b r) -> p b r", b=8), sel8[:, :, 0:8],
                                 sm8[0:NS, 40:48].unsqueeze(1).broadcast_to([NS, 8, 8]), ALU.mult))
            v.scalar_tensor_tensor(Comb[0:64], cn[0:64, C_COMB + 32:C_COMB + 64], neglam[0:64, 0:1],
                                   cn[0:64, C_COMB:C_COMB + 32], ALU.mult, ALU.add).then_inc(for_pe, 1)
            settled(dve, for_pe)
            ig, lf = gst[0:NS, 0:4], gst[0:NS, 4:8]
            link(v.tensor_tensor(sm8[0:NS, 4:8], lf, mpv[0:NS], ALU.add))
            link(v.tensor_tensor(sm8[0:NS, 0:4], sm8[0:NS, 4:8], ig, ALU.max))
            link(v.tensor_tensor(sm8[0:NS, 16:20], ig, sm8[0:NS, 0:4], ALU.subtract))
            v.tensor_tensor(sm8[0:NS, 20:24], sm8[0:NS, 4:8], sm8[0:NS, 0:4], ALU.subtract).then_inc(dve_q, 1)
            settled(dve, dve_q)
            q_, k_ = stok[0:NS, 1536:1792], stok[0:NS, 1792:2048]
            link(v.tensor_tensor(np8[0:NS, 256:512], q_, k_, ALU.mult))
            link(v.tensor_reduce(sm8[0:NS, 28:32], np8[0:NS, 256:512].rearrange("p (h k) -> p h k", h=H), AX.X, ALU.add))
            link(v.tensor_tensor(np8[0:NS, 256:512], q_, np8[0:NS, 0:256], ALU.mult))
            link(v.tensor_reduce(sm8[0:NS, 32:36], np8[0:NS, 256:512].rearrange("p (h k) -> p h k", h=H), AX.X, ALU.add))
            dve.wait_ge(act_q, 9)
            w8, g8 = sm8[0:NS, 16:20], sm8[0:NS, 20:24]
            link(v.tensor_tensor(sm8[0:NS, 48:52], sm8[0:NS, 28:32], w8, ALU.mult))
            link(v.tensor_tensor(sm8[0:NS, 52:56], sm8[0:NS, 32:36], g8, ALU.mult))
            link(v.tensor_tensor(sm8[0:NS, 56:60], sm8[0:NS, 48:52], sm8[0:NS, 52:56], ALU.add))
            link(v.scalar_tensor_tensor(sm8[0:NS, 60:64], sm8[0:NS, 56:60], -1.0, sm8[0:NS, 24:28], ALU.mult, ALU.max))
            link(v.tensor_tensor(sm8[0:NS, 56:60], sm8[0:NS, 56:60], sm8[0:NS, 60:64], ALU.max))
            link(v.reciprocal(sm8[0:NS, 56:60], sm8[0:NS, 56:60]))
            pack = sm8[0:NS, 64:80]
            link(v.tensor_copy(pack[:, 0:4], g8))
            link(v.tensor_copy(pack[:, 4:8], w8))
            link(v.tensor_tensor(pack[:, 8:12], sm8[0:NS, 48:52], sm8[0:NS, 56:60], ALU.mult))
            link(v.tensor_tensor(pack[:, 12:16], g8, sm8[0:NS, 56:60], ALU.mult))
            bc = lambda x: x.unsqueeze(2).broadcast_to([NS, H, DK])
            hk = lambda x: x.rearrange("p (h k) -> p h k", h=H)
            link(v.tensor_tensor(hk(np8[0:NS, 256:512]), hk(np8[0:NS, 0:256]), bc(g8), ALU.mult))
            link(v.tensor_tensor(hk(np8[0:NS, 0:256]), hk(k_), bc(w8), ALU.mult))
            link(v.tensor_tensor(np8[0:NS, 256:512], np8[0:NS, 256:512], np8[0:NS, 0:256], ALU.add))
            v.memset(sml[:, 10:11], 0.0).then_inc(for_store, 1)
            settled(dve, for_store)
            v.memset(sml[:, 10:11], 0.0).then_inc(for_pe, 1)
            settled(dve, for_pe)
            g = use["st"]
            wait_filled(dve, g)
            link(v.tensor_copy(Pq[0:64, 256:257], ps(g)[0:64, 1, 0:1]))
            free(v.scalar_tensor_tensor(Pq[0:64, 0:256], cn[0:64, C_DROW:C_DROW + 256], cn[0:64, C_SLOPE:C_SLOPE + 1],
                                        ps(g)[0:64, 0, 0:256], ALU.mult, ALU.add), g)
            dve.wait_ge(freed[g % NGRP], g // NGRP + 1)
            dve.wait_ge(freed[g % NGRP], g // NGRP + 1)
            link(v.tensor_reduce(t32[0:64, 0, 2:3], Pq[0:64], AX.X, ALU.max))
            v.tensor_scalar(t32[0:64, 0, 0:1], t32[0:64, 0, 2:3], -1.0, None, ALU.mult).then_inc(dve_q, 1)
            settled(dve, dve_q)
            dve.wait_ge(act_q, 10)
            link(v.reciprocal(t32[0:64, 0, 3:4], t32[0:64, 0, 1:2]))
            v.tensor_scalar(Pq[0:64], Pq[0:64], t32[0:64, 0, 3:4], None, ALU.mult).then_inc(for_pe, 1)
            settled(dve, for_pe)
            g = use["wT"]
            wait_filled(dve, g)
            v.tensor_copy(wTs[:], ps(g)[:, 0, 0:96].rearrange("p (a b) -> p a b", a=3)).then_inc(for_pe, 1)
            settled(dve, for_pe)
            dve.wait_ge(for_pe, 11)
            free(v.tensor_copy(sml[0:1, 11:12], ps(g)[0:1, 0, 0:1]), g)
            dve.wait_ge(freed[g % NGRP], g // NGRP + 1)
            def hb_view(x):
                return x.rearrange("p (b h) -> p h b", h=H)
            vnew = smp[:, 8:12]
            link(v.tensor_tensor(t32[:, 0].rearrange("p (h b) -> p h b", h=H), vnew, hb_view(wTs[:, 2]), ALU.mult))
            g = use["pvs"]
            wait_filled(dve, g)
            link(v.tensor_tensor(t32[:, 1].rearrange("p (h b) -> p h b", h=H), hb_view(ps(g)[:, 0, 0:32]),
                                 t32[:, 0].rearrange("p (h b) -> p h b", h=H), ALU.add))
            free(v.tensor_copy(sml[0:1, 11:12], ps(g)[0:1, 0, 0:1]), g)
            dve.wait_ge(freed[g % NGRP], g // NGRP + 1)
            link(v.tensor_copy(proj[:, 0:4, :, HALF:HT], t32[:, 1].rearrange("p (h a b) -> p h a b", h=H, a=2)))
            g = use["pk"]
            wait_filled(dve, g)
            free(v.tensor_copy(pks[:], ps(g)[:, 0, 0:128].rearrange("p (b r) -> p b r", b=NS)), g)
            dve.wait_ge(freed[g % NGRP], g // NGRP + 1)
            dve.wait_ge(freed[g % NGRP], g // NGRP + 1)
            bv = smp[:, 16:20].rearrange("p h b -> p b h")
            tt = t32[:].rearrange("p a (b h) -> p a b h", h=H)
            link(v.tensor_tensor(tt[:, 0], bv, pks[:, :, 8:12], ALU.mult))
            link(v.tensor_tensor(tt[:, 1], CqS[:], pks[:, :, 12:16], ALU.mult))
            link(v.tensor_tensor(tt[:, 0], tt[:, 0], tt[:, 1], ALU.add))
            for hf in range(2):
                link(v.tensor_copy(proj[:, 16:20, hf, HALF:HT], tt[:, 0, hf * HS:(hf + 1) * HS].rearrange("p b h -> p h b")))
            v.memset(sml[:, 10:11], 0.0).then_inc(for_pe, 1)
            settled(dve, for_pe)
            link(v.tensor_tensor(tt[:, 0], bv, pks[:, :, 4:8], ALU.mult))
            C4 = Cs[:].rearrange("p b (h k) -> p (b h) k", h=H)
            K4 = kbc[:].rearrange("p b (h k) -> p (b h) k", h=H)
            bck = lambda x: x.unsqueeze(2).broadcast_to([P, 32, DK])
            link(v.tensor_tensor(K4, K4, bck(t32[:, 0]), ALU.mult))
            link(v.tensor_copy(t32[:, 1].rearrange("p (b h) -> p b h", h=H), pks[:, :, 0:4]))
            link(v.tensor_tensor(C4, C4, bck(t32[:, 1]), ALU.mult))
            link(v.tensor_tensor(C4, C4, K4, ALU.add))
            v.memset(sml[:, 10:11], 0.0).then_inc(for_store, 1)
            settled(dve, for_store)
            for t in range(8):
                g = use[("rms", t)]
                dve.wait_ge(freed[g % NGRP], g // NGRP + 1)
                link(v.reciprocal(rmb[t % 2][:], rmb[t % 2][:]))
                src = proj[:, t] if t < 4 else proj[:, 12 + t]
                gain = gA[:, 0:1] if t < 4 else bT[:, 97 + t - 4:98 + t - 4]
                if t < 4:
                    v.scalar_tensor_tensor(mxb[t % 2][:], src, gain, rmb[t % 2][:], ALU.mult, ALU.mult).then_inc(mx_ready, 1)
                    settled(dve, mx_ready)
                else:
                    link(v.scalar_tensor_tensor(mxb[t % 2][:], src, gain, rmb[t % 2][:], ALU.mult, ALU.mult))
                    v.tensor_tensor(mxb[t % 2][:], mxb[t % 2][:], proj[:, 16 + t], ALU.mult).then_inc(mx_ready, 1)
                    settled(dve, mx_ready)
                dve.wait_ge(mix_hi, t + 1)
                v.tensor_tensor(ML[:, t], mxb[t % 2][:], MH[:, t].bitcast(F32), ALU.subtract).then_inc(mix_lo, 1)
                settled(dve, mix_lo)

        @block.vector
        def _(dve):
            link = chain(dve, dve_step)
            v = nc.vector

            def lo(c):
                if c >= n_chunks:
                    return
                s = chunk_stage[c]
                dve.wait_ge(hi_done, c + 1)
                if s.name == "gate":
                    src = raw[c % NRAW][:, 0:64].rearrange("p (k g m) -> p k g m", k=8, g=2)
                    vh = whi[c % 2][:, 0:1024].rearrange("p (k g m) -> p k g m", k=8, m=32)[:, :, 0:2, 0:4]
                    vl = wlo[c % 2][:, 0:1024].rearrange("p (k g m) -> p k g m", k=8, m=32)[:, :, 0:2, 0:4]
                    ins = v.tensor_tensor(vl, src, vh.bitcast(F32), ALU.subtract)
                else:
                    f = chunk_floats(c)
                    ins = v.tensor_tensor(wlo[c % 2][:, 0:f], raw[c % NRAW][:, 0:f], whi[c % 2][:, 0:f].bitcast(F32),
                                          ALU.subtract)
                ins.then_inc(lo_done, 1)
                settled(dve, lo_done)

            for tb in range(4):
                g = use[("tx", tb)]
                wait_filled(dve, g)
                off = (tb % 2) * P
                free(v.tensor_copy(xT[:, :, tb // 2, off:off + P], ps(g)[:].rearrange("p a (b c) -> p (a b) c", c=P)), g)
                dve.wait_ge(freed[g % NGRP], g // NGRP + 1)
            g = use["ra"]
            wait_filled(dve, g)
            rv = ps(g)[:, 0, 0:128].rearrange("p (k r) -> p k r", r=16)
            for hf in range(2):
                v.tensor_copy(xT[:, :, hf, HALF:HT], rv[:, :, hf * HS:(hf + 1) * HS])
            link(v.tensor_copy(lnT[:], rv[:, :, 8:16]))
            free(v.tensor_scalar(lnA[:], rv[:, :, 8:16], ALPHA, None, ALU.mult), g)
            dve.wait_ge(freed[g % NGRP], g // NGRP + 1)
            g = use["tc"]
            wait_filled(dve, g)
            dve.wait_ge(c_hi, 1)
            link(v.tensor_tensor(cH[:, :, 9:18], ps(g)[:, 0, 0:72].rearrange("p (k c) -> p k c", c=9),
                                 cH[:, :, 0:9].bitcast(F32), ALU.subtract))
            free(v.tensor_copy(sml[0:1, 0:1], ps(g)[0:1, 0, 0:1]), g)
            dve.wait_ge(freed[g % NGRP], g // NGRP + 1)
            dve.wait_ge(freed[g % NGRP], g // NGRP + 1)
            v.memset(sml[:, 1:2], 0.0).then_inc(c_lo, 1)
            settled(dve, c_lo)
            g = use["tb"]
            wait_filled(dve, g)
            link(v.tensor_copy(bT[:], ps(g)[:, 0, 0:101]))
            free(v.tensor_scalar(gA[:], ps(g)[:, 0, 96:97], 1.0 - LAM_INIT, None, ALU.mult), g)
            dve.wait_ge(freed[g % NGRP], g // NGRP + 1)
            g = use["to"]
            wait_filled(dve, g)
            free(v.tensor_copy(OT[:], ps(g)[:, 0, 0:400].rearrange("p (k r) -> p k r", r=40)), g)
            dve.wait_ge(freed[g % NGRP], g // NGRP + 1)
            dve.wait_ge(freed[g % NGRP], g // NGRP + 1)
            lam_ = OT[:, :, 39]
            link(v.tensor_scalar(sp8[:, 0], lam_, -1.0, None, ALU.mult))
            v.tensor_tensor(sp8[:, 1], sp8[:, 0], lam_, ALU.max).then_inc(dve_q, 1)
            settled(dve, dve_q)
            dve.wait_ge(dve_q, 1)
            link(v.tensor_scalar(sp8[:, 0], sp8[:, 0], 0.0, None, ALU.max))
            link(v.tensor_tensor(lamr[0:1, 0:64], lamr[0:1, 0:64], lamr[0:1, 64:128], ALU.mult))
            link(v.tensor_tensor(lamr[0:1, 64:128], lamr[0:1, 128:192], lamr[0:1, 192:256], ALU.mult))
            v.tensor_reduce(lamr[0:1, 256:258], lamr[0:1, 0:128].rearrange("p (a b) -> p a b", a=2), AX.X,
                            ALU.add).then_inc(dve_q, 1)
            settled(dve, dve_q)
            dve.wait_ge(act_q, 3)
            link(v.tensor_tensor(sp8[:, 0], sp8[:, 0], sp8[:, 1], ALU.add))
            v.tensor_scalar(sp8[:, 2], sp8[:, 0], 8.0, None, ALU.mult)
            link(v.tensor_scalar(sp8[:, 3], sp8[:, 0], -8.0, None, ALU.mult))
            link(v.tensor_tensor(lamr[0:1, 260:261], lamr[0:1, 259:260], lamr[0:1, 258:259], ALU.subtract))
            v.tensor_scalar(lamr[0:1, 261:262], lamr[0:1, 260:261], -LAM_INIT, None, ALU.add).then_inc(for_pe, 1)
            settled(dve, for_pe)
            g = use["lam"]
            wait_filled(dve, g)
            free(v.tensor_copy(neglam[:], ps(g)[:, 0, 0:1]), g)
            dve.wait_ge(freed[g % NGRP], g // NGRP + 1)
            lo(0)
            lo(1)
            dve.wait_ge(memset_done, 5)

            for l in range(2):
                s = st[f"ada{l}"]
                for c in range(s.n):
                    g = s.g0 + c
                    wait_filled(dve, g)
                    ins = v.tensor_copy(modrow[0:18, c * 256:(c + 1) * 256], ps(g)[0:18, 0, 0:256])
                    free(ins, g)
                    dve.wait_ge(freed[g % NGRP], g // NGRP + 1)
                    lo(s.c0 + c + 2)
                g = s.g0 + s.n - 1
                dve.wait_ge(freed[g % NGRP], g // NGRP + 1)
                v.memset(sml[:, 2:3], 0.0).then_inc(modrow_done, 1)
                settled(dve, modrow_done)
                g = use[("sel", l)]
                wait_filled(dve, g)
                free(v.tensor_tensor(modT[l][:], ps(g)[:, 0, 0:432].rearrange("p (r c) -> p r c", c=9),
                                     bT[:, l * 48:(l + 1) * 48].unsqueeze(2).broadcast_to([P, 48, 9]), ALU.add), g)
                dve.wait_ge(freed[g % NGRP], g // NGRP + 1)
                dve.wait_ge(freed[g % NGRP], g // NGRP + 1)
                for j in range(2):
                    q = 2 * l + j
                    r = q - 1
                    sc, sh, gt = (modT[l][:, (3 * j + i) * 8:(3 * j + i + 1) * 8] for i in (1, 0, 2))
                    link(v.tensor_scalar(G9[:, q], sc, 1.0, None, ALU.add))
                    link(v.tensor_scalar(gt, gt, 1.0, None, ALU.add))
                    if r < 0:
                        link(v.tensor_copy(B9[:, q], sh))
                    else:
                        lb = lnT[:, :, 4 + r:5 + r].broadcast_to([P, KD, 9])
                        lg = lnT[:, :, r:r + 1].broadcast_to([P, KD, 9])
                        link(v.tensor_tensor(B9[:, q], G9[:, q], lb, ALU.mult))
                        link(v.tensor_tensor(B9[:, q], B9[:, q], sh, ALU.add))
                        link(v.tensor_tensor(G9[:, q], G9[:, q], lg, ALU.mult))

            def make_u(q):
                r = q - 1

                def low(t):
                    dve.wait_ge(uhi_ready, 8 * q + t + 1)
                    v.tensor_tensor(UL[:, t], ub[t % 2][:], UH[:, t].bitcast(F32), ALU.subtract).then_inc(ulo_ready, 1)
                    settled(dve, ulo_ready)
                for t in range(KD):
                    if r >= 0:
                        dve.wait_ge(d_ready, 8 * r + t + 1)
                        if t >= 2:
                            dve.wait_ge(x_ready, 8 * r + t - 1)
                        v.tensor_tensor(nb[t % 2][:], db[t % 2][:], rstd[:], ALU.mult).then_inc(n_ready, 1)
                        settled(dve, n_ready)
                        dve.wait_ge(n_ready, 8 * r + t + 1)
                        n = nb[t % 2]
                    else:
                        n = xT[:, t]
                    if q == 4:
                        continue
                    link(v.tensor_tensor(stmp[:], smpl(n), G9[:, q, t, 1:9].rearrange("p (a b) -> p a b", a=2), ALU.mult))
                    v.tensor_scalar(tok(ub[t % 2]), tok(n), G9[:, q, t, 0:1], B9[:, q, t, 0:1], ALU.mult, ALU.add)
                    v.tensor_tensor(smpl(ub[t % 2]), stmp[:], B9[:, q, t, 1:9].rearrange("p (a b) -> p a b", a=2),
                                    ALU.add).then_inc(u_ready, 1)
                    settled(dve, u_ready)
                    if t >= 1:
                        low(t - 1)
                if q < 4:
                    low(KD - 1)
                if r < 0:
                    link(v.tensor_scalar(xT[:], xT[:], ALPHA, None, ALU.mult))

            def residual(r, t, g, last):
                gt = modT[r // 2][:, (3 * (r % 2) + 2) * 8 + t]
                x = xT[:, t]
                wait_filled(dve, g)
                link(v.tensor_tensor(stmp[:], ps(g)[:, :, HALF:HT], gt[:, 1:9].rearrange("p (a b) -> p a b", a=2), ALU.mult))
                free(v.scalar_tensor_tensor(tok(x), ps(g)[:, :, 0:HALF], gt[:, 0:1], tok(x), ALU.mult, ALU.add), g)
                dve.wait_ge(freed[g % NGRP], g // NGRP + 1)
                ins = v.tensor_tensor(smpl(x), stmp[:], smpl(x), ALU.add)
                if last:
                    ins.then_inc(z_ready, 1)
                    settled(dve, z_ready)
                else:
                    link(ins)

            def ln_stats(r):
                g = use[("lnm", r)]
                wait_filled(dve, g)
                free(v.tensor_copy(mu[:], pT(g)), g)
                dve.wait_ge(freed[g % NGRP], g // NGRP + 1)
                dve.wait_ge(freed[g % NGRP], g // NGRP + 1)
                v.tensor_tensor(tv[:], mu[:], mu[:], ALU.mult).then_inc(mu_ready, 1)
                settled(dve, mu_ready)
                dve.wait_ge(mu_ready, r + 1)
                g = use[("lnq", r)]
                wait_filled(dve, g)
                free(v.tensor_tensor(tv[:], pT(g), tv[:], ALU.subtract), g)
                dve.wait_ge(freed[g % NGRP], g // NGRP + 1)
                dve.wait_ge(freed[g % NGRP], g // NGRP + 1)
                link(v.tensor_scalar(tv[:], tv[:], 0.0, EPS, ALU.max, ALU.add))
                v.memset(sml[:, 3:4], 0.0).then_inc(var_ready, 1)
                settled(dve, var_ready)
                dve.wait_ge(sd_ready, r + 1)
                link(v.reciprocal(rstd[:], tv[:]))

            def ffn(l):
                for hf in range(2):
                    s = st[f"fi{l}{hf}"]
                    for c in range(s.n):
                        k = (2 * l + hf) * KH + c
                        g = s.g0 + 2 * c + 1
                        wait_filled(dve, g)
                        dve.wait_ge(freed[(g - 1) % NGRP], (g - 1) // NGRP + 1)
                        v.tensor_tensor(hb[c % 2][:], pT(g), silb[c % 2][:], ALU.mult).then_inc(h_ready, 1)
                        settled(dve, h_ready)
                        dve.wait_ge(h_ready, k + 1)
                        free(v.tensor_copy(sml[0:1, 4:5], ps(g)[0:1, 0, 0:1]), g)
                        dve.wait_ge(freed[g % NGRP], g // NGRP + 1)
                        lo(s.c0 + c + 2)
                        dve.wait_ge(hhi_ready, k + 1)
                        v.tensor_tensor(HL[:, c], hb[c % 2][:], HH[:, c].bitcast(F32), ALU.subtract).then_inc(hlo_ready, 1)
                        settled(dve, hlo_ready)
                    s = st[f"fo{l}{hf}"]
                    for c in range(s.n):
                        residual(2 * l + 1, c, s.g0 + c, hf == 1)
                        lo(s.c0 + c + 2)
                ln_stats(2 * l + 1)

            make_u(0)
            s = st["ein"]
            for c in range(s.n):
                for m in range(2):
                    t, g = 2 * c + m, s.g0 + 2 * c + m
                    wait_filled(dve, g)
                    scale = 0.125 if t < 4 or 12 <= t < 14 else 1.0
                    free(v.tensor_scalar(proj[:, t], pT(g), scale, None, ALU.mult), g)
                    dve.wait_ge(freed[g % NGRP], g // NGRP + 1)
                dve.wait_ge(freed[g % NGRP], g // NGRP + 1)
                v.memset(sml[:, 5:6], 0.0).then_inc(evac, 2)
                settled(dve, evac, 2)
                lo(s.c0 + c + 2)
            lo(st["gate"].c0 + 2)
            middle_dve(dve, link)
            s = st["eout"]
            for c in range(s.n):
                for m in range(2):
                    residual(0, 2 * c + m, s.g0 + 2 * c + m, True)
                lo(s.c0 + c + 2)
            ln_stats(0)
            make_u(1)
            ffn(0)
            make_u(2)
            s = st["oin"]
            dve.wait_ge(zero_ready, 1)
            for c in range(s.n):
                for m in range(2):
                    t = 2 * c + m - KR
                    g = s.g0 + 2 * c + m
                    if t < 0:
                        continue
                    wait_filled(dve, g)
                    link(v.tensor_copy(xrS[:, t].rearrange("p (a b) -> p a b", a=2), ps(g)[:, :, HALF:HT]))
                    free(v.tensor_copy(xr[:, t, 3:3 + SEQ].rearrange("p (a b) -> p a b", a=2), ps(g)[:, :, 0:HALF]), g)
                    dve.wait_ge(freed[g % NGRP], g // NGRP + 1)
                    dve.wait_ge(freed[g % NGRP], g // NGRP + 1)
                    v.tensor_copy(OS[:, t, 0:3], xr[:, t, SEQ:SEQ + 3]).then_inc(xr_ready, 1)
                    settled(dve, xr_ready)
                    dve.wait_ge(cv0, t + 1)
                    for j in range(1, 4):
                        link(v.scalar_tensor_tensor(tok(xc[:, t]), xr[:, t, j:j + SEQ].rearrange("p (a b) -> p a b", a=2),
                                                    OT[:, t, 32 + j:33 + j], tok(xc[:, t]), ALU.mult, ALU.add))
                if c < s.n - 0:
                    lo(s.c0 + c + 2)

            def per_tile(col, n=NS):
                return OT[:, :, col:col + 1].broadcast_to([P, KR, n])
            link(v.tensor_tensor(tS[:, 0], xrS[:], per_tile(35), ALU.mult))
            link(v.tensor_tensor(tS[:, 0], tS[:, 0], per_tile(36), ALU.add))
            for j in range(3):
                link(v.tensor_tensor(tS[:, 1], OT[:, :, j:24:3], per_tile(32 + j), ALU.mult))
                link(v.tensor_tensor(tS[:, 0], tS[:, 0], tS[:, 1], ALU.add))
            link(v.tensor_copy(OS[:, :, 3:11], xrS[:]))
            v.tensor_copy(xc[:, :, :, HALF:HT], tS[:, 0].rearrange("p k (a b) -> p k a b", a=2)).then_inc(cv_ready, 1)
            settled(dve, cv_ready)
            for t in range(KR):
                dve.wait_ge(xch, t + 1)
                v.tensor_tensor(XL[:, t], xc[:, t], XH[:, t].bitcast(F32), ALU.subtract).then_inc(xcl, 1)
                settled(dve, xcl)
            v.memset(sml[:, 6:7], 0.0).then_inc(for_store, 1)
            settled(dve, for_store)
            for w in ("wa", "wx"):
                s = st[w]
                for c in range(2):
                    if w == "wx":
                        for b in range(5):
                            g = s.g0 + 5 * c + b
                            t, k = 2 * b + c, 5 * c + b
                            dve.wait_ge(freed[g % NGRP], g // NGRP + 1)
                            v.tensor_tensor(xc[:, t], xc[:, t], isb[k % 2][:], ALU.mult).then_inc(ix_ready, 1)
                            settled(dve, ix_ready)
                    lo(s.c0 + c + 2)
            dve.wait_ge(ix_ready, KR)
            for t in range(KR):
                dve.wait_ge(a_ready, t + 1)
                v.scalar_tensor_tensor(qT[:, t], isb[t % 2][:], 1.0, qT[:, t], ALU.add, ALU.mult).then_inc(q_ready, 1)
                settled(dve, q_ready)
            for t in range(KR):
                dve.wait_ge(sqrt_ready, t + 1)
                link(v.tensor_tensor(qT[:, t], qT[:, t], xc[:, t], ALU.mult))
                link(v.tensor_tensor(stmp[:], smpl(aT[:, t]), OT[:, t, 24:32].rearrange("p (a b) -> p a b", a=2), ALU.mult))
                link(v.tensor_tensor_scan(rT[:, t, 0, 0:HALF], aT[:, t, 0, 0:HALF], qT[:, t, 0, 0:HALF], 0.0, ALU.mult, ALU.add))
                link(v.tensor_tensor_scan(rT[:, t, 1, 0:HALF], aT[:, t, 1, 0:HALF], qT[:, t, 1, 0:HALF],
                                          rT[:, t, 0, HALF - 1:HALF], ALU.mult, ALU.add))
                link(v.tensor_tensor(smpl(rT[:, t]), stmp[:], smpl(qT[:, t]), ALU.add))
                link(v.tensor_copy(OS[:, t, 11:12], rT[:, t, 1, HALF - 1:HALF]))
                link(v.tensor_copy(OS[:, t, 12:20].rearrange("p (a b) -> p a b", a=2), smpl(rT[:, t])))
                v.tensor_tensor(ysb[t % 2][:], rT[:, t], gT[:, t], ALU.mult).then_inc(y_ready, 1)
                settled(dve, y_ready)
                if t >= 1:
                    dve.wait_ge(yhi_ready, t)
                    v.tensor_tensor(YL[:, t - 1], ysb[(t - 1) % 2][:], YH[:, t - 1].bitcast(F32), ALU.subtract).then_inc(ylo_ready, 1)
                    settled(dve, ylo_ready)
            dve.wait_ge(yhi_ready, KR)
            v.tensor_tensor(YL[:, KR - 1], ysb[(KR - 1) % 2][:], YH[:, KR - 1].bitcast(F32), ALU.subtract).then_inc(ylo_ready, 1)
            settled(dve, ylo_ready)
            for i, key in enumerate(("osA", "osB")):
                g = use[key]
                wait_filled(dve, g)
                n = 1024 if i == 0 else 256
                ins = v.tensor_copy(OST[0:20, i * 1024:i * 1024 + n], ps(g)[0:20].rearrange("p a b -> p (a b)")[:, 0:n])
                free(ins, g)
                dve.wait_ge(freed[g % NGRP], g // NGRP + 1)
                dve.wait_ge(freed[g % NGRP], g // NGRP + 1)
                v.memset(sml[:, 7:8], 0.0).then_inc(out_ready, 1)
                settled(dve, out_ready)
            s = st["oout"]
            for c in range(s.n):
                residual(2, c, s.g0 + c, True)
                lo(s.c0 + c + 2)
            ln_stats(2)
            make_u(3)
            ffn(1)
            make_u(4)
            dve.wait_ge(x_ready, 32)
            v.tensor_copy(xsm[:].rearrange("p k (a b) -> p k a b", a=2), xT[:, :, :, HALF:HT]).then_inc(for_pe, 1)
            settled(dve, for_pe)
            for tb in range(4):
                g = use[("ty", tb)]
                wait_filled(dve, g)
                if tb >= 2:
                    dve.wait_ge(ytok_stored[tb % 2], 16)
                free(v.tensor_copy(ytok[tb % 2][:], ps(g)[:].rearrange("p a b -> p (a b)")), g)
                dve.wait_ge(freed[g % NGRP], g // NGRP + 1)
                dve.wait_ge(freed[g % NGRP], g // NGRP + 1)
                v.memset(sml[:, 7:8], 0.0).then_inc(out_ready, 1)
                settled(dve, out_ready)
            g = use["tys"]
            wait_filled(dve, g)
            v.tensor_copy(ysamp[0:NS], ps(g)[0:NS].rearrange("p a b -> p (a b)")).then_inc(out_ready, 1)
            settled(dve, out_ready)

        def middle_pe(pe, begin, done):
            T = nc.tensor

            def blk(t, tb, lo_=0, hi_=P):
                return proj[lo_:hi_, t, tb // 2, (tb % 2) * P:(tb % 2 + 1) * P]
            pe.wait_ge(evac, 24)
            for tb in range(4):
                g = use[("kv", tb)]
                begin(g)
                for i in range(8):
                    ins = T.transpose(ps(g)[:, i // 4, (i % 4) * P:(i % 4 + 1) * P], blk(4 + i, tb), ident)
                done(ins)
            for tb in range(4):
                g = use[("bkv", tb)]
                begin(g)
                for i in range(4):
                    T.transpose(ps(g)[:, 0, i * P:(i + 1) * P], blk(16 + i, tb), ident)
                for i in range(2):
                    ins = T.transpose(ps(g)[:, 1, i * P:(i + 1) * P], blk(14 + i, tb), ident)
                done(ins)
            pe.wait_ge(for_pe, 2)
            for key, tiles in (("stokA", list(range(8))), ("stokB", [8, 9, 10, 11, 12, 13, 14, 15])):
                g = use[key]
                begin(g)
                for i, t in enumerate(tiles):
                    ins = T.transpose(ps(g)[0:NS, i // 4, (i % 4) * P:(i % 4 + 1) * P], smp[:, t], ident)
                done(ins)
            pe.wait_ge(for_pe, 3)
            g = use["acol"]
            begin(g)
            for tb in range(4):
                ins = T.transpose(ps(g)[:, 0, 4 * tb:4 * tb + 4], rows[0:4, 4, tb // 2, (tb % 2) * P:(tb % 2 + 1) * P], ident[0:4, 0:4])
            done(ins)
            g = use["gs"]
            begin(g)
            T.transpose(ps(g)[0:NS, 0, 0:4], rows[0:4, 5, 0, 0:8], ident[0:4, 0:4])
            done(T.transpose(ps(g)[0:NS, 0, 4:8], rows[0:4, 5, 0, 8:16], ident[0:4, 0:4]))
            for h in range(H):
                g = use[("bc", h)]
                begin(g)
                sel = cn[0:4, C_SEL + h * P:C_SEL + (h + 1) * P]
                for j in range(2):
                    ins = T.matmul(ps(g)[:, j], sel, rowc[0:4, j], start=True, stop=True)
                done(ins)
                p0 = 64 * (h % 2)
                for s_ in range(4):
                    g = use[("mS", h, s_)]
                    begin(g)
                    kT = blk(14 + h // 2, s_, p0, p0 + 64)
                    n = 0
                    for tb in range(s_, 4):
                        ins = T.matmul(ps(g)[:, 0, n:n + P], kT, blk(12 + h // 2, tb, p0, p0 + 64), start=True, stop=True)
                        n += P
                    done(ins)
                g = use[("mN", h)]
                begin(g)
                pe.wait_ge(pt_ready, 5 * h + 4)
                for s_ in range(4):
                    n = SEQ - s_ * P
                    T.matmul(ps(g)[:, 0, s_ * P:SEQ], bkv[:, s_, h * DV:(h + 1) * DV], PT[s_][:, 0:n], start=(s_ == 0),
                             stop=(s_ == 3), skip_group_check=True)
                for s_ in range(4):
                    n = SEQ - s_ * P
                    ins = T.matmul(ps(g)[:, 1, s_ * P:SEQ], ones[:], PT[s_][:, 0:n], start=(s_ == 0), stop=(s_ == 3),
                                   skip_group_check=True)
                done(ins)
                g = use[("mC", h)]
                begin(g)
                pe.wait_ge(pt_ready, 5 * h + 5)
                for s_ in range(4):
                    T.matmul(ps(g)[:, 0, 0:DK], bkv[:, s_, h * DV:(h + 1) * DV], kw[:, s_], start=(s_ == 0), stop=(s_ == 3))
                for s_ in range(4):
                    ins = T.matmul(ps(g)[0:1, 1, 0:DK], wl[:, s_:s_ + 1], bkv[:, s_, 512 + h * DK:512 + (h + 1) * DK],
                                   start=(s_ == 0), stop=(s_ == 3))
                done(ins)
            def scores(u):
                h, i = u // 4, u % 4
                g = use[("S", u)]
                begin(g)
                for j in range(2):
                    q = blk(h, i, 64 * j, 64 * j + 64)
                    for hf in range(i // 2 + 1):
                        n = HALF if hf < i // 2 or i % 2 else P
                        ins = T.matmul(ps(g)[:, j, hf * HALF:hf * HALF + n], q, proj[64 * j:64 * j + 64, 4 + h, hf, 0:n],
                                       start=True, stop=True)
                done(ins)

            def transposes(u):
                g = use[("T", u)]
                begin(g)
                pe.wait_ge(w_ready, u + 1)
                for kb in range(u % 4 + 1):
                    ins = T.transpose(ps(g)[:, 0, kb * P:(kb + 1) * P], Wb[u % 2][:, kb * P:(kb + 1) * P], ident)
                done(ins)

            def pv(u):
                h, i = u // 4, u % 4
                g = use[("PV", u)]
                begin(g)
                pe.wait_ge(wT_ready, u + 1)
                for kb in range(i + 1):
                    ins = T.matmul(ps(g)[:, 0, 0:P], vtok[:, kb, h * DV:(h + 1) * DV], wTb[u % 2][:, kb * P:(kb + 1) * P],
                                   start=(kb == 0), stop=(kb == i))
                done(ins)
            for s_ in range(18):
                if s_ < 16:
                    scores(s_)
                if 1 <= s_ < 17:
                    transposes(s_ - 1)
                if s_ >= 2:
                    pv(s_ - 2)
            for b in range(NS):
                g = use[("qb", b)]
                begin(g)
                sel = cn[0:NS, C_SEL + b * P:C_SEL + (b + 1) * P]
                T.matmul(ps(g)[:, 0], sel, stok[0:NS, 0:512], start=True, stop=True)
                done(T.matmul(ps(g)[:, 1], sel, stok[0:NS, 1536:2048], start=True, stop=True))
            g = use["st"]
            begin(g)
            pe.wait_ge(for_pe, 8)
            for pg in range(NPG):
                T.transpose(ps(g)[0:64, 0, pg * P:(pg + 1) * P], Sc[:, pg], ident)
            done(T.matmul(ps(g)[0:64, 1, 0:1], s8[0:NS, 0:64], ones[0:NS, 0:1], start=True, stop=True))
            g = use["wT"]
            begin(g)
            pe.wait_ge(for_pe, 10)
            for pg in range(NPG):
                T.matmul(ps(g)[:, 0, pg * 32:(pg + 1) * 32], Pq[0:64, pg * P:(pg + 1) * P], Comb[0:64], start=True, stop=True)
            done(T.matmul(ps(g)[:, 0, 64:96], Pq[0:64, 256:257].broadcast_to([64, P]), Comb[0:64], start=True, stop=True))
            g = use["pvs"]
            begin(g)
            pe.wait_ge(for_pe, 11)
            for b in range(NS):
                pe.wait_ge(past_v[b % 3], 32 * (b // 3 + 1))
                for h in range(H):
                    for pg in range(NPG):
                        col = 4 * b + h
                        ins = T.matmul(ps(g)[:, 0, col:col + 1], Vp[b % 3][:, pg, h * DV:(h + 1) * DV], wTs[:, pg, col:col + 1],
                                       start=(pg == 0), stop=(pg == NPG - 1))
                if b < NS - 1:
                    ins.then_inc(v_used, 1)
            done(ins)
            g = use["pk"]
            begin(g)
            pe.wait_ge(for_pe, 9)
            for b in range(NS):
                ins = T.matmul(ps(g)[:, 0, 16 * b:16 * b + 16], cn[0:NS, C_SEL + b * P:C_SEL + (b + 1) * P], sm8[0:NS, 64:80],
                               start=True, stop=True)
            done(ins)
            for t in range(8):
                g = use[("rms", t)]
                begin(g)
                pe.wait_ge(rm_sq, t + 1)
                for hf in range(2):
                    ins = T.matmul(ps(g)[:, hf, 0:HT], onesV[:], rsq[t % 2][:, hf], start=True, stop=True)
                done(ins)

        @block.tensor
        def _(pe):
            T = nc.tensor

            def begin(g, it=None, per=0):
                if g >= NGRP:
                    pe.wait_ge(freed[g % NGRP], g // NGRP if it is None else g // NGRP + it * per)

            def done(ins):
                ins.then_inc(filled, 1)

            def products(s, c, xh, xl, it=None):
                gc = s.c0 + c
                pe.wait_ge(lo_done, gc + 1 if it is None else gc + 1 + it * NRAW)
                wh = whi[gc % 2][:, 0:s.k * s.m].rearrange("p (k m) -> p k m", m=s.m)
                wl_ = wlo[gc % 2][:, 0:s.k * s.m].rearrange("p (k m) -> p k m", m=s.m)
                for m in range(s.uses):
                    g = s.g0 + c * s.uses + m
                    begin(g, it, s.uses * NRAW // NGRP)
                    for k in range(s.k):
                        wc = slice(m * P, (m + 1) * P)
                        for w, x in ((wh, xh), (wh, xl), (wl_, xh)):
                            for hf in range(2):
                                ins = T.matmul(ps(g)[:, hf, 0:HT], w[:, k, wc], x[:, k, hf], start=(k == 0 and w is wh and x is xh),
                                               stop=(k == s.k - 1 and w is wl_))
                    done(ins)

            def gemm(name, xh, xl):
                s = st[name]
                bodies = s.n // NRAW
                c = 0
                if bodies > 1:
                    with pe.Fori(0, bodies) as it:
                        for c in range(NRAW):
                            products(s, c, xh, xl, it)
                    c = bodies * NRAW
                for c in range(c, s.n):
                    products(s, c, xh, xl)

            pe.wait_ge(consts_loaded, 16)
            pe.wait_ge(memset_done, 5)
            pe.wait_ge(x_loaded, 16)
            for tb in range(4):
                g = use[("tx", tb)]
                begin(g)
                for k in range(KD):
                    ins = T.transpose(ps(g)[:].rearrange("p a (b c) -> p (a b) c", c=P)[:, k], xtok[:, tb, k * P:(k + 1) * P], ident)
                done(ins)

            def rows_to_cols(g, src, n, cols, off=0):
                for k in range(cols):
                    ins = T.transpose(ps(g)[:, 0, off + k * n:off + (k + 1) * n], src[0:n, k * P:(k + 1) * P], ident[0:n, 0:n])
                return ins
            pe.wait_ge(small_loaded, 16 * N_SMALL)
            begin(use["ra"])
            done(rows_to_cols(use["ra"], RA, 16, KD))
            pe.wait_ge(silu_c, 1)
            begin(use["tc"])
            done(rows_to_cols(use["tc"], CR, 9, KD))
            begin(use["tb"])
            rows_to_cols(use["tb"], BR, 96, 1)
            done(rows_to_cols(use["tb"], NR, 5, 1, 96))
            begin(use["to"])
            done(rows_to_cols(use["to"], RO, 40, KR))
            begin(use["lam"])
            pe.wait_ge(for_pe, 1)
            done(T.matmul(ps(use["lam"])[:, 0, 0:1], ones[0:1, :], lamr[0:1, 261:262], start=True, stop=True))

            def mod_products(s, c, it=None):
                gc = s.c0 + c
                pe.wait_ge(lo_done, gc + 1 if it is None else gc + 1 + it * NRAW)
                g = s.g0 + c
                begin(g, it, 1)
                for k in range(KD):
                    for w in (whi, wlo):
                        ins = T.matmul(ps(g)[:, 0, 0:256], cH[:, k], w[gc % 2][:, k * 256:(k + 1) * 256],
                                       start=(k == 0 and w is whi), stop=(k == KD - 1 and w is wlo))
                done(ins)
            pe.wait_ge(c_lo, 1)
            for l in range(2):
                s = st[f"ada{l}"]
                with pe.Fori(0, s.n // NRAW) as it:
                    for c in range(NRAW):
                        mod_products(s, c, it)
                g = use[("sel", l)]
                begin(g)
                pe.wait_ge(modrow_done, l + 1)
                for k in range(48):
                    ins = T.matmul(ps(g)[:, 0, k * 9:(k + 1) * 9], modrow[0:18, k * P:(k + 1) * P], cn[0:18, C_ADA:C_ADA + 9],
                                   start=True, stop=True)
                done(ins)

            pe.wait_ge(ulo_ready, 8)
            gemm("ein", UH, UL)
            products(st["gate"], 0, UH, UL)
            middle_pe(pe, begin, done)
            pe.wait_ge(mix_lo, 8)
            gemm("eout", MH, ML)

            def ln_sums(r):
                pe.wait_ge(acc_step, 16 * r + 16)
                for key, acc in (("lnm", accS), ("lnq", accQ)):
                    g = use[(key, r)]
                    begin(g)
                    for hf in range(2):
                        ins = T.matmul(ps(g)[:, hf, 0:HT], onesD[:], acc[:, hf], start=True, stop=True)
                    done(ins)

            def ffn(l):
                pe.wait_ge(ulo_ready, 8 * (2 * l + 2))
                for hf in range(2):
                    gemm(f"fi{l}{hf}", UH, UL)
                    pe.wait_ge(hlo_ready, (2 * l + hf + 1) * KH)
                    gemm(f"fo{l}{hf}", HH, HL)
                ln_sums(2 * l + 1)
            ln_sums(0)
            ffn(0)
            pe.wait_ge(ulo_ready, 24)
            gemm("oin", UH, UL)
            pe.wait_ge(xcl, KR)
            for w in ("wa", "wx"):
                s = st[w]
                for c in range(2):
                    gc = s.c0 + c
                    pe.wait_ge(lo_done, gc + 1)
                    for b in range(5):
                        g = s.g0 + 5 * c + b
                        begin(g)
                        for k in range(2):
                            wc = slice((2 * b + k) * P, (2 * b + k + 1) * P)
                            for wt, x in ((whi, XH), (whi, XL), (wlo, XH)):
                                for hf in range(2):
                                    ins = T.matmul(ps(g)[:, hf, 0:HT], wt[gc % 2][:, wc], x[:, 2 * b + k, hf],
                                                   start=(k == 0 and wt is whi and x is XH), stop=(k == 1 and wt is wlo))
                        done(ins)
            pe.wait_ge(ylo_ready, KR)
            for i, key in enumerate(("osA", "osB")):
                g = use[key]
                begin(g)
                for k in range(8 if i == 0 else 2):
                    ins = T.transpose(ps(g)[0:20].rearrange("p a (b c) -> p (a b) c", c=P)[:, k], OS[:, 8 * i + k], ident)
                done(ins)
            gemm("oout", YH, YL)
            ln_sums(2)
            ffn(1)
            pe.wait_ge(x_ready, 32)
            for tb in range(4):
                g = use[("ty", tb)]
                begin(g)
                off = (tb % 2) * P
                for k in range(KD):
                    ins = T.transpose(ps(g)[:].rearrange("p a (b c) -> p (a b) c", c=P)[:, k], xT[:, k, tb // 2, off:off + P], ident)
                done(ins)
            g = use["tys"]
            begin(g)
            pe.wait_ge(for_pe, 13)
            for k in range(KD):
                ins = T.transpose(ps(g)[0:NS].rearrange("p a (b c) -> p (a b) c", c=P)[:, k], xsm[:, k], ident)
            done(ins)


_OUTS = [
    ("y_prompt", (1, 512, 1024)), ("y_sample", (8, 1, 1024)), ("k_prompt", (1, 1, 4, 128, 4, 2, 64)),
    ("v_prompt", (1, 1, 4, 128, 4, 128)), ("k_sample", (1, 8, 1, 4, 2, 64)), ("v_sample", (1, 8, 1, 4, 128)),
    ("C_prompt", (1, 1, 4, 128, 64)), ("n_prompt", (1, 1, 4, 64)), ("m_prompt", (1, 1, 4)),
    ("C_sample", (1, 8, 4, 128, 64)), ("n_sample", (1, 8, 4, 64)), ("m_sample", (1, 8, 4)),
    ("h_prompt", (1, 1, 1280)), ("conv_prompt", (1, 1, 3, 1280)), ("h_sample", (1, 8, 1280)),
    ("conv_sample", (1, 8, 3, 1280)),
]


def kernel(**inputs):
    import concourse.bacc as _bacc
    from concourse.bass_utils import run_bass_kernel_spmd as _run

    nc = _bacc.Bacc("TRN2", target_bir_lowering=False, num_devices=1)
    arrays, ins = {}, {}
    for name, value in list(inputs.items()) + [("consts", constants())]:
        arr = np.ascontiguousarray(value)
        arrays[f"in_{name}"] = arr
        ins[name] = nc.dram_tensor(f"in_{name}", arr.shape, mybir.dt.from_np(arr.dtype), kind="ExternalInput").ap()
    outs = {n: nc.dram_tensor(f"out_{n}", shape, F32, kind="ExternalOutput").ap() for n, shape in _OUTS}
    trunk(nc, ins, outs)
    r = _run(nc, [arrays], core_ids=[0])
    return tuple(r.results[0][f"out_{n}"] for n, _ in _OUTS)
```

```python
from contextlib import ExitStack
import math

import numpy as np
import concourse.bass as bass
from concourse import mybir

F32 = mybir.dt.float32
F32R = mybir.dt.float32r
I32 = mybir.dt.int32
ACT = mybir.ActivationFunctionType
ALU = mybir.AluOpType
AX = mybir.AxisListType

P = 128
D = 1024
KD = D // P
SEQ = 512
NS = 8
HALF = 256
HS = NS // 2
HT = HALF + HS
H = 4
DK = 64
DV = 128
DR = 1280
KR = DR // P
DFF = 2816
KF = DFF // P
KH = KF // 2
PAGE = 128
NPG = 2
NPOOL = 20
E_COLS = 3072
ALPHA = 4.0 ** 0.25
LAM_INIT = 0.2
BIG = 1e30
EPS = 1e-5
NRAW, NSPLIT, NGRP = 4, 2, 4
SLOT = 2048
STEPS, ADA_EARLY = 18, 6

C_ID, C_MASK, C_DIST, C_SEL, C_COMB, C_SLOPE, C_DROW, C_ADA = 0, 128, 640, 1152, 2176, 2240, 2241, 2498
C_SELV = 2507
C_END = 2571


def constants():
    c = np.zeros((P, C_END), np.float32)
    i = np.arange(P)
    c[:, C_ID:C_ID + P] = np.eye(P)
    c[:, C_MASK:C_MASK + P] = np.where(i[:, None] > i[None, :], BIG, 0.0)
    d = i[:, None] - np.arange(512)[None, :] + 384
    c[:, C_DIST:C_DIST + 512] = np.where(d >= 0, d, BIG)
    for b in range(8):
        c[b, C_SEL + b * P:C_SEL + (b + 1) * P] = 1.0
    for r in range(64):
        b, h, j = r // 8, (r // 2) % 4, r % 2
        c[r, C_COMB + (0 if j == 0 else 32) + b * 4 + h] = 1.0
        c[r, C_SLOPE] = -(2.0 ** (-2.0 * (h + 1)))
    c[:, C_DROW:C_DROW + 256] = (256 - np.arange(256))[None, :]
    for r in range(9):
        c[r, C_ADA + r] = 1.0
        c[r + 9, C_ADA + r] = 1.0
    for t in range(8):
        c[:, C_SELV + 8 * t + t] = 1.0 / DV
    return c


class Stage:

    def __init__(self, name, n, k, m, uses):
        self.name, self.n, self.k, self.m, self.uses = name, n, k, m, uses


def plan():
    st, use, order = {}, {}, []

    def one(*keys):
        for key in keys:
            use[key] = one.g
            one.g += 1
    one.g = 0

    def stage(name, n, k, m, uses):
        s = Stage(name, n, k, m, uses)
        s.c0, s.g0 = stage.c, one.g
        stage.c += n
        one.g += n * uses
        st[name] = s
        order.append(s)
    stage.c = 0

    one("tc", "tb")
    stage("ada0", 24, 8, 256, 2)
    one(*[("tx", i) for i in range(4)], "ra", "to", "lam")
    stage("ein", 12, 8, 256, 2)
    stage("gate", 1, 8, 128, 1)
    stage("ada1", 24, 8, 256, 0)

    def mod(c):
        one(("mod", c))
        if c >= 1:
            one(("sel", c - 1))
    for i in range(4):
        one(("kv", i))
        mod(i)
    for i in range(4):
        one(("bkv", i))
        if i < ADA_EARLY - 4:
            mod(4 + i)
    one("acol", "gs", ("S", 0))
    for s in range(STEPS):
        h, quarter = s // 4, s % 4
        if quarter == 0 and 1 <= h <= H:
            one(("mN", h - 1), ("mC", h - 1))
        if s < 16:
            if quarter == 0:
                one(("bc", h))
            one(("mS", h, quarter))
        if s >= 2:
            one(("PV", s - 2))
        one(("mod", ADA_EARLY + s))
        if s < 15:
            one(("S", s + 1))
        if 1 <= s < 17:
            one(("T", s - 1))
        one(("sel", ADA_EARLY + s - 1))
    one(("sel", 23), "stokA", "stokB")
    for b in range(NS):
        one(("qb", b))
    one("st", "wT", "pvs", "pk")
    one("rms")
    for t in range(8):
        one(("rb", t))
    stage("eout", 4, 8, 256, 2)
    one(("lnm", 0), ("lnq", 0))

    def ffn(l):
        for hf in range(2):
            stage(f"fi{l}{hf}", 11, 8, 256, 2)
            stage(f"fo{l}{hf}", 8, 11, 128, 1)
        one(("lnm", 2 * l + 1), ("lnq", 2 * l + 1))
    ffn(0)
    stage("oin", 10, 8, 256, 2)
    stage("wa", 2, 10, 128, 5)
    stage("wx", 2, 10, 128, 5)
    one("osA", "osB")
    stage("oout", 8, 10, 128, 1)
    one(("lnm", 2), ("lnq", 2))
    ffn(1)
    one(*[("ty", i) for i in range(4)], "tys")
    return st, use, order


def trunk(nc, a, o):
    st, use, order = plan()

    def mod_use(s, c):
        return use[("mod", c)] if s.name == "ada1" else s.g0 + (2 * c - 1 if c else 0)

    def sel_use(s, c):
        if s.name == "ada1":
            return use[("sel", c)]
        return s.g0 + (2 * c + 2 if c < s.n - 1 else 2 * c + 1)
    chunk_stage = {}
    for s in order:
        for c in range(s.c0, s.c0 + s.n):
            chunk_stage[c] = s
    n_chunks = len(chunk_stage)

    def chunk_last_use(c):
        s = chunk_stage[c]
        if s.name[:3] == "ada":
            return mod_use(s, c - s.c0)
        return s.g0 + (c - s.c0 + 1) * s.uses - 1

    def chunk_floats(c):
        s = chunk_stage[c]
        return s.k * s.m

    with ExitStack() as ctx:
        def sb(name, shape, dt=F32):
            return ctx.enter_context(nc.sbuf_tensor(name, shape, dt))

        def sem(name):
            return ctx.enter_context(nc.semaphore(name))

        raw = [sb(f"raw{i}", [P, SLOT]) for i in range(NRAW)]
        whi = [sb(f"whi{i}", [P, SLOT], F32R) for i in range(NSPLIT)]
        wlo = [sb(f"wlo{i}", [P, SLOT], F32R) for i in range(NSPLIT)]
        xT = sb("xT", [P, KD, 2, HT])
        cn = sb("cn", [P, C_END])
        modT = [sb(f"modT{l}", [P, 48, 9]) for l in range(2)]
        G9 = sb("G9", [P, 4, KD, 9])
        B9 = sb("B9", [P, 4, KD, 9])
        lnT = sb("lnT", [P, KD, 8])
        lnA = sb("lnA", [P, KD, 8])
        OT = sb("OT", [P, KR, 40])
        sp8 = sb("sp8", [P, 4, KR])
        bT = sb("bT", [P, 101])
        gA = sb("gA", [P, 1])
        neglam = sb("neglam", [P, 1])
        ones = sb("ones", [P, P])
        onesD = sb("onesD", [P, P])
        epsc = sb("epsc", [P, 1])
        stmp = sb("stmp", [P, 2, HS])
        sml = sb("sml", [P, 64])
        psig = sb("psig", [P, 1])
        xrS = sb("xrS", [P, KR, NS])
        tS = sb("tS", [P, 2, KR, NS])
        pgt = sb("pgt", [P, 16], I32)
        mpv = sb("mpv", [P, H])
        bgi = sb("bgi", [P, 2])
        ident = cn[:, C_ID:C_ID + P]

        base = (nc.sbuf_base + 31) // 32 * 32 if not callable(nc.sbuf_base) else None
        HTB = 2 * HT * 4
        cH = nc.alloc_sbuf_tensor_at("cH", [P, KD, 18], F32R, offset=base)
        OS = nc.alloc_sbuf_tensor_at("OS", [P, KR, 20], F32, offset=base)
        base += KR * 20 * 4

        def at(name, shape, off, dt=F32):
            return nc.alloc_sbuf_tensor_at(name, shape, dt, offset=base + off)

        O_U = 24 * HTB
        O_L = 40 * HTB
        accS, accQ = at("accS", [P, 2, HT], O_L), at("accQ", [P, 2, HT], O_L + HTB)
        sqb = [at(f"sqb{i}", [P, 2, HT], O_L + (2 + i) * HTB) for i in range(2)]
        mu, tv, rstd = (at(n, [P, 2, HT], O_L + (2 + i) * HTB) for i, n in enumerate(["mu", "tv", "rstd"]))
        db = [at(f"db{i}", [P, 2, HT], O_L + (5 + i) * HTB) for i in range(2)]
        nb = [at(f"nb{i}", [P, 2, HT], O_L + (7 + i) * HTB) for i in range(2)]
        ub = [at(f"ub{i}", [P, 2, HT], O_L + (9 + i) * HTB) for i in range(2)]
        UH, UL = at("UH", [P, KD, 2, HT], O_U, F32R), at("UL", [P, KD, 2, HT], O_U + 8 * HTB, F32R)
        xtok = at("xtok", [P, 4, D], 0)
        RA, CR = at("RA", [P, D], 16384), at("CR", [P, D], 20480)
        RO = at("RO", [P, DR], 24576)
        BR, NR = at("BR", [P, P], 29696), at("NR", [P, P], 30208)
        lamr = at("lamr", [P, 272], 30720)
        proj = at("proj", [P, 24, 2, HT], 0)
        O_M = O_U
        def am(name, shape, off, dt=F32):
            n = 4
            for x in shape[1:]:
                n *= x
            assert O_M + off + n <= O_L + 12 * HTB, name
            return at(name, shape, O_M + off, dt)

        vtok = am("vtok", [P, 4, 512], 0)
        bkv = am("bkv", [P, 4, 768], 8192)
        stok = am("stok", [P, 2048], 20480)
        smp = am("smp", [P, 24, NS], 28672)
        rowc = am("rowc", [P, 2, SEQ], 29440)
        acol = am("acol", [P, 4, H], 33536)
        gst = sml[:, 16:24]
        ncT = am("ncT", [P, 1], 33632)
        wl = am("wl", [P, 4], 33664)
        kw = am("kw", [P, 4, DK], 33696)
        Cst = am("Cst", [P, H, DK], 34720)
        nst = am("nst", [P, H, DK], 35744)
        cmB = [am(f"cmB{i}", [P, 2, 512], 36768 + i * 4096) for i in range(2)]
        PTall = am("PT", [P, 1280], 20480)
        Ex = [am("Ex0", [P, 512], 25600), am("Ex1", [P, 512], 53152)]
        pt_off = [0, 512, 896, 1152]
        PT = [PTall[:, pt_off[i]:pt_off[i] + 512 - i * P] for i in range(4)]
        rows = am("rows", [P, 6, 2, HT], 36768)
        ktok = am("ktok", [P, 4, 512], 20480)
        Sb = [at(f"Sb{i}", [P, 2, 512], 8 * HTB + i * 4096) for i in range(2)]
        Wb = [am(f"Wb{i}", [P, 512], 44960 + i * 2048) for i in range(2)]
        wTb = [am(f"wTb{i}", [P, 512], 49056 + i * 2048) for i in range(2)]
        st8 = [am(f"st8{i}", [P, 8], 55200 + i * 32) for i in range(2)]
        modrow = am("modrow", [P, 2, 256], 56192)
        Kp = [am(f"Kp{i}", [P, NPG, 512], i * 4096) for i in range(2)]
        Vp = [am(f"Vp{i}", [P, NPG, 512], 8192 + i * 4096) for i in range(3)]
        kbc = am("kbc", [P, NS, 256], 29440)
        prod = am("prod", [P, NPG, 512], 37632)
        Sc = am("Sc", [P, NPG, 64], 41728)
        Pq = am("Pq", [P, 257], 42240)
        s8 = am("s8", [P, 64], 43296)
        CqS = am("CqS", [P, NS, H], 44320)
        wTs = am("wTs", [P, 3, 32], 44448)
        pks = am("pks", [P, NS, 16], 44832)
        Comb = am("Comb", [P, 32], 45344)
        sm8 = am("sm8", [P, 96], 45472)
        np8 = am("np8", [P, 512], 45856)
        t32 = am("t32", [P, 2, 32], 44064)
        Cs = am("Cs", [P, NS, 256], 47968)
        MH, ML = at("MH", [P, 8, 2, HT], O_U, F32R), at("ML", [P, 8, 2, HT], O_U + 8 * HTB, F32R)
        rmb = [at(f"rmb{i}", [P, 2, HT], O_L + (4 + i) * HTB) for i in range(2)]
        rsq = [at(f"rsq{i}", [P, 2, HT], O_L + (6 + i) * HTB) for i in range(2)]
        mxb = [at(f"mxb{i}", [P, 2, HT], O_L + (8 + i) * HTB) for i in range(2)]
        HH, HL = at("HH", [P, KH, 2, HT], 0, F32R), at("HL", [P, KH, 2, HT], 11 * HTB, F32R)
        silb = [at(f"silb{i}", [P, 2, HT], O_L + (5 + i) * HTB) for i in range(2)]
        hb = [at(f"hb{i}", [P, 2, HT], O_L + (7 + i) * HTB) for i in range(2)]
        gT = at("gT", [P, KR, 2, HT], 0)
        rT = at("rT", [P, KR, 2, HT], 10 * HTB)
        xr = at("xr", [P, KR, 3 + SEQ], 10 * HTB)
        XH, XL = at("XH", [P, KR, 2, HT], 20 * HTB, F32R), at("XL", [P, KR, 2, HT], 30 * HTB, F32R)
        aT, qT = at("aT", [P, KR, 2, HT], 20 * HTB), at("qT", [P, KR, 2, HT], 30 * HTB)
        YH, YL = at("YH", [P, KR, 2, HT], 20 * HTB, F32R), at("YL", [P, KR, 2, HT], 30 * HTB, F32R)
        xc = at("xc", [P, KR, 2, HT], 40 * HTB)
        xc_end = 50
        isb = [at(f"isb{i}", [P, 2, HT], (xc_end + i) * HTB) for i in range(2)]
        ysb = [at(f"ysb{i}", [P, 2, HT], (xc_end + i) * HTB) for i in range(2)]
        OST = at("OST", [P, DR], 0)
        ytok = [at(f"ytok{i}", [P, D], i * 4096) for i in range(4)]
        ysamp = at("ysamp", [P, D], 16384)
        xsm = at("xsm", [P, KD, NS], 20480)

        psum = [ctx.enter_context(nc.psum_tensor(f"ps{i}", [P, 2, 512], F32)) for i in range(NGRP)]

        raw_loaded = [sem(f"raw_loaded{i}") for i in range(NRAW)]
        hi_done, lo_done = sem("hi_done"), sem("lo_done")
        filled = sem("psum_filled")
        freed = [sem(f"psum_freed{i}") for i in range(NGRP)]
        consts_loaded, x_loaded, small_loaded = sem("consts_loaded"), sem("x_loaded"), sem("small_loaded")
        memset_done = sem("memset_done")
        silu_c, c_hi, c_lo = sem("silu_c"), sem("c_hi"), sem("c_lo")
        dve_step, act_step, pool_step = sem("dve_step"), sem("act_step"), sem("pool_step")
        d_ready, n_ready, u_ready = sem("d_ready"), sem("n_ready"), sem("u_ready")
        uhi_ready, ulo_ready, x_ready = sem("uhi_ready"), sem("ulo_ready"), sem("x_ready")
        z_ready, sq_ready, acc_step = sem("z_ready"), sem("sq_ready"), sem("acc_step")
        mu_ready, var_ready, sd_ready = sem("mu_ready"), sem("var_ready"), sem("sd_ready")
        sil_ready, h_ready, hhi_ready, hlo_ready = sem("sil_ready"), sem("h_ready"), sem("hhi_ready"), sem("hlo_ready")
        evac = sem("proj_evacuated")
        act_q, dve_q = sem("act_answer"), sem("dve_ask")
        exq, pxq = sem("score_arg_ready"), sem("score_exp_ready")
        pt_ready, cm_ready = sem("pt_ready"), sem("cm_ready")
        for_pe = sem("dve_for_pe")
        pb_ready, w_ready = sem("p_ready"), sem("w_ready")
        smax_ready = sem("smax_ready")
        past_k = [sem(f"past_k{i}") for i in range(2)]
        past_v = [sem(f"past_v{i}") for i in range(3)]
        k_used, v_used = sem("past_k_used"), sem("past_v_used")
        state_loaded, region_q = sem("state_loaded"), sem("region_free")
        state_n_loaded = sem("state_n_loaded")
        region_p = sem("prompt_states_stored")
        for_store = sem("dve_for_store")
        stored = sem("stored")
        rm_sq, rm_sd, rm_in, mix_hi, mix_lo = sem("rms_sq"), sem("rms_sd"), sem("rms_in"), sem("mix_hi"), sem("mix_lo")
        mx_ready = sem("mixed_ready")
        xr_ready, cv0, cv_ready, xch, xcl = sem("xr_ready"), sem("conv_first"), sem("conv_ready"), sem("xc_hi"), sem("xc_lo")
        i_ready, ix_ready, a_ready, q_ready, sqrt_ready = sem("i_ready"), sem("ix_ready"), sem("a_ready"), sem("q_ready"), sem("sqrt_ready")
        y_ready, yhi_ready, ylo_ready = sem("y_ready"), sem("yhi_ready"), sem("ylo_ready")
        y_stored, c_loaded, rsq_used, rr_ready = sem("y_stored"), sem("c_loaded"), sem("rsq_used"), sem("rr_ready")
        out_ready = sem("out_ready")
        zero_ready = sem("history_zero")

        block = ctx.enter_context(nc.Block())

        def ps(g):
            return psum[g % NGRP]

        def wait_filled(eng, g):
            eng.wait_ge(filled, g + 1)

        def free(ins, g):
            ins.then_inc(freed[g % NGRP], 1)

        def chain(eng, s):
            n = [0]

            def link(ins):
                n[0] += 1
                ins.then_inc(s, 1)
                eng.wait_ge(s, n[0])
            return link

        landed = {}

        def settled(eng, s, n=1):
            landed[s] = landed.get(s, 0) + n
            eng.wait_ge(s, landed[s])

        def tok(t):
            return t[:, :, 0:HALF]

        def smpl(t):
            return t[:, :, HALF:HT]

        def pT(g):
            return ps(g)[:, :, 0:HT]

        def weight_view(s):
            n = s.name
            if n[:3] == "ada":
                return a["w_ada"][int(n[3])].rearrange("(k p) (c m) -> c p k m", p=P, m=256)
            if n == "ein":
                return a["w_in_even"][0][:, 0:E_COLS].rearrange("(k p) (c m) -> c p k m", p=P, m=256)
            if n == "eout":
                return a["w_out_even"][0].rearrange("(k p) (c m) -> c p k m", p=P, m=256)
            if n[:2] == "fi":
                l, hf = int(n[2]), int(n[3])
                v = a["w_ffn_in"][l].rearrange("(k p) (g c m) -> c p k g m", p=P, g=2, m=P)
                return v[hf * KH:(hf + 1) * KH]
            if n[:2] == "fo":
                l, hf = int(n[2]), int(n[3])
                return a["w_ffn_out"][l][hf * KH * P:(hf + 1) * KH * P].rearrange("(k p) (c m) -> c p k m", p=P, m=P)
            if n == "oin":
                return a["w_in_odd"][0].rearrange("(k p) (c m) -> c p k m", p=P, m=256)
            if n in ("wa", "wx"):
                w = a["w_a" if n == "wa" else "w_x"][0].rearrange("n r m -> (n r) m")
                return w.rearrange("(k p) (c m) -> c p k m", p=P, m=P)
            return a["w_out_odd"][0].rearrange("(k p) (c m) -> c p k m", p=P, m=P)

        def past(sp):
            sp.wait_ge(small_loaded, 16 * N_SMALL)
            sp.wait_ge(region_q, 1)
            sp.dma_start(Cs[:], a["state_C"][0].rearrange("b h v k -> v (b h) k")).then_inc(state_loaded, 16)
            pages = [None] * 16

            def page(b, g):
                return sp.value_load(pgt[0:1, 2 * b + g:2 * b + g + 1], min_val=0, max_val=NPOOL - 1)

            def load_k(b):
                if b >= 2:
                    sp.wait_ge(k_used, b - 1)
                for g in range(NPG):
                    pg = page(b, g)
                    src = a["cache_k"][0][bass.ds(pg, 1)].rearrange("a p h j d -> (a p) (h j d)")
                    sp.dma_start(Kp[b % 2][:, g], src).then_inc(past_k[b % 2], 16)

            def load_v(b):
                if b >= 3:
                    sp.wait_ge(v_used, b - 2)
                for g in range(NPG):
                    pg = page(b, g)
                    src = a["cache_v"][0][bass.ds(pg, 1)].rearrange("a p h d -> (a p) (h d)")
                    sp.dma_start(Vp[b % 3][:, g], src).then_inc(past_v[b % 3], 16)
            for b in range(NS):
                load_k(b)
                if b < 3:
                    load_v(b)
            for b in range(3, NS):
                load_v(b)

        N_SMALL = 15
        count = {}

        @block.sync
        def _(sp):
            def load(s, c, it=None):
                gc = s.c0 + c
                slot = gc % NRAW
                if gc >= NRAW:
                    sp.wait_ge(lo_done, gc - NRAW + 1 + (0 if it is None else it * NRAW))
                v = weight_view(s)
                if s.name[:2] == "fi":
                    src = v[bass.ds(c + it * NRAW, 1)].rearrange("a p k g m -> (a p) k g m") if it is not None else v[c]
                    dst = raw[slot][:].rearrange("p (k g m) -> p k g m", k=8, g=2)
                    for g in range(2):
                        sp.dma_start(dst[:, :, g], src[:, :, g]).then_inc(raw_loaded[slot], 16)
                else:
                    src = v[bass.ds(c + it * NRAW, 1)].rearrange("a p k m -> (a p) k m") if it is not None else v[c]
                    dst = raw[slot][:, 0:s.k * s.m].rearrange("p (k m) -> p k m", m=s.m)
                    kh = s.k // 2
                    sp.dma_start(dst[:, 0:kh], src[:, 0:kh]).then_inc(raw_loaded[slot], 16)
                    sp.dma_start(dst[:, kh:], src[:, kh:]).then_inc(raw_loaded[slot], 16)

            sp.dma_start(cn[:], a["consts"]).then_inc(consts_loaded, 16)
            sp.dma_start(xtok[:], a["x_prompt"][0].rearrange("(b p) d -> p b d", p=P)).then_inc(x_loaded, 16)
            for s in order:
                if s.name == "gate":
                    gc = s.c0
                    sp.wait_ge(lo_done, gc - NRAW + 1)
                    dst = raw[gc % NRAW][:, 0:64].rearrange("p (k g m) -> p k g m", k=8, g=2)
                    src = a["w_in_even"][0][:, E_COLS:E_COLS + 8].rearrange("(k p) (g m) -> p k g m", p=P, g=2)
                    for g in range(2):
                        sp.dma_start(dst[:, :, g], src[:, :, g]).then_inc(raw_loaded[gc % NRAW], 16)
                    continue
                peel = NRAW if s.c0 == 0 else 0
                for c in range(peel):
                    load(s, c)
                bodies = (s.n - peel) // NRAW
                if bodies > 1:
                    with sp.Fori(0, bodies) as it:
                        for c in range(NRAW):
                            load(s, peel + c, it=it)
                    peel += bodies * NRAW
                for c in range(peel, s.n):
                    load(s, c)
                if s.name == "eout":
                    past(sp)
            for tb in range(4):
                sp.wait_ge(out_ready, 3 + tb)
                sp.dma_start(o["y_prompt"][0][tb * P:(tb + 1) * P], ytok[tb][:]).then_inc(y_stored, 16)
            sp.wait_ge(out_ready, 7)
            sp.dma_start(o["y_sample"].rearrange("b t d -> (b t) d"), ysamp[0:NS]).then_inc(y_stored, 16)
            sp.wait_ge(y_stored, 16 * 5)

        @block.gpsimd
        def _(pool):
            link = chain(pool, pool_step)

            pool.memset(ones[:], 1.0).then_inc(memset_done, 1)
            settled(pool, memset_done)
            pool.memset(onesD[:], 1.0 / D).then_inc(memset_done, 1)
            settled(pool, memset_done)
            pool.memset(epsc[:], EPS).then_inc(memset_done, 1)
            settled(pool, memset_done)

            n = [0]

            def small(dst, src):
                pool.dma_start(dst, src).then_inc(small_loaded, 16)
                n[0] += 1
            small(RA[0:8], a["x_sample"].rearrange("b t d -> (b t) d"))
            small(RA[8:12], a["ln_g"].rearrange("l j d -> (l j) d"))
            small(RA[12:16], a["ln_b"].rearrange("l j d -> (l j) d"))
            small(RO[0:24], a["state_conv"][0].rearrange("b j d -> (b j) d"))
            small(RO[24:32], a["state_h"][0])
            small(RO[32:36], a["conv_w"][0])
            small(RO[36:37], a["conv_b"])
            small(RO[37:38], a["b_a"])
            small(RO[38:39], a["b_x"])
            small(RO[39:40], a["lru_lambda"])
            small(lamr[0:1, 0:256], a["lam"].rearrange("e r d -> e (r d)"))
            small(pgt[0:1, :], a["page_table"].rearrange("(e b) g -> e (b g)", e=1))
            small(mpv[0:NS], a["state_m"][0])
            small(bgi[0:4, 0:1], a["b_i"].rearrange("e h -> h e"))
            small(bgi[32:36, 1:2], a["b_f"].rearrange("e h -> h e"))
            assert n[0] == N_SMALL

            stores = [0]

            def store(dst, src):
                pool.dma_start(dst, src).then_inc(stored, 16)
                stores[0] += 1

            store(o["conv_sample"][0][:, 0:2, :], a["state_conv"][0][:, 1:3, :])

            for tb in range(4):
                g = use[("kv", tb)]
                pool.wait_ge(freed[g % NGRP], g // NGRP + 1)
                store(o["k_prompt"][0, 0, tb].rearrange("t h j d -> t (h j d)"), ktok[:, tb])
                store(o["v_prompt"][0, 0, tb].rearrange("t h d -> t (h d)"), vtok[:, tb])
            pool.wait_ge(for_store, 1)
            store(o["m_prompt"][0, 0].rearrange("(h e) -> h e", e=1), rowc[0:4, 1, SEQ - 1:SEQ])
            pool.wait_ge(stored, 16 * stores[0])
            for k in range(16):
                h, quarter = k // 4, k % 4
                n = SEQ - quarter * P
                g = use[("bc", h)]
                pool.wait_ge(freed[g % NGRP], g // NGRP + 1)
                if k >= 2:
                    g = use[("mS", (k - 2) // 4, (k - 2) % 4)]
                    pool.wait_ge(freed[g % NGRP], g // NGRP + 1)
                pool.tensor_tensor(Ex[k % 2][:, 0:n], cmB[h % 2][:, 0, quarter * P:SEQ], cn[:, C_MASK:C_MASK + n],
                                   ALU.add).then_inc(exq, 1)
                settled(pool, exq)
            pool.wait_ge(for_store, 2)
            store(o["C_prompt"][0, 0].rearrange("h v k -> v h k"), Cst[:])
            store(o["n_prompt"][0].rearrange("a h k -> a (h k)"), nst[0:1].rearrange("p h k -> p (h k)"))
            pool.wait_ge(stored, 16 * stores[0])
            pool.wait_ge(for_store, 3)
            pool.memset(np8[:], 0.0).then_inc(region_p, 1)
            settled(pool, region_p)
            pool.dma_start(np8[0:NS, 0:256], a["state_n"][0].rearrange("b h k -> b (h k)")).then_inc(state_n_loaded, 16)
            pool.wait_ge(for_store, 5)
            store(o["k_sample"][0].rearrange("b t h j d -> (b t) (h j d)"), stok[0:NS, 512:1024])
            store(o["v_sample"][0].rearrange("b t h d -> (b t) (h d)"), stok[0:NS, 1024:1536])
            pool.wait_ge(for_store, 6)
            store(o["m_sample"][0], sm8[0:NS, 0:4])
            store(o["n_sample"][0].rearrange("b h k -> b (h k)"), np8[0:NS, 256:512])
            pool.wait_ge(for_store, 7)
            store(o["C_sample"][0].rearrange("b h v k -> v (b h) k"), Cs[:].rearrange("p b (h k) -> p (b h) k", h=H))
            mid_stores = count["middle"] = stores[0]

            def ln_sums(r):
                if r == 0:
                    pool.wait_ge(stored, 16 * mid_stores)
                for t in range(KD):
                    pool.wait_ge(z_ready, 8 * r + t + 1)
                    k = 16 * r + 2 * t
                    if t == 0:
                        pool.tensor_copy(accS[:], xT[:, t]).then_inc(acc_step, 1)
                        settled(pool, acc_step)
                    else:
                        pool.wait_ge(acc_step, k)
                        pool.tensor_tensor(accS[:], accS[:], xT[:, t], ALU.add).then_inc(acc_step, 1)
                        settled(pool, acc_step)
                    pool.wait_ge(sq_ready, 8 * r + t + 1)
                    if t == 0:
                        pool.tensor_copy(accQ[:], sqb[t % 2][:]).then_inc(acc_step, 1)
                        settled(pool, acc_step)
                    else:
                        pool.tensor_tensor(accQ[:], accQ[:], sqb[t % 2][:], ALU.add).then_inc(acc_step, 1)
                        settled(pool, acc_step)

            def ln_center(r):
                pool.wait_ge(mu_ready, r + 1)
                for t in range(KD):
                    if t >= 2:
                        pool.wait_ge(n_ready, 8 * r + t - 1)
                    pool.tensor_tensor(db[t % 2][:], xT[:, t], mu[:], ALU.subtract).then_inc(d_ready, 1)
                    settled(pool, d_ready)

            for r in range(4):
                ln_sums(r)
                ln_center(r)
                if r == 1:
                    pool.wait_ge(ulo_ready, 8 * 3)
                    pool.memset(xr[:, :, 0:3], 0.0).then_inc(zero_ready, 1)
                    settled(pool, zero_ready)
                    pool.wait_ge(out_ready, 2)
                    store(o["conv_prompt"][0, 0], OST[0:3])
                    store(o["conv_sample"][0][:, 2, :], OST[3:11])
                    store(o["h_prompt"][0], OST[11:12])
                    store(o["h_sample"][0], OST[12:20])
                    count["rows_stored"] = stores[0]
            pool.wait_ge(stored, 16 * stores[0])

        def middle_act(act, link, hi):
            act.wait_ge(evac, 24)
            nc.scalar.activation(proj[:, 20:24], proj[:, 20:24], ACT.Sigmoid).then_inc(act_q, 1)
            settled(act, act_q)
            act.wait_ge(act_q, 4)
            g = use_gate
            wait_filled(act, g)
            act.wait_ge(dve_q, 3)
            nc.scalar.activation(rows[0:4, 0], ps(g)[0:4, :, 0:HT], ACT.Tanh, scale=1.0 / 15.0,
                                 bias=sml[0:4, 8:9]).then_inc(act_q, 1)
            settled(act, act_q)
            act.wait_ge(dve_q, 4)
            nc.scalar.activation(rows[0:4, 2], rows[0:4, 2], ACT.Exp, scale=-1.0).then_inc(act_q, 1)
            settled(act, act_q)
            act.wait_ge(act_q, 6)
            nc.scalar.activation(rows[0:4, 2], rows[0:4, 2], ACT.Ln, bias=1.0).then_inc(act_q, 1)
            settled(act, act_q)
            ada = st["ada1"]
            for tb in range(4):
                g = use[("kv", tb)]
                wait_filled(act, g)
                link(nc.scalar.activation(ktok[:, tb], ps(g)[:, 0], ACT.Identity))
                free(nc.scalar.activation(vtok[:, tb], ps(g)[:, 1], ACT.Identity), g)
                act.wait_ge(freed[g % NGRP], g // NGRP + 1)
                hi(ada.c0 + tb + 2)
            for tb in range(4):
                g = use[("bkv", tb)]
                wait_filled(act, g)
                free(nc.scalar.activation(bkv[:, tb], ps(g)[:].rearrange("p a b -> p (a b)")[:, 0:768], ACT.Identity), g)
                act.wait_ge(freed[g % NGRP], g // NGRP + 1)
                if tb < ADA_EARLY - 4:
                    hi(ada.c0 + 4 + tb + 2)

            def unit_exp(u):
                n = (u % 4 + 1) * P
                act.wait_ge(pb_ready, u + 1)
                for j in range(2):
                    ins = nc.scalar.activation(Sb[u % 2][:, j, 0:n], Sb[u % 2][:, j, 0:n], ACT.Exp,
                                               bias=st8[u % 2][:, j:j + 1], accum_out=st8[u % 2][:, 2 + j:3 + j])
                    ins.then_inc(smax_ready, 1)
                    settled(act, smax_ready)

            def head_rows(h):
                g = use[("bc", h)]
                wait_filled(act, g)
                cm = cmB[h % 2]
                if h >= 2:
                    act.wait_ge(for_pe, h + 2)
                link(nc.scalar.activation(cm[:, 0], ps(g)[:, 0], ACT.Identity))
                free(nc.scalar.activation(cm[:, 1], ps(g)[:, 1], ACT.Exp, scale=-1.0), g)
                act.wait_ge(freed[g % NGRP], g // NGRP + 1)

            def head_state_weights(h):
                nc.scalar.activation(ncT[:], cmB[h % 2][:, 0, SEQ - 1:SEQ], ACT.Copy, scale=-1.0).then_inc(cm_ready, 1)
                settled(act, cm_ready)
                if h >= 1:
                    act.wait_ge(for_pe, h + 3)
                nc.scalar.activation(wl[:], acol[:, :, h], ACT.Exp, bias=ncT[:]).then_inc(cm_ready, 1)
                settled(act, cm_ready)

            def decay(k):
                h, quarter = k // 4, k % 4
                n = SEQ - quarter * P
                act.wait_ge(exq, k + 1)
                nc.scalar.activation(Ex[k % 2][:, 0:n], Ex[k % 2][:, 0:n], ACT.Exp, scale=-1.0,
                                     bias=acol[:, quarter, h:h + 1]).then_inc(pxq, 1)
                settled(act, pxq)

            def unit_wT(u):
                n = (u % 4 + 1) * P
                g = use[("T", u)]
                wait_filled(act, g)
                if u >= 2:
                    wait_filled(act, use[("PV", u - 2)])
                free(nc.scalar.activation(wTb[u % 2][:, 0:n], ps(g)[:, 0, 0:n], ACT.Identity), g)
                act.wait_ge(freed[g % NGRP], g // NGRP + 1)
            act.wait_ge(for_store, 1)
            for s_ in range(STEPS):
                h, quarter = s_ // 4, s_ % 4
                if s_ < 16:
                    if quarter == 0:
                        head_rows(h)
                    unit_exp(s_)
                    decay(s_)
                if s_ >= 1:
                    hi(ada.c0 + ADA_EARLY + s_ + 1)
                if 1 <= s_ < 17:
                    unit_wT(s_ - 1)
                if s_ < 16 and quarter == 0:
                    head_state_weights(h)
            hi(ada.c0 + ada.n + 1)
            act.wait_ge(dve_q, 5)
            nc.scalar.activation(sm8[0:NS, 16:24], sm8[0:NS, 16:24], ACT.Exp).then_inc(act_q, 1)
            settled(act, act_q)
            nc.scalar.activation(sm8[0:NS, 24:28], sm8[0:NS, 0:4], ACT.Exp, scale=-1.0).then_inc(act_q, 1)
            settled(act, act_q)
            act.wait_ge(dve_q, 6)
            nc.scalar.activation(Pq[0:64], Pq[0:64], ACT.Exp, bias=t32[0:64, 0, 0:1],
                                 accum_out=t32[0:64, 0, 1:2]).then_inc(act_q, 1)
            settled(act, act_q)
            act.wait_ge(for_pe, 12)
            act.wait_ge(stored, 16 * count["middle"])
            for t in range(8):
                src = proj[:, t] if t < 4 else proj[:, 12 + t]
                if t >= 2:
                    act.wait_ge(rsq_used, t - 1)
                nc.scalar.activation(rsq[t % 2][:], src, ACT.Square).then_inc(rm_sq, 1)
                settled(act, rm_sq)
            g = use["rms"]
            wait_filled(act, g)
            free(nc.scalar.activation(rmb[0][0:8], ps(g)[0:8, :, 0:HT], ACT.Sqrt, bias=epsc[0:8]), g)
            act.wait_ge(freed[g % NGRP], g // NGRP + 1)
            for t in range(8):
                g = use[("rb", t)]
                if t < 4:
                    act.wait_ge(freed[g % NGRP], g // NGRP + 1)
                else:
                    act.wait_ge(mx_ready, t - 3)
                nc.scalar.activation(MH[:, t], mxb[t % 2][:], ACT.Identity).then_inc(mix_hi, 1)
                settled(act, mix_hi)

        def cm_sem(ins):
            ins.then_inc(cm_ready, 1)
            settled(nc.scalar, cm_ready)

        use_gate = st["gate"].g0

        @block.scalar
        def _(act):
            link = chain(act, act_step)

            def hi(c):
                if c >= n_chunks:
                    return
                s = chunk_stage[c]
                act.wait_ge(raw_loaded[c % NRAW], 32 * (c // NRAW + 1))
                if c >= NSPLIT:
                    wait_filled(act, chunk_last_use(c - NSPLIT))
                if s.name == "gate":
                    src = raw[c % NRAW][:, 0:64].rearrange("p (k g m) -> p k g m", k=8, g=2)
                    dst = whi[c % 2][:, 0:1024].rearrange("p (k g m) -> p k g m", k=8, m=32)[:, :, 0:2, 0:4]
                    ins = nc.scalar.activation(dst, src, ACT.Identity)
                else:
                    f = chunk_floats(c)
                    ins = nc.scalar.activation(whi[c % 2][:, 0:f], raw[c % NRAW][:, 0:f], ACT.Identity)
                ins.then_inc(hi_done, 1)
                settled(act, hi_done)

            act.dma_start(CR[0:1], a["c_prompt"]).then_inc(c_loaded, 16)
            act.dma_start(CR[1:9], a["c_sample"]).then_inc(c_loaded, 16)
            act.dma_start(BR[0:96], a["b_ada"].rearrange("l (r m) -> (l r) m", m=P)).then_inc(c_loaded, 16)
            act.dma_start(NR[0:1], a["attn_norm_g"]).then_inc(c_loaded, 16)
            act.dma_start(NR[1:5], a["mlstm_norm_g"][0]).then_inc(c_loaded, 16)
            act.wait_ge(c_loaded, 80)
            nc.scalar.activation(CR[0:9], CR[0:9], ACT.Silu).then_inc(silu_c, 1)
            settled(act, silu_c)
            hi(0)
            hi(1)
            act.wait_ge(memset_done, 3)
            wait_filled(act, use["tc"])
            nc.scalar.activation(cH[:, :, 0:9], ps(use["tc"])[:, 0, 0:72].rearrange("p (k c) -> p k c", c=9),
                                 ACT.Identity).then_inc(c_hi, 1)
            settled(act, c_hi)
            for c in range(24):
                hi(c + 2)
            act.wait_ge(dve_q, 1)
            nc.scalar.activation(sp8[:, 1], sp8[:, 1], ACT.Exp, scale=-1.0).then_inc(act_q, 1)
            settled(act, act_q)
            act.wait_ge(dve_q, 2)
            nc.scalar.activation(lamr[0:1, 258:260], lamr[0:1, 256:258], ACT.Exp).then_inc(act_q, 1)
            settled(act, act_q)
            act.wait_ge(act_q, 2)
            nc.scalar.activation(sp8[:, 1], sp8[:, 1], ACT.Ln, bias=1.0).then_inc(act_q, 1)
            settled(act, act_q)

            def split_u(q):
                r = q - 1
                for t in range(KD):
                    if r >= 0:
                        act.wait_ge(n_ready, 8 * r + t + 1)
                        lt = lnT if r == 3 else lnA
                        nc.scalar.activation(xT[:, t], nb[t % 2][:], ACT.Identity, scale=lt[:, t, r:r + 1],
                                             bias=lt[:, t, 4 + r:5 + r]).then_inc(x_ready, 1)
                        settled(act, x_ready)
                    if q < 4:
                        act.wait_ge(u_ready, 8 * q + t + 1)
                        nc.scalar.activation(UH[:, t], ub[t % 2][:], ACT.Identity).then_inc(uhi_ready, 1)
                        settled(act, uhi_ready)

            def squares(r, t):
                act.wait_ge(z_ready, 8 * r + t + 1)
                if t >= 2:
                    act.wait_ge(acc_step, 16 * r + 2 * (t - 2) + 2)
                nc.scalar.activation(sqb[t % 2][:], xT[:, t], ACT.Square).then_inc(sq_ready, 1)
                settled(act, sq_ready)

            def ln_sqrt(r):
                act.wait_ge(var_ready, r + 1)
                nc.scalar.activation(tv[:], tv[:], ACT.Sqrt).then_inc(sd_ready, 1)
                settled(act, sd_ready)

            def ffn(l):
                for hf in range(2):
                    s = st[f"fi{l}{hf}"]
                    for c in range(s.n):
                        k = (2 * l + hf) * KH + c
                        g = s.g0 + 2 * c
                        wait_filled(act, g)
                        if k >= 2:
                            act.wait_ge(h_ready, k - 1)
                        ins = nc.scalar.activation(silb[c % 2][:], pT(g), ACT.Silu)
                        free(ins, g)
                        act.wait_ge(freed[g % NGRP], g // NGRP + 1)
                        hi(s.c0 + c + 2)
                        act.wait_ge(h_ready, k + 1)
                        if l == 1 and hf == 0 and c == 0:
                            act.wait_ge(stored, 16 * count["rows_stored"])
                        nc.scalar.activation(HH[:, c], hb[c % 2][:], ACT.Identity).then_inc(hhi_ready, 1)
                        settled(act, hhi_ready)
                    s = st[f"fo{l}{hf}"]
                    for c in range(s.n):
                        hi(s.c0 + c + 2)
                        if hf == 1 and c >= 1:
                            squares(2 * l + 1, c - 1)
                squares(2 * l + 1, KD - 1)
                ln_sqrt(2 * l + 1)

            split_u(0)
            for c in range(12):
                hi(st["ein"].c0 + c + 2)
            hi(st["gate"].c0 + 2)
            middle_act(act, link, hi)
            for c in range(4):
                hi(st["eout"].c0 + c + 2)
                if c >= 1:
                    squares(0, 2 * c - 2)
                    squares(0, 2 * c - 1)
            squares(0, 6)
            squares(0, 7)
            ln_sqrt(0)
            split_u(1)
            ffn(0)
            split_u(2)
            s = st["oin"]
            for c in range(s.n):
                hi(s.c0 + c + 2)
                for m in range(2):
                    t = 2 * c + m
                    g = s.g0 + t
                    if t < KR:
                        wait_filled(act, g)
                        free(nc.scalar.activation(gT[:, t], pT(g), ACT.Gelu_apprx_tanh), g)
                        act.wait_ge(freed[g % NGRP], g // NGRP + 1)
                    else:
                        t -= KR
                        act.wait_ge(xr_ready, t + 1)
                        nc.scalar.activation(tok(xc[:, t]), xr[:, t, 0:SEQ].rearrange("p (a b) -> p a b", a=2),
                                             ACT.Identity, scale=OT[:, t, 32:33],
                                             bias=OT[:, t, 36:37]).then_inc(cv0, 1)
                        settled(act, cv0)
            for t in range(KR):
                act.wait_ge(cv_ready, 1)
                nc.scalar.activation(XH[:, t], xc[:, t], ACT.Identity).then_inc(xch, 1)
                settled(act, xch)
            for w, col in (("wa", 37), ("wx", 38)):
                s = st[w]
                for c in range(2):
                    for b in range(5):
                        g = s.g0 + 5 * c + b
                        t = 2 * b + c
                        wait_filled(act, g)
                        if w == "wa":
                            if g == s.g0:
                                act.wait_ge(for_store, 8)
                            ins = nc.scalar.activation(rT[:, t], pT(g), ACT.Sigmoid, bias=OT[:, t, col:col + 1])
                            free(ins, g)
                            act.wait_ge(freed[g % NGRP], g // NGRP + 1)
                        else:
                            k = 5 * c + b
                            if k >= 2:
                                act.wait_ge(ix_ready, k - 1)
                            ins = nc.scalar.activation(isb[k % 2][:], pT(g), ACT.Sigmoid, bias=OT[:, t, col:col + 1])
                            free(ins, g)
                            act.wait_ge(freed[g % NGRP], g // NGRP + 1)
                    hi(s.c0 + c + 2)
            act.wait_ge(xcl, KR)
            act.wait_ge(ix_ready, KR)
            act.wait_ge(freed[(st["wx"].g0 + 9) % NGRP], (st["wx"].g0 + 9) // NGRP + 1)
            for t in range(KR):
                link(nc.scalar.activation(aT[:, t], rT[:, t], ACT.Exp, scale=sp8[:, 3, t:t + 1]))
                nc.scalar.activation(qT[:, t], rT[:, t], ACT.Tanh, scale=sp8[:, 2, t:t + 1])
                if t >= 2:
                    act.wait_ge(q_ready, t - 1)
                nc.scalar.activation(isb[t % 2][:], aT[:, t], ACT.Square).then_inc(a_ready, 1)
                settled(act, a_ready)
            for t in range(KR):
                act.wait_ge(q_ready, t + 1)
                nc.scalar.activation(qT[:, t], qT[:, t], ACT.Sqrt).then_inc(sqrt_ready, 1)
                settled(act, sqrt_ready)
            for t in range(KR):
                act.wait_ge(y_ready, t + 1)
                nc.scalar.activation(YH[:, t], ysb[t % 2][:], ACT.Identity).then_inc(yhi_ready, 1)
                settled(act, yhi_ready)
            s = st["oout"]
            for c in range(s.n):
                hi(s.c0 + c + 2)
                if c >= 1:
                    squares(2, c - 1)
            squares(2, KD - 1)
            ln_sqrt(2)
            split_u(3)
            ffn(1)
            split_u(4)

        def middle_dve(dve, link, lo, modulation_rows, select, modulation_sums):
            v = nc.vector
            v.tensor_copy(smp[:, 0:20].rearrange("p t (a b) -> p t a b", a=2), proj[:, 0:20, :, HALF:HT]).then_inc(for_pe, 1)
            settled(dve, for_pe)
            v.tensor_scalar(sml[0:4, 8:9], bgi[0:4, 0:1], 1.0 / 15.0, None, ALU.mult).then_inc(dve_q, 1)
            settled(dve, dve_q)
            g = use_gate
            wait_filled(dve, g)
            x_f = rows[0:4, 1]
            link(v.tensor_scalar(x_f, ps(g)[32:36, :, 0:HT], bgi[32:36, 1:2], None, ALU.add))
            link(v.tensor_scalar(rows[0:4, 2], x_f, -1.0, None, ALU.mult))
            v.tensor_tensor(rows[0:4, 2], rows[0:4, 2], x_f, ALU.max).then_inc(dve_q, 1)
            settled(dve, dve_q)
            dve.wait_ge(dve_q, 4)
            link(v.tensor_scalar(x_f, x_f, 0.0, None, ALU.min))
            dve.wait_ge(act_q, 7)
            free(v.tensor_scalar(rows[0:4, 0], rows[0:4, 0], 15.0, None, ALU.mult), g)
            dve.wait_ge(freed[g % NGRP], g // NGRP + 1)
            link(v.tensor_tensor(x_f, x_f, rows[0:4, 2], ALU.subtract))
            one_row = ones[0:4, 0:1].broadcast_to([4, HALF])
            for hf in range(2):
                ini = 0.0 if hf == 0 else rows[0:4, 3, 0, HALF - 1:HALF]
                link(v.tensor_tensor_scan(rows[0:4, 3, hf, 0:HALF], one_row, x_f[:, hf, 0:HALF], ini, ALU.mult, ALU.add))
            link(v.tensor_tensor(tok(rows[0:4, 4]), tok(rows[0:4, 0]), tok(rows[0:4, 3]), ALU.subtract))
            for hf in range(2):
                ini = 0.0 if hf == 0 else rowc[0:4, 0, HALF - 1:HALF]
                link(v.tensor_tensor_scan(rowc[0:4, 0, hf * HALF:(hf + 1) * HALF], one_row, rows[0:4, 4, hf, 0:HALF], ini,
                                          ALU.mult, ALU.max))
            link(v.tensor_tensor(rowc[0:4, 1].rearrange("p (a b) -> p a b", a=2), tok(rows[0:4, 3]),
                                 rowc[0:4, 0].rearrange("p (a b) -> p a b", a=2), ALU.add))
            link(v.tensor_copy(rows[0:4, 5, 0, 0:8].rearrange("p (a b) -> p a b", a=2), smpl(rows[0:4, 0])))
            v.tensor_copy(rows[0:4, 5, 0, 8:16].rearrange("p (a b) -> p a b", a=2), smpl(x_f)).then_inc(for_pe, 1)
            settled(dve, for_pe)
            ada = st["ada1"]
            for c in range(ADA_EARLY):
                modulation_rows(ada, c)
                lo(ada.c0 + c + 2)
                if c >= 1:
                    select(ada, c - 1)
            g = use["acol"]
            wait_filled(dve, g)
            free(v.tensor_copy(acol[:], ps(g)[:, 0, 0:16].rearrange("p (a b) -> p a b", a=4)), g)
            dve.wait_ge(freed[g % NGRP], g // NGRP + 1)
            g = use["gs"]
            wait_filled(dve, g)
            free(v.tensor_copy(gst[0:NS], ps(g)[0:NS, 0, 0:8]), g)
            dve.wait_ge(freed[g % NGRP], g // NGRP + 1)
            v.memset(sml[:, 10:11], 0.0).then_inc(for_store, 1)
            settled(dve, for_store)

            def scores(u):
                h, i = u // 4, u % 4
                n = (i + 1) * P
                g = use[("S", u)]
                S, s8_ = Sb[u % 2], st8[u % 2]
                wait_filled(dve, g)
                dist = cn[:, C_DIST + 512 - n:C_DIST + 512].unsqueeze(1).broadcast_to([P, 2, n])
                free(v.scalar_tensor_tensor(S[:, :, 0:n], dist, -(2.0 ** (-2.0 * (h + 1))), ps(g)[:, :, 0:n], ALU.mult, ALU.add), g)
                dve.wait_ge(freed[g % NGRP], g // NGRP + 1)
                link(v.tensor_reduce(s8_[:, 4:6], S[:, :, 0:n], AX.X, ALU.max))
                v.tensor_scalar(s8_[:, 0:2], s8_[:, 4:6], -1.0, None, ALU.mult).then_inc(pb_ready, 1)
                settled(dve, pb_ready)

            def weights(u):
                n = (u % 4 + 1) * P
                S, s8_ = Sb[u % 2], st8[u % 2]
                dve.wait_ge(smax_ready, 2 * u + 2)
                link(v.reciprocal(s8_[:, 2:4], s8_[:, 2:4]))
                link(v.tensor_scalar(s8_[:, 3:4], s8_[:, 3:4], neglam[:, 0:1], None, ALU.mult))
                link(v.tensor_scalar(S[:, 1, 0:n], S[:, 1, 0:n], s8_[:, 3:4], None, ALU.mult))
                if u >= 2:
                    wait_filled(dve, use[("T", u - 2)])
                v.scalar_tensor_tensor(Wb[u % 2][:, 0:n], S[:, 0, 0:n], s8_[:, 2:3], S[:, 1, 0:n], ALU.mult, ALU.add).then_inc(w_ready, 1)
                settled(dve, w_ready)

            def outputs(u):
                h, i = u // 4, u % 4
                g = use[("PV", u)]
                wait_filled(dve, g)
                free(v.tensor_copy(proj[:, h, i // 2, (i % 2) * P:(i % 2 + 1) * P], ps(g)[:, 0, 0:P]), g)
                dve.wait_ge(freed[g % NGRP], g // NGRP + 1)

            def decayed(k):
                h, quarter = k // 4, k % 4
                n = SEQ - quarter * P
                g = use[("mS", h, quarter)]
                dve.wait_ge(pxq, k + 1)
                wait_filled(dve, g)
                if h >= 1 and quarter == 0:
                    wait_filled(dve, use[("mN", h - 1)])
                free(v.tensor_tensor(PT[quarter][:, 0:n], ps(g)[:, 0, 0:n], Ex[k % 2][:, 0:n], ALU.mult), g)
                dve.wait_ge(freed[g % NGRP], g // NGRP + 1)

            def state_keys(h):
                dve.wait_ge(cm_ready, 2 * h + 2)
                if h >= 1:
                    wait_filled(dve, use[("mC", h - 1)])
                v.tensor_tensor(kw[:], bkv[:, :, 512 + h * DK:512 + (h + 1) * DK],
                                wl[:].unsqueeze(2).broadcast_to([P, 4, DK]), ALU.mult).then_inc(pt_ready, 1)
                settled(dve, pt_ready)

            def head_end(h):
                cm = cmB[h % 2]
                g = use[("mN", h)]
                wait_filled(dve, g)
                link(v.scalar_tensor_tensor(cm[:, 1], ps(g)[:, 1], -1.0, cm[:, 1], ALU.mult, ALU.max))
                link(v.tensor_tensor(cm[:, 1], ps(g)[:, 1], cm[:, 1], ALU.max))
                link(v.reciprocal(cm[:, 1], cm[:, 1]))
                free(v.tensor_tensor(tok(proj[:, 16 + h]), ps(g)[:, 0].rearrange("p (a b) -> p a b", a=2),
                                     cm[:, 1].rearrange("p (a b) -> p a b", a=2), ALU.mult), g)
                dve.wait_ge(freed[g % NGRP], g // NGRP + 1)
                g = use[("mC", h)]
                wait_filled(dve, g)
                link(v.tensor_copy(nst[0:1, h], ps(g)[0:1, 1, 0:DK]))
                free(v.tensor_copy(Cst[:, h], ps(g)[:, 0, 0:DK]), g)
                dve.wait_ge(freed[g % NGRP], g // NGRP + 1)
                v.memset(sml[:, 10:11], 0.0).then_inc(for_pe, 1)
                settled(dve, for_pe)
            for s_ in range(STEPS):
                h, quarter = s_ // 4, s_ % 4
                c = ADA_EARLY + s_
                if s_ < 16:
                    scores(s_)
                if s_ >= 1:
                    select(ada, c - 2)
                if 1 <= s_ < 17:
                    weights(s_ - 1)
                if quarter == 0 and 1 <= h <= H:
                    head_end(h - 1)
                if s_ >= 2:
                    outputs(s_ - 2)
                if s_ < 16:
                    decayed(s_)
                    if quarter == 3:
                        state_keys(h)
                modulation_rows(ada, c)
                if s_ >= 1:
                    lo(ada.c0 + c + 1)
            lo(ada.c0 + ada.n + 1)
            v.memset(sml[:, 10:11], 0.0).then_inc(for_store, 1)
            settled(dve, for_store)
            v.memset(sml[:, 10:11], 0.0).then_inc(region_q, 1)
            settled(dve, region_q)
            v.memset(sml[:, 10:11], 0.0).then_inc(for_store, 1)
            settled(dve, for_store)
            select(ada, 22)
            select(ada, 23)
            for i, key in enumerate(("stokA", "stokB")):
                g = use[key]
                wait_filled(dve, g)
                free(v.tensor_copy(stok[0:NS, i * 1024:(i + 1) * 1024], ps(g)[0:NS].rearrange("p a b -> p (a b)")), g)
                dve.wait_ge(freed[g % NGRP], g // NGRP + 1)
                v.memset(sml[:, 10:11], 0.0).then_inc(for_store, 1)
                settled(dve, for_store)
            modulation_sums(1)
            dve.wait_ge(region_p, 1)
            dve.wait_ge(state_loaded, 16)
            dve.wait_ge(state_n_loaded, 16)
            for b in range(NS):
                g = use[("qb", b)]
                wait_filled(dve, g)
                dve.wait_ge(past_k[b % 2], 32 * (b // 2 + 1))
                link(v.tensor_tensor(prod[:], Kp[b % 2][:], ps(g)[:, 0:1, :].broadcast_to([P, NPG, 512]), ALU.mult))
                v.tensor_reduce(Sc[:, :, b * 8:(b + 1) * 8], prod[:].rearrange("p g (r d) -> p g r d", d=DK), AX.X,
                                ALU.add).then_inc(k_used, 1)
                settled(dve, k_used)
                dve.wait_ge(k_used, b + 1)
                link(v.tensor_tensor(prod[:, 0, 0:256], Cs[:, b], ps(g)[:, 1, 0:256], ALU.mult))
                link(v.tensor_reduce(CqS[:, b], prod[:, 0, 0:256].rearrange("p (h k) -> p h k", h=H), AX.X, ALU.add))
                free(v.tensor_copy(kbc[:, b], ps(g)[:, 1, 256:512]), g)
                dve.wait_ge(freed[g % NGRP], g // NGRP + 1)
            link(v.tensor_tensor(np8[0:NS, 256:512], stok[0:NS, 0:256], stok[0:NS, 512:768], ALU.mult))
            link(v.tensor_reduce(sm8[0:NS, 40:44], np8[0:NS, 256:512].rearrange("p (r d) -> p r d", d=DK), AX.X, ALU.add))
            link(v.tensor_tensor(np8[0:NS, 256:512], stok[0:NS, 256:512], stok[0:NS, 768:1024], ALU.mult))
            link(v.tensor_reduce(sm8[0:NS, 44:48], np8[0:NS, 256:512].rearrange("p (r d) -> p r d", d=DK), AX.X, ALU.add))
            sel8 = cn[0:NS, C_SEL:C_SEL + 1024].rearrange("p (b m) -> p b m", b=8)
            link(v.tensor_tensor(s8[0:NS, 0:64].rearrange("p (b r) -> p b r", b=8), sel8[:, :, 0:8],
                                 sm8[0:NS, 40:48].unsqueeze(1).broadcast_to([NS, 8, 8]), ALU.mult))
            v.scalar_tensor_tensor(Comb[0:64], cn[0:64, C_COMB + 32:C_COMB + 64], neglam[0:64, 0:1],
                                   cn[0:64, C_COMB:C_COMB + 32], ALU.mult, ALU.add).then_inc(for_pe, 1)
            settled(dve, for_pe)
            ig, lf = gst[0:NS, 0:4], gst[0:NS, 4:8]
            link(v.tensor_tensor(sm8[0:NS, 4:8], lf, mpv[0:NS], ALU.add))
            link(v.tensor_tensor(sm8[0:NS, 0:4], sm8[0:NS, 4:8], ig, ALU.max))
            link(v.tensor_tensor(sm8[0:NS, 16:20], ig, sm8[0:NS, 0:4], ALU.subtract))
            v.tensor_tensor(sm8[0:NS, 20:24], sm8[0:NS, 4:8], sm8[0:NS, 0:4], ALU.subtract).then_inc(dve_q, 1)
            settled(dve, dve_q)
            q_, k_ = stok[0:NS, 1536:1792], stok[0:NS, 1792:2048]
            link(v.tensor_tensor(np8[0:NS, 256:512], q_, k_, ALU.mult))
            link(v.tensor_reduce(sm8[0:NS, 28:32], np8[0:NS, 256:512].rearrange("p (h k) -> p h k", h=H), AX.X, ALU.add))
            link(v.tensor_tensor(np8[0:NS, 256:512], q_, np8[0:NS, 0:256], ALU.mult))
            link(v.tensor_reduce(sm8[0:NS, 32:36], np8[0:NS, 256:512].rearrange("p (h k) -> p h k", h=H), AX.X, ALU.add))
            dve.wait_ge(act_q, 9)
            w8, g8 = sm8[0:NS, 16:20], sm8[0:NS, 20:24]
            link(v.tensor_tensor(sm8[0:NS, 48:52], sm8[0:NS, 28:32], w8, ALU.mult))
            link(v.tensor_tensor(sm8[0:NS, 52:56], sm8[0:NS, 32:36], g8, ALU.mult))
            link(v.tensor_tensor(sm8[0:NS, 56:60], sm8[0:NS, 48:52], sm8[0:NS, 52:56], ALU.add))
            link(v.scalar_tensor_tensor(sm8[0:NS, 60:64], sm8[0:NS, 56:60], -1.0, sm8[0:NS, 24:28], ALU.mult, ALU.max))
            link(v.tensor_tensor(sm8[0:NS, 56:60], sm8[0:NS, 56:60], sm8[0:NS, 60:64], ALU.max))
            link(v.reciprocal(sm8[0:NS, 56:60], sm8[0:NS, 56:60]))
            pack = sm8[0:NS, 64:80]
            link(v.tensor_copy(pack[:, 0:4], g8))
            link(v.tensor_copy(pack[:, 4:8], w8))
            link(v.tensor_tensor(pack[:, 8:12], sm8[0:NS, 48:52], sm8[0:NS, 56:60], ALU.mult))
            link(v.tensor_tensor(pack[:, 12:16], g8, sm8[0:NS, 56:60], ALU.mult))
            bc = lambda x: x.unsqueeze(2).broadcast_to([NS, H, DK])
            hk = lambda x: x.rearrange("p (h k) -> p h k", h=H)
            link(v.tensor_tensor(hk(np8[0:NS, 256:512]), hk(np8[0:NS, 0:256]), bc(g8), ALU.mult))
            link(v.tensor_tensor(hk(np8[0:NS, 0:256]), hk(k_), bc(w8), ALU.mult))
            link(v.tensor_tensor(np8[0:NS, 256:512], np8[0:NS, 256:512], np8[0:NS, 0:256], ALU.add))
            v.memset(sml[:, 10:11], 0.0).then_inc(for_store, 1)
            settled(dve, for_store)
            v.memset(sml[:, 10:11], 0.0).then_inc(for_pe, 1)
            settled(dve, for_pe)
            g = use["st"]
            wait_filled(dve, g)
            link(v.tensor_copy(Pq[0:64, 256:257], ps(g)[0:64, 1, 0:1]))
            free(v.scalar_tensor_tensor(Pq[0:64, 0:256], cn[0:64, C_DROW:C_DROW + 256], cn[0:64, C_SLOPE:C_SLOPE + 1],
                                        ps(g)[0:64, 0, 0:256], ALU.mult, ALU.add), g)
            dve.wait_ge(freed[g % NGRP], g // NGRP + 1)
            dve.wait_ge(freed[g % NGRP], g // NGRP + 1)
            link(v.tensor_reduce(t32[0:64, 0, 2:3], Pq[0:64], AX.X, ALU.max))
            v.tensor_scalar(t32[0:64, 0, 0:1], t32[0:64, 0, 2:3], -1.0, None, ALU.mult).then_inc(dve_q, 1)
            settled(dve, dve_q)
            dve.wait_ge(act_q, 10)
            link(v.reciprocal(t32[0:64, 0, 3:4], t32[0:64, 0, 1:2]))
            v.tensor_scalar(Pq[0:64], Pq[0:64], t32[0:64, 0, 3:4], None, ALU.mult).then_inc(for_pe, 1)
            settled(dve, for_pe)
            g = use["wT"]
            wait_filled(dve, g)
            v.tensor_copy(wTs[:], ps(g)[:, 0, 0:96].rearrange("p (a b) -> p a b", a=3)).then_inc(for_pe, 1)
            settled(dve, for_pe)
            dve.wait_ge(for_pe, 11)
            free(v.tensor_copy(sml[0:1, 11:12], ps(g)[0:1, 0, 0:1]), g)
            dve.wait_ge(freed[g % NGRP], g // NGRP + 1)
            def hb_view(x):
                return x.rearrange("p (b h) -> p h b", h=H)
            vnew = smp[:, 8:12]
            link(v.tensor_tensor(t32[:, 0].rearrange("p (h b) -> p h b", h=H), vnew, hb_view(wTs[:, 2]), ALU.mult))
            g = use["pvs"]
            wait_filled(dve, g)
            link(v.tensor_tensor(t32[:, 1].rearrange("p (h b) -> p h b", h=H), hb_view(ps(g)[:, 0, 0:32]),
                                 t32[:, 0].rearrange("p (h b) -> p h b", h=H), ALU.add))
            free(v.tensor_copy(sml[0:1, 11:12], ps(g)[0:1, 0, 0:1]), g)
            dve.wait_ge(freed[g % NGRP], g // NGRP + 1)
            link(v.tensor_copy(proj[:, 0:4, :, HALF:HT], t32[:, 1].rearrange("p (h a b) -> p h a b", h=H, a=2)))
            g = use["pk"]
            wait_filled(dve, g)
            free(v.tensor_copy(pks[:], ps(g)[:, 0, 0:128].rearrange("p (b r) -> p b r", b=NS)), g)
            dve.wait_ge(freed[g % NGRP], g // NGRP + 1)
            dve.wait_ge(freed[g % NGRP], g // NGRP + 1)
            bv = smp[:, 16:20].rearrange("p h b -> p b h")
            tt = t32[:].rearrange("p a (b h) -> p a b h", h=H)
            link(v.tensor_tensor(tt[:, 0], bv, pks[:, :, 8:12], ALU.mult))
            link(v.tensor_tensor(tt[:, 1], CqS[:], pks[:, :, 12:16], ALU.mult))
            link(v.tensor_tensor(tt[:, 0], tt[:, 0], tt[:, 1], ALU.add))
            for hf in range(2):
                link(v.tensor_copy(proj[:, 16:20, hf, HALF:HT], tt[:, 0, hf * HS:(hf + 1) * HS].rearrange("p b h -> p h b")))
            v.memset(sml[:, 10:11], 0.0).then_inc(for_pe, 1)
            settled(dve, for_pe)
            link(v.tensor_tensor(tt[:, 0], bv, pks[:, :, 4:8], ALU.mult))
            C4 = Cs[:].rearrange("p b (h k) -> p (b h) k", h=H)
            K4 = kbc[:].rearrange("p b (h k) -> p (b h) k", h=H)
            bck = lambda x: x.unsqueeze(2).broadcast_to([P, 32, DK])
            link(v.tensor_tensor(K4, K4, bck(t32[:, 0]), ALU.mult))
            link(v.tensor_copy(t32[:, 1].rearrange("p (b h) -> p b h", h=H), pks[:, :, 0:4]))
            link(v.tensor_tensor(C4, C4, bck(t32[:, 1]), ALU.mult))
            link(v.tensor_tensor(C4, C4, K4, ALU.add))
            v.memset(sml[:, 10:11], 0.0).then_inc(for_store, 1)
            settled(dve, for_store)
            g = use["rms"]
            dve.wait_ge(freed[g % NGRP], g // NGRP + 1)
            v.reciprocal(rmb[1][0:8], rmb[0][0:8]).then_inc(rr_ready, 1)
            settled(dve, rr_ready)

            def low_mixed(t):
                dve.wait_ge(mix_hi, t + 1)
                v.tensor_tensor(ML[:, t], mxb[t % 2][:], MH[:, t].bitcast(F32), ALU.subtract).then_inc(mix_lo, 1)
                settled(dve, mix_lo)
            for t in range(8):
                g = use[("rb", t)]
                wait_filled(dve, g)
                src = proj[:, t] if t < 4 else proj[:, 12 + t]
                gain = gA[:, 0:1] if t < 4 else bT[:, 97 + t - 4:98 + t - 4]
                free(v.scalar_tensor_tensor(mxb[t % 2][:], src, gain, pT(g), ALU.mult, ALU.mult), g)
                dve.wait_ge(freed[g % NGRP], g // NGRP + 1)
                if t >= 4:
                    v.tensor_tensor(mxb[t % 2][:], mxb[t % 2][:], proj[:, 16 + t], ALU.mult).then_inc(mx_ready, 1)
                    settled(dve, mx_ready)
                if t >= 1:
                    low_mixed(t - 1)
            low_mixed(7)

        @block.vector
        def _(dve):
            link = chain(dve, dve_step)
            v = nc.vector

            def lo(c):
                if c >= n_chunks:
                    return
                s = chunk_stage[c]
                dve.wait_ge(hi_done, c + 1)
                if s.name == "gate":
                    src = raw[c % NRAW][:, 0:64].rearrange("p (k g m) -> p k g m", k=8, g=2)
                    vh = whi[c % 2][:, 0:1024].rearrange("p (k g m) -> p k g m", k=8, m=32)[:, :, 0:2, 0:4]
                    vl = wlo[c % 2][:, 0:1024].rearrange("p (k g m) -> p k g m", k=8, m=32)[:, :, 0:2, 0:4]
                    ins = v.tensor_tensor(vl, src, vh.bitcast(F32), ALU.subtract)
                else:
                    f = chunk_floats(c)
                    ins = v.tensor_tensor(wlo[c % 2][:, 0:f], raw[c % NRAW][:, 0:f], whi[c % 2][:, 0:f].bitcast(F32),
                                          ALU.subtract)
                ins.then_inc(lo_done, 1)
                settled(dve, lo_done)

            g = use["tc"]
            wait_filled(dve, g)
            dve.wait_ge(c_hi, 1)
            link(v.tensor_tensor(cH[:, :, 9:18], ps(g)[:, 0, 0:72].rearrange("p (k c) -> p k c", c=9),
                                 cH[:, :, 0:9].bitcast(F32), ALU.subtract))
            free(v.tensor_copy(sml[0:1, 0:1], ps(g)[0:1, 0, 0:1]), g)
            dve.wait_ge(freed[g % NGRP], g // NGRP + 1)
            dve.wait_ge(freed[g % NGRP], g // NGRP + 1)
            v.memset(sml[:, 1:2], 0.0).then_inc(c_lo, 1)
            settled(dve, c_lo)
            g = use["tb"]
            wait_filled(dve, g)
            link(v.tensor_copy(bT[:], ps(g)[:, 0, 0:101]))
            free(v.tensor_scalar(gA[:], ps(g)[:, 0, 96:97], 1.0 - LAM_INIT, None, ALU.mult), g)
            dve.wait_ge(freed[g % NGRP], g // NGRP + 1)
            lo(0)
            lo(1)
            dve.wait_ge(memset_done, 3)

            def setup_dve():
                for tb in range(4):
                    g = use[("tx", tb)]
                    wait_filled(dve, g)
                    off = (tb % 2) * P
                    free(v.tensor_copy(xT[:, :, tb // 2, off:off + P], ps(g)[:].rearrange("p a (b c) -> p (a b) c", c=P)), g)
                    dve.wait_ge(freed[g % NGRP], g // NGRP + 1)
                g = use["ra"]
                wait_filled(dve, g)
                rv = ps(g)[:, 0, 0:128].rearrange("p (k r) -> p k r", r=16)
                for hf in range(2):
                    v.tensor_copy(xT[:, :, hf, HALF:HT], rv[:, :, hf * HS:(hf + 1) * HS])
                link(v.tensor_copy(lnT[:], rv[:, :, 8:16]))
                free(v.tensor_scalar(lnA[:], rv[:, :, 8:16], ALPHA, None, ALU.mult), g)
                dve.wait_ge(freed[g % NGRP], g // NGRP + 1)
                g = use["to"]
                wait_filled(dve, g)
                free(v.tensor_copy(OT[:], ps(g)[:, 0, 0:400].rearrange("p (k r) -> p k r", r=40)), g)
                dve.wait_ge(freed[g % NGRP], g // NGRP + 1)
                dve.wait_ge(freed[g % NGRP], g // NGRP + 1)
                lam_ = OT[:, :, 39]
                link(v.tensor_scalar(sp8[:, 0], lam_, -1.0, None, ALU.mult))
                v.tensor_tensor(sp8[:, 1], sp8[:, 0], lam_, ALU.max).then_inc(dve_q, 1)
                settled(dve, dve_q)
                dve.wait_ge(dve_q, 1)
                link(v.tensor_scalar(sp8[:, 0], sp8[:, 0], 0.0, None, ALU.max))
                link(v.tensor_tensor(lamr[0:1, 0:64], lamr[0:1, 0:64], lamr[0:1, 64:128], ALU.mult))
                link(v.tensor_tensor(lamr[0:1, 64:128], lamr[0:1, 128:192], lamr[0:1, 192:256], ALU.mult))
                v.tensor_reduce(lamr[0:1, 256:258], lamr[0:1, 0:128].rearrange("p (a b) -> p a b", a=2), AX.X,
                                ALU.add).then_inc(dve_q, 1)
                settled(dve, dve_q)
                dve.wait_ge(act_q, 3)
                link(v.tensor_tensor(sp8[:, 0], sp8[:, 0], sp8[:, 1], ALU.add))
                v.tensor_scalar(sp8[:, 2], sp8[:, 0], 8.0, None, ALU.mult)
                link(v.tensor_scalar(sp8[:, 3], sp8[:, 0], -8.0, None, ALU.mult))
                link(v.tensor_tensor(lamr[0:1, 260:261], lamr[0:1, 259:260], lamr[0:1, 258:259], ALU.subtract))
                v.tensor_scalar(lamr[0:1, 261:262], lamr[0:1, 260:261], -LAM_INIT, None, ALU.add).then_inc(for_pe, 1)
                settled(dve, for_pe)
                g = use["lam"]
                wait_filled(dve, g)
                free(v.tensor_copy(neglam[:], ps(g)[:, 0, 0:1]), g)
                dve.wait_ge(freed[g % NGRP], g // NGRP + 1)

            def select(s, c):
                g = sel_use(s, c)
                l = int(s.name[3])
                wait_filled(dve, g)
                b = bT[:, l * 48 + 2 * c:l * 48 + 2 * c + 2].unsqueeze(2).broadcast_to([P, 2, 9])
                free(v.tensor_tensor(modT[l][:, 2 * c:2 * c + 2], ps(g)[:, 0, 0:18].rearrange("p (r c) -> p r c", c=9),
                                     b, ALU.add), g)
                dve.wait_ge(freed[g % NGRP], g // NGRP + 1)

            def modulation_rows(s, c):
                g = mod_use(s, c)
                wait_filled(dve, g)
                free(v.tensor_copy(modrow[0:18, c % 2], ps(g)[0:18, 0, 0:256]), g)
                dve.wait_ge(freed[g % NGRP], g // NGRP + 1)

            def modulation_sums(l):
                for j in range(2):
                    q = 2 * l + j
                    r = q - 1
                    sc, sh, gt = (modT[l][:, (3 * j + i) * 8:(3 * j + i + 1) * 8] for i in (1, 0, 2))
                    link(v.tensor_scalar(G9[:, q], sc, 1.0, None, ALU.add))
                    link(v.tensor_scalar(gt, gt, 1.0, None, ALU.add))
                    if r < 0:
                        link(v.tensor_copy(B9[:, q], sh))
                    else:
                        lb = lnT[:, :, 4 + r:5 + r].broadcast_to([P, KD, 9])
                        lg = lnT[:, :, r:r + 1].broadcast_to([P, KD, 9])
                        link(v.tensor_tensor(B9[:, q], G9[:, q], lb, ALU.mult))
                        link(v.tensor_tensor(B9[:, q], B9[:, q], sh, ALU.add))
                        link(v.tensor_tensor(G9[:, q], G9[:, q], lg, ALU.mult))
            for c in range(24):
                modulation_rows(st["ada0"], c)
                lo(c + 2)
                if c >= 1:
                    select(st["ada0"], c - 1)
            select(st["ada0"], 23)
            setup_dve()
            modulation_sums(0)

            def make_u(q):
                r = q - 1

                def low(t):
                    dve.wait_ge(uhi_ready, 8 * q + t + 1)
                    v.tensor_tensor(UL[:, t], ub[t % 2][:], UH[:, t].bitcast(F32), ALU.subtract).then_inc(ulo_ready, 1)
                    settled(dve, ulo_ready)
                for t in range(KD):
                    if r >= 0:
                        dve.wait_ge(d_ready, 8 * r + t + 1)
                        if t >= 2:
                            dve.wait_ge(x_ready, 8 * r + t - 1)
                        v.tensor_tensor(nb[t % 2][:], db[t % 2][:], rstd[:], ALU.mult).then_inc(n_ready, 1)
                        settled(dve, n_ready)
                        dve.wait_ge(n_ready, 8 * r + t + 1)
                        n = nb[t % 2]
                    else:
                        n = xT[:, t]
                    if q == 4:
                        continue
                    link(v.tensor_tensor(stmp[:], smpl(n), G9[:, q, t, 1:9].rearrange("p (a b) -> p a b", a=2), ALU.mult))
                    v.tensor_scalar(tok(ub[t % 2]), tok(n), G9[:, q, t, 0:1], B9[:, q, t, 0:1], ALU.mult, ALU.add)
                    v.tensor_tensor(smpl(ub[t % 2]), stmp[:], B9[:, q, t, 1:9].rearrange("p (a b) -> p a b", a=2),
                                    ALU.add).then_inc(u_ready, 1)
                    settled(dve, u_ready)
                    if t >= 1:
                        low(t - 1)
                if q < 4:
                    low(KD - 1)
                if r < 0:
                    link(v.tensor_scalar(xT[:], xT[:], ALPHA, None, ALU.mult))

            def residual(r, t, g, last):
                gt = modT[r // 2][:, (3 * (r % 2) + 2) * 8 + t]
                x = xT[:, t]
                wait_filled(dve, g)
                link(v.tensor_tensor(stmp[:], ps(g)[:, :, HALF:HT], gt[:, 1:9].rearrange("p (a b) -> p a b", a=2), ALU.mult))
                free(v.scalar_tensor_tensor(tok(x), ps(g)[:, :, 0:HALF], gt[:, 0:1], tok(x), ALU.mult, ALU.add), g)
                dve.wait_ge(freed[g % NGRP], g // NGRP + 1)
                ins = v.tensor_tensor(smpl(x), stmp[:], smpl(x), ALU.add)
                if last:
                    ins.then_inc(z_ready, 1)
                    settled(dve, z_ready)
                else:
                    link(ins)

            def ln_stats(r):
                g = use[("lnm", r)]
                wait_filled(dve, g)
                free(v.tensor_copy(mu[:], pT(g)), g)
                dve.wait_ge(freed[g % NGRP], g // NGRP + 1)
                dve.wait_ge(freed[g % NGRP], g // NGRP + 1)
                v.tensor_tensor(tv[:], mu[:], mu[:], ALU.mult).then_inc(mu_ready, 1)
                settled(dve, mu_ready)
                dve.wait_ge(mu_ready, r + 1)
                g = use[("lnq", r)]
                wait_filled(dve, g)
                free(v.tensor_tensor(tv[:], pT(g), tv[:], ALU.subtract), g)
                dve.wait_ge(freed[g % NGRP], g // NGRP + 1)
                dve.wait_ge(freed[g % NGRP], g // NGRP + 1)
                link(v.tensor_scalar(tv[:], tv[:], 0.0, EPS, ALU.max, ALU.add))
                v.memset(sml[:, 3:4], 0.0).then_inc(var_ready, 1)
                settled(dve, var_ready)
                dve.wait_ge(sd_ready, r + 1)
                link(v.reciprocal(rstd[:], tv[:]))

            def ffn(l):
                for hf in range(2):
                    s = st[f"fi{l}{hf}"]
                    for c in range(s.n):
                        k = (2 * l + hf) * KH + c
                        g = s.g0 + 2 * c + 1
                        wait_filled(dve, g)
                        dve.wait_ge(freed[(g - 1) % NGRP], (g - 1) // NGRP + 1)
                        v.tensor_tensor(hb[c % 2][:], pT(g), silb[c % 2][:], ALU.mult).then_inc(h_ready, 1)
                        settled(dve, h_ready)
                        dve.wait_ge(h_ready, k + 1)
                        free(v.tensor_copy(sml[0:1, 4:5], ps(g)[0:1, 0, 0:1]), g)
                        dve.wait_ge(freed[g % NGRP], g // NGRP + 1)
                        lo(s.c0 + c + 2)
                        dve.wait_ge(hhi_ready, k + 1)
                        v.tensor_tensor(HL[:, c], hb[c % 2][:], HH[:, c].bitcast(F32), ALU.subtract).then_inc(hlo_ready, 1)
                        settled(dve, hlo_ready)
                    s = st[f"fo{l}{hf}"]
                    for c in range(s.n):
                        residual(2 * l + 1, c, s.g0 + c, hf == 1)
                        lo(s.c0 + c + 2)
                ln_stats(2 * l + 1)

            make_u(0)
            s = st["ein"]
            for c in range(s.n):
                for m in range(2):
                    t, g = 2 * c + m, s.g0 + 2 * c + m
                    wait_filled(dve, g)
                    scale = 0.125 if t < 4 or 12 <= t < 14 else 1.0
                    free(v.tensor_scalar(proj[:, t], pT(g), scale, None, ALU.mult), g)
                    dve.wait_ge(freed[g % NGRP], g // NGRP + 1)
                dve.wait_ge(freed[g % NGRP], g // NGRP + 1)
                v.memset(sml[:, 5:6], 0.0).then_inc(evac, 2)
                settled(dve, evac, 2)
                lo(s.c0 + c + 2)
            lo(st["gate"].c0 + 2)
            middle_dve(dve, link, lo, modulation_rows, select, modulation_sums)
            s = st["eout"]
            for c in range(s.n):
                for m in range(2):
                    residual(0, 2 * c + m, s.g0 + 2 * c + m, True)
                lo(s.c0 + c + 2)
            ln_stats(0)
            make_u(1)
            ffn(0)
            make_u(2)
            s = st["oin"]
            dve.wait_ge(zero_ready, 1)
            for c in range(s.n):
                for m in range(2):
                    t = 2 * c + m - KR
                    g = s.g0 + 2 * c + m
                    if t < 0:
                        continue
                    wait_filled(dve, g)
                    link(v.tensor_copy(xrS[:, t].rearrange("p (a b) -> p a b", a=2), ps(g)[:, :, HALF:HT]))
                    free(v.tensor_copy(xr[:, t, 3:3 + SEQ].rearrange("p (a b) -> p a b", a=2), ps(g)[:, :, 0:HALF]), g)
                    dve.wait_ge(freed[g % NGRP], g // NGRP + 1)
                    dve.wait_ge(freed[g % NGRP], g // NGRP + 1)
                    v.tensor_copy(OS[:, t, 0:3], xr[:, t, SEQ:SEQ + 3]).then_inc(xr_ready, 1)
                    settled(dve, xr_ready)
                    dve.wait_ge(cv0, t + 1)
                    for j in range(1, 4):
                        link(v.scalar_tensor_tensor(tok(xc[:, t]), xr[:, t, j:j + SEQ].rearrange("p (a b) -> p a b", a=2),
                                                    OT[:, t, 32 + j:33 + j], tok(xc[:, t]), ALU.mult, ALU.add))
                if c < s.n - 0:
                    lo(s.c0 + c + 2)

            def per_tile(col, n=NS):
                return OT[:, :, col:col + 1].broadcast_to([P, KR, n])
            link(v.tensor_tensor(tS[:, 0], xrS[:], per_tile(35), ALU.mult))
            link(v.tensor_tensor(tS[:, 0], tS[:, 0], per_tile(36), ALU.add))
            for j in range(3):
                link(v.tensor_tensor(tS[:, 1], OT[:, :, j:24:3], per_tile(32 + j), ALU.mult))
                link(v.tensor_tensor(tS[:, 0], tS[:, 0], tS[:, 1], ALU.add))
            link(v.tensor_copy(OS[:, :, 3:11], xrS[:]))
            v.tensor_copy(xc[:, :, :, HALF:HT], tS[:, 0].rearrange("p k (a b) -> p k a b", a=2)).then_inc(cv_ready, 1)
            settled(dve, cv_ready)
            for t in range(KR):
                dve.wait_ge(xch, t + 1)
                v.tensor_tensor(XL[:, t], xc[:, t], XH[:, t].bitcast(F32), ALU.subtract).then_inc(xcl, 1)
                settled(dve, xcl)
            v.memset(sml[:, 6:7], 0.0).then_inc(for_store, 1)
            settled(dve, for_store)
            for w in ("wa", "wx"):
                s = st[w]
                for c in range(2):
                    if w == "wx":
                        for b in range(5):
                            g = s.g0 + 5 * c + b
                            t, k = 2 * b + c, 5 * c + b
                            dve.wait_ge(freed[g % NGRP], g // NGRP + 1)
                            v.tensor_tensor(xc[:, t], xc[:, t], isb[k % 2][:], ALU.mult).then_inc(ix_ready, 1)
                            settled(dve, ix_ready)
                    lo(s.c0 + c + 2)
            dve.wait_ge(ix_ready, KR)
            for t in range(KR):
                dve.wait_ge(a_ready, t + 1)
                v.scalar_tensor_tensor(qT[:, t], isb[t % 2][:], 1.0, qT[:, t], ALU.add, ALU.mult).then_inc(q_ready, 1)
                settled(dve, q_ready)
            for t in range(KR):
                dve.wait_ge(sqrt_ready, t + 1)
                link(v.tensor_tensor(qT[:, t], qT[:, t], xc[:, t], ALU.mult))
                link(v.tensor_tensor(stmp[:], smpl(aT[:, t]), OT[:, t, 24:32].rearrange("p (a b) -> p a b", a=2), ALU.mult))
                link(v.tensor_tensor_scan(rT[:, t, 0, 0:HALF], aT[:, t, 0, 0:HALF], qT[:, t, 0, 0:HALF], 0.0, ALU.mult, ALU.add))
                link(v.tensor_tensor_scan(rT[:, t, 1, 0:HALF], aT[:, t, 1, 0:HALF], qT[:, t, 1, 0:HALF],
                                          rT[:, t, 0, HALF - 1:HALF], ALU.mult, ALU.add))
                link(v.tensor_tensor(smpl(rT[:, t]), stmp[:], smpl(qT[:, t]), ALU.add))
                link(v.tensor_copy(OS[:, t, 11:12], rT[:, t, 1, HALF - 1:HALF]))
                link(v.tensor_copy(OS[:, t, 12:20].rearrange("p (a b) -> p a b", a=2), smpl(rT[:, t])))
                v.tensor_tensor(ysb[t % 2][:], rT[:, t], gT[:, t], ALU.mult).then_inc(y_ready, 1)
                settled(dve, y_ready)
                if t >= 1:
                    dve.wait_ge(yhi_ready, t)
                    v.tensor_tensor(YL[:, t - 1], ysb[(t - 1) % 2][:], YH[:, t - 1].bitcast(F32), ALU.subtract).then_inc(ylo_ready, 1)
                    settled(dve, ylo_ready)
            dve.wait_ge(yhi_ready, KR)
            v.tensor_tensor(YL[:, KR - 1], ysb[(KR - 1) % 2][:], YH[:, KR - 1].bitcast(F32), ALU.subtract).then_inc(ylo_ready, 1)
            settled(dve, ylo_ready)
            for i, key in enumerate(("osA", "osB")):
                g = use[key]
                wait_filled(dve, g)
                n = 1024 if i == 0 else 256
                ins = v.tensor_copy(OST[0:20, i * 1024:i * 1024 + n], ps(g)[0:20].rearrange("p a b -> p (a b)")[:, 0:n])
                free(ins, g)
                dve.wait_ge(freed[g % NGRP], g // NGRP + 1)
                dve.wait_ge(freed[g % NGRP], g // NGRP + 1)
                v.memset(sml[:, 7:8], 0.0).then_inc(out_ready, 1)
                settled(dve, out_ready)
            s = st["oout"]
            for c in range(s.n):
                residual(2, c, s.g0 + c, True)
                lo(s.c0 + c + 2)
            ln_stats(2)
            make_u(3)
            ffn(1)
            make_u(4)
            dve.wait_ge(x_ready, 32)
            v.tensor_copy(xsm[:].rearrange("p k (a b) -> p k a b", a=2), xT[:, :, :, HALF:HT]).then_inc(for_pe, 1)
            settled(dve, for_pe)
            for tb in range(4):
                g = use[("ty", tb)]
                wait_filled(dve, g)
                free(v.tensor_copy(ytok[tb][:], ps(g)[:].rearrange("p a b -> p (a b)")), g)
                dve.wait_ge(freed[g % NGRP], g // NGRP + 1)
                dve.wait_ge(freed[g % NGRP], g // NGRP + 1)
                v.memset(sml[:, 7:8], 0.0).then_inc(out_ready, 1)
                settled(dve, out_ready)
            g = use["tys"]
            wait_filled(dve, g)
            v.tensor_copy(ysamp[0:NS], ps(g)[0:NS].rearrange("p a b -> p (a b)")).then_inc(out_ready, 1)
            settled(dve, out_ready)

        def middle_pe(pe, begin, done, mod_products, mod_select):
            T = nc.tensor

            def blk(t, tb, lo_=0, hi_=P):
                return proj[lo_:hi_, t, tb // 2, (tb % 2) * P:(tb % 2 + 1) * P]
            pe.wait_ge(evac, 24)
            ada = st["ada1"]
            for tb in range(4):
                g = use[("kv", tb)]
                begin(g)
                for i in range(8):
                    ins = T.transpose(ps(g)[:, i // 4, (i % 4) * P:(i % 4 + 1) * P], blk(4 + i, tb), ident)
                done(ins)
                mod_products(ada, tb)
                if tb >= 1:
                    mod_select(ada, tb - 1)
            for tb in range(4):
                g = use[("bkv", tb)]
                begin(g)
                for i in range(4):
                    T.transpose(ps(g)[:, 0, i * P:(i + 1) * P], blk(16 + i, tb), ident)
                for i in range(2):
                    ins = T.transpose(ps(g)[:, 1, i * P:(i + 1) * P], blk(14 + i, tb), ident)
                done(ins)
                if tb < ADA_EARLY - 4:
                    mod_products(ada, 4 + tb)
                    mod_select(ada, 3 + tb)
            pe.wait_ge(for_pe, 3)
            g = use["acol"]
            begin(g)
            for tb in range(4):
                ins = T.transpose(ps(g)[:, 0, 4 * tb:4 * tb + 4], rows[0:4, 4, tb // 2, (tb % 2) * P:(tb % 2 + 1) * P], ident[0:4, 0:4])
            done(ins)
            g = use["gs"]
            begin(g)
            T.transpose(ps(g)[0:NS, 0, 0:4], rows[0:4, 5, 0, 0:8], ident[0:4, 0:4])
            done(T.transpose(ps(g)[0:NS, 0, 4:8], rows[0:4, 5, 0, 8:16], ident[0:4, 0:4]))

            def head_rows(h):
                g = use[("bc", h)]
                begin(g)
                sel = cn[0:4, C_SEL + h * P:C_SEL + (h + 1) * P]
                for j in range(2):
                    ins = T.matmul(ps(g)[:, j], sel, rowc[0:4, j], start=True, stop=True)
                done(ins)

            def head_scores(h, s_):
                p0 = 64 * (h % 2)
                g = use[("mS", h, s_)]
                begin(g)
                kT = blk(14 + h // 2, s_, p0, p0 + 64)
                n = 0
                for tb in range(s_, 4):
                    ins = T.matmul(ps(g)[:, 0, n:n + P], kT, blk(12 + h // 2, tb, p0, p0 + 64), start=True, stop=True)
                    n += P
                done(ins)

            def head_sums(h):
                g = use[("mN", h)]
                begin(g)
                for s_ in range(4):
                    gs = use[("mS", h, s_)]
                    pe.wait_ge(freed[gs % NGRP], gs // NGRP + 1)
                for s_ in range(4):
                    n = SEQ - s_ * P
                    T.matmul(ps(g)[:, 0, s_ * P:SEQ], bkv[:, s_, h * DV:(h + 1) * DV], PT[s_][:, 0:n], start=(s_ == 0),
                             stop=(s_ == 3), skip_group_check=True)
                for s_ in range(4):
                    n = SEQ - s_ * P
                    ins = T.matmul(ps(g)[:, 1, s_ * P:SEQ], ones[:], PT[s_][:, 0:n], start=(s_ == 0), stop=(s_ == 3),
                                   skip_group_check=True)
                done(ins)
                g = use[("mC", h)]
                begin(g)
                pe.wait_ge(pt_ready, h + 1)
                for s_ in range(4):
                    T.matmul(ps(g)[:, 0, 0:DK], bkv[:, s_, h * DV:(h + 1) * DV], kw[:, s_], start=(s_ == 0), stop=(s_ == 3))
                for s_ in range(4):
                    ins = T.matmul(ps(g)[0:1, 1, 0:DK], wl[:, s_:s_ + 1], bkv[:, s_, 512 + h * DK:512 + (h + 1) * DK],
                                   start=(s_ == 0), stop=(s_ == 3))
                done(ins)

            def scores(u):
                h, i = u // 4, u % 4
                g = use[("S", u)]
                begin(g)
                for j in range(2):
                    q = blk(h, i, 64 * j, 64 * j + 64)
                    for hf in range(i // 2 + 1):
                        n = HALF if hf < i // 2 or i % 2 else P
                        ins = T.matmul(ps(g)[:, j, hf * HALF:hf * HALF + n], q, proj[64 * j:64 * j + 64, 4 + h, hf, 0:n],
                                       start=True, stop=True)
                done(ins)

            def transposes(u):
                g = use[("T", u)]
                begin(g)
                pe.wait_ge(w_ready, u + 1)
                for kb in range(u % 4 + 1):
                    ins = T.transpose(ps(g)[:, 0, kb * P:(kb + 1) * P], Wb[u % 2][:, kb * P:(kb + 1) * P], ident)
                done(ins)

            def pv(u):
                h, i = u // 4, u % 4
                g = use[("PV", u)]
                begin(g)
                gt = use[("T", u)]
                pe.wait_ge(freed[gt % NGRP], gt // NGRP + 1)
                for kb in range(i + 1):
                    ins = T.matmul(ps(g)[:, 0, 0:P], vtok[:, kb, h * DV:(h + 1) * DV], wTb[u % 2][:, kb * P:(kb + 1) * P],
                                   start=(kb == 0), stop=(kb == i))
                done(ins)
            scores(0)
            for s_ in range(STEPS):
                h, quarter = s_ // 4, s_ % 4
                if quarter == 0 and 1 <= h <= H:
                    head_sums(h - 1)
                if s_ < 16:
                    if quarter == 0:
                        head_rows(h)
                    head_scores(h, quarter)
                if s_ >= 2:
                    pv(s_ - 2)
                mod_products(ada, ADA_EARLY + s_)
                if s_ < 15:
                    scores(s_ + 1)
                if 1 <= s_ < 17:
                    transposes(s_ - 1)
                mod_select(ada, ADA_EARLY + s_ - 1)
            mod_select(ada, 23)
            pe.wait_ge(for_store, 3)
            for key, tiles in (("stokA", list(range(8))), ("stokB", [8, 9, 10, 11, 12, 13, 14, 15])):
                g = use[key]
                begin(g)
                for i, t in enumerate(tiles):
                    ins = T.transpose(ps(g)[0:NS, i // 4, (i % 4) * P:(i % 4 + 1) * P], smp[:, t], ident)
                done(ins)
            pe.wait_ge(for_store, 5)
            for b in range(NS):
                g = use[("qb", b)]
                begin(g)
                sel = cn[0:NS, C_SEL + b * P:C_SEL + (b + 1) * P]
                T.matmul(ps(g)[:, 0], sel, stok[0:NS, 0:512], start=True, stop=True)
                done(T.matmul(ps(g)[:, 1], sel, stok[0:NS, 1536:2048], start=True, stop=True))
            g = use["st"]
            begin(g)
            pe.wait_ge(for_pe, 8)
            for pg in range(NPG):
                T.transpose(ps(g)[0:64, 0, pg * P:(pg + 1) * P], Sc[:, pg], ident)
            done(T.matmul(ps(g)[0:64, 1, 0:1], s8[0:NS, 0:64], ones[0:NS, 0:1], start=True, stop=True))
            g = use["wT"]
            begin(g)
            pe.wait_ge(for_pe, 10)
            for pg in range(NPG):
                T.matmul(ps(g)[:, 0, pg * 32:(pg + 1) * 32], Pq[0:64, pg * P:(pg + 1) * P], Comb[0:64], start=True, stop=True)
            done(T.matmul(ps(g)[:, 0, 64:96], Pq[0:64, 256:257].broadcast_to([64, P]), Comb[0:64], start=True, stop=True))
            g = use["pvs"]
            begin(g)
            pe.wait_ge(for_pe, 11)
            for b in range(NS):
                pe.wait_ge(past_v[b % 3], 32 * (b // 3 + 1))
                for h in range(H):
                    for pg in range(NPG):
                        col = 4 * b + h
                        ins = T.matmul(ps(g)[:, 0, col:col + 1], Vp[b % 3][:, pg, h * DV:(h + 1) * DV], wTs[:, pg, col:col + 1],
                                       start=(pg == 0), stop=(pg == NPG - 1))
                if b < NS - 1:
                    ins.then_inc(v_used, 1)
            done(ins)
            g = use["pk"]
            begin(g)
            pe.wait_ge(for_pe, 9)
            for b in range(NS):
                ins = T.matmul(ps(g)[:, 0, 16 * b:16 * b + 16], cn[0:NS, C_SEL + b * P:C_SEL + (b + 1) * P], sm8[0:NS, 64:80],
                               start=True, stop=True)
            done(ins)
            g = use["rms"]
            begin(g)
            for t in range(8):
                pe.wait_ge(rm_sq, t + 1)
                for hf in range(2):
                    ins = T.matmul(ps(g)[0:8, hf, 0:HT], cn[:, C_SELV + 8 * t:C_SELV + 8 * t + 8], rsq[t % 2][:, hf],
                                   start=(t == 0), stop=(t == 7))
                if t < 7:
                    ins.then_inc(rsq_used, 1)
            done(ins)
            pe.wait_ge(rr_ready, 1)
            for t in range(8):
                g = use[("rb", t)]
                begin(g)
                for hf in range(2):
                    ins = T.matmul(ps(g)[:, hf, 0:HT], cn[0:8, C_SEL + t * P:C_SEL + (t + 1) * P], rmb[1][0:8, hf],
                                   start=True, stop=True)
                done(ins)

        @block.tensor
        def _(pe):
            T = nc.tensor

            def begin(g, it=None, per=0):
                if g >= NGRP:
                    pe.wait_ge(freed[g % NGRP], g // NGRP if it is None else g // NGRP + it * per)

            def done(ins):
                ins.then_inc(filled, 1)

            def products(s, c, xh, xl, it=None):
                gc = s.c0 + c
                pe.wait_ge(lo_done, gc + 1 if it is None else gc + 1 + it * NRAW)
                wh = whi[gc % 2][:, 0:s.k * s.m].rearrange("p (k m) -> p k m", m=s.m)
                wl_ = wlo[gc % 2][:, 0:s.k * s.m].rearrange("p (k m) -> p k m", m=s.m)
                for m in range(s.uses):
                    g = s.g0 + c * s.uses + m
                    begin(g, it, s.uses * NRAW // NGRP)
                    for k in range(s.k):
                        wc = slice(m * P, (m + 1) * P)
                        for w, x in ((wh, xh), (wh, xl), (wl_, xh)):
                            for hf in range(2):
                                ins = T.matmul(ps(g)[:, hf, 0:HT], w[:, k, wc], x[:, k, hf], start=(k == 0 and w is wh and x is xh),
                                               stop=(k == s.k - 1 and w is wl_))
                    done(ins)

            def gemm(name, xh, xl, ready, n_ready):
                s = st[name]
                first = [(c, m) for c in range(2) for m in range(s.uses)]
                for c, m in first:
                    begin(s.g0 + c * s.uses + m)
                pe.wait_ge(lo_done, s.c0 + 2)
                for k in range(s.k):
                    pe.wait_ge(ready, n_ready + k + 1)
                    for c, m in first:
                        g = s.g0 + c * s.uses + m
                        slot = (s.c0 + c) % 2
                        wc = slice(k * s.m + m * P, k * s.m + (m + 1) * P)
                        for w, x in ((whi, xh), (whi, xl), (wlo, xh)):
                            for hf in range(2):
                                ins = T.matmul(ps(g)[:, hf, 0:HT], w[slot][:, wc], x[:, k, hf],
                                               start=(k == 0 and w is whi and x is xh), stop=(k == s.k - 1 and w is wlo))
                        if k == s.k - 1:
                            done(ins)
                bodies = (s.n - 2) // NRAW
                c0 = 2
                if bodies > 1:
                    with pe.Fori(0, bodies) as it:
                        for c in range(c0, c0 + NRAW):
                            products(s, c, xh, xl, it)
                    c0 += bodies * NRAW
                for c in range(c0, s.n):
                    products(s, c, xh, xl)

            pe.wait_ge(consts_loaded, 16)
            pe.wait_ge(memset_done, 3)

            def rows_to_cols(g, src, n, cols, off=0):
                for k in range(cols):
                    ins = T.transpose(ps(g)[:, 0, off + k * n:off + (k + 1) * n], src[0:n, k * P:(k + 1) * P], ident[0:n, 0:n])
                return ins
            pe.wait_ge(silu_c, 1)
            begin(use["tc"])
            done(rows_to_cols(use["tc"], CR, 9, KD))
            begin(use["tb"])
            rows_to_cols(use["tb"], BR, 96, 1)
            done(rows_to_cols(use["tb"], NR, 5, 1, 96))

            def setup_pe():
                pe.wait_ge(x_loaded, 16)
                for tb in range(4):
                    g = use[("tx", tb)]
                    begin(g)
                    for k in range(KD):
                        ins = T.transpose(ps(g)[:].rearrange("p a (b c) -> p (a b) c", c=P)[:, k],
                                          xtok[:, tb, k * P:(k + 1) * P], ident)
                    done(ins)
                pe.wait_ge(small_loaded, 16 * N_SMALL)
                begin(use["ra"])
                done(rows_to_cols(use["ra"], RA, 16, KD))
                begin(use["to"])
                done(rows_to_cols(use["to"], RO, 40, KR))
                begin(use["lam"])
                pe.wait_ge(for_pe, 1)
                done(T.matmul(ps(use["lam"])[:, 0, 0:1], ones[0:1, :], lamr[0:1, 261:262], start=True, stop=True))

            def mod_products(s, c, it=None):
                gc = s.c0 + c
                pe.wait_ge(lo_done, gc + 1 if it is None else gc + 1 + it * NRAW)
                g = mod_use(s, c)
                begin(g, it, 2)
                for k in range(KD):
                    for w in (whi, wlo):
                        ins = T.matmul(ps(g)[0:18, 0, 0:256], cH[:, k], w[gc % 2][:, k * 256:(k + 1) * 256],
                                       start=(k == 0 and w is whi), stop=(k == KD - 1 and w is wlo))
                done(ins)

            def mod_select(s, c, it=None):
                g = sel_use(s, c)
                begin(g, it, 2)
                gm = mod_use(s, c)
                pe.wait_ge(freed[gm % NGRP], gm // NGRP + 1 if it is None else gm // NGRP + 1 + it * 2)
                for k in range(2):
                    ins = T.matmul(ps(g)[:, 0, k * 9:(k + 1) * 9], modrow[0:18, c % 2, k * P:(k + 1) * P],
                                   cn[0:18, C_ADA:C_ADA + 9], start=True, stop=True)
                done(ins)
            pe.wait_ge(c_lo, 1)
            s = st["ada0"]
            for c in range(NRAW):
                mod_products(s, c)
                if c >= 1:
                    mod_select(s, c - 1)
            with pe.Fori(0, s.n // NRAW - 1) as it:
                for c in range(NRAW, 2 * NRAW):
                    mod_products(s, c, it)
                    mod_select(s, c - 1, it)
            mod_select(s, s.n - 1)
            setup_pe()

            gemm("ein", UH, UL, ulo_ready, 0)
            products(st["gate"], 0, UH, UL)
            middle_pe(pe, begin, done, mod_products, mod_select)
            gemm("eout", MH, ML, mix_lo, 0)

            def ln_sums(r):
                pe.wait_ge(acc_step, 16 * r + 16)
                for key, acc in (("lnm", accS), ("lnq", accQ)):
                    g = use[(key, r)]
                    begin(g)
                    for hf in range(2):
                        ins = T.matmul(ps(g)[:, hf, 0:HT], onesD[:], acc[:, hf], start=True, stop=True)
                    done(ins)

            def ffn(l):
                for hf in range(2):
                    gemm(f"fi{l}{hf}", UH, UL, ulo_ready, 8 * (2 * l + 1))
                    gemm(f"fo{l}{hf}", HH, HL, hlo_ready, (2 * l + hf) * KH)
                ln_sums(2 * l + 1)
            ln_sums(0)
            ffn(0)
            gemm("oin", UH, UL, ulo_ready, 16)
            pe.wait_ge(xcl, KR)
            for w in ("wa", "wx"):
                s = st[w]
                for c in range(2):
                    gc = s.c0 + c
                    pe.wait_ge(lo_done, gc + 1)
                    for b in range(5):
                        g = s.g0 + 5 * c + b
                        begin(g)
                        for k in range(2):
                            wc = slice((2 * b + k) * P, (2 * b + k + 1) * P)
                            for wt, x in ((whi, XH), (whi, XL), (wlo, XH)):
                                for hf in range(2):
                                    ins = T.matmul(ps(g)[:, hf, 0:HT], wt[gc % 2][:, wc], x[:, 2 * b + k, hf],
                                                   start=(k == 0 and wt is whi and x is XH), stop=(k == 1 and wt is wlo))
                        done(ins)
            pe.wait_ge(ylo_ready, KR)
            for i, key in enumerate(("osA", "osB")):
                g = use[key]
                begin(g)
                for k in range(8 if i == 0 else 2):
                    ins = T.transpose(ps(g)[0:20].rearrange("p a (b c) -> p (a b) c", c=P)[:, k], OS[:, 8 * i + k], ident)
                done(ins)
            gemm("oout", YH, YL, ylo_ready, 0)
            ln_sums(2)
            ffn(1)
            pe.wait_ge(x_ready, 32)
            for tb in range(4):
                g = use[("ty", tb)]
                begin(g)
                off = (tb % 2) * P
                for k in range(KD):
                    ins = T.transpose(ps(g)[:].rearrange("p a (b c) -> p (a b) c", c=P)[:, k], xT[:, k, tb // 2, off:off + P], ident)
                done(ins)
            g = use["tys"]
            begin(g)
            pe.wait_ge(for_pe, 13)
            for k in range(KD):
                ins = T.transpose(ps(g)[0:NS].rearrange("p a (b c) -> p (a b) c", c=P)[:, k], xsm[:, k], ident)
            done(ins)


_OUTS = [
    ("y_prompt", (1, 512, 1024)), ("y_sample", (8, 1, 1024)), ("k_prompt", (1, 1, 4, 128, 4, 2, 64)),
    ("v_prompt", (1, 1, 4, 128, 4, 128)), ("k_sample", (1, 8, 1, 4, 2, 64)), ("v_sample", (1, 8, 1, 4, 128)),
    ("C_prompt", (1, 1, 4, 128, 64)), ("n_prompt", (1, 1, 4, 64)), ("m_prompt", (1, 1, 4)),
    ("C_sample", (1, 8, 4, 128, 64)), ("n_sample", (1, 8, 4, 64)), ("m_sample", (1, 8, 4)),
    ("h_prompt", (1, 1, 1280)), ("conv_prompt", (1, 1, 3, 1280)), ("h_sample", (1, 8, 1280)),
    ("conv_sample", (1, 8, 3, 1280)),
]


def kernel(**inputs):
    import concourse.bacc as _bacc
    from concourse.bass_utils import run_bass_kernel_spmd as _run

    nc = _bacc.Bacc("TRN2", target_bir_lowering=False, num_devices=1)
    arrays, ins = {}, {}
    for name, value in list(inputs.items()) + [("consts", constants())]:
        arr = np.ascontiguousarray(value)
        arrays[f"in_{name}"] = arr
        ins[name] = nc.dram_tensor(f"in_{name}", arr.shape, mybir.dt.from_np(arr.dtype), kind="ExternalInput").ap()
    outs = {n: nc.dram_tensor(f"out_{n}", shape, F32, kind="ExternalOutput").ap() for n, shape in _OUTS}
    trunk(nc, ins, outs)
    r = _run(nc, [arrays], core_ids=[0])
    return tuple(r.results[0][f"out_{n}"] for n, _ in _OUTS)
```

```python
from contextlib import ExitStack
import math

import numpy as np
import concourse.bass as bass
from concourse import mybir

F32 = mybir.dt.float32
F32R = mybir.dt.float32r
I32 = mybir.dt.int32
ACT = mybir.ActivationFunctionType
ALU = mybir.AluOpType
AX = mybir.AxisListType

P = 128
D = 1024
KD = D // P
SEQ = 512
NS = 8
HALF = 256
HS = NS // 2
HT = HALF + HS
H = 4
DK = 64
DV = 128
DR = 1280
KR = DR // P
DFF = 2816
KF = DFF // P
KH = KF // 2
PAGE = 128
NPG = 2
NPOOL = 20
E_COLS = 3072
ALPHA = 4.0 ** 0.25
LAM_INIT = 0.2
BIG = 1e30
EPS = 1e-5
NRAW, NSPLIT, NGRP = 4, 2, 4
SLOT = 2048
STEPS, ADA_EARLY = 18, 6

C_ID, C_MASK, C_DIST, C_SEL, C_COMB, C_SLOPE, C_DROW, C_ADA = 0, 128, 640, 1152, 2176, 2240, 2241, 2498
C_SELV = 2507
C_END = 2571


def constants():
    c = np.zeros((P, C_END), np.float32)
    i = np.arange(P)
    c[:, C_ID:C_ID + P] = np.eye(P)
    c[:, C_MASK:C_MASK + P] = np.where(i[:, None] > i[None, :], BIG, 0.0)
    d = i[:, None] - np.arange(512)[None, :] + 384
    c[:, C_DIST:C_DIST + 512] = np.where(d >= 0, d, BIG)
    for b in range(8):
        c[b, C_SEL + b * P:C_SEL + (b + 1) * P] = 1.0
    for r in range(64):
        b, h, j = r // 8, (r // 2) % 4, r % 2
        c[r, C_COMB + (0 if j == 0 else 32) + b * 4 + h] = 1.0
        c[r, C_SLOPE] = -(2.0 ** (-2.0 * (h + 1)))
    c[:, C_DROW:C_DROW + 256] = (256 - np.arange(256))[None, :]
    for r in range(9):
        c[r, C_ADA + r] = 1.0
        c[r + 9, C_ADA + r] = 1.0
    for t in range(8):
        c[:, C_SELV + 8 * t + t] = 1.0 / DV
    return c


class Stage:

    def __init__(self, name, n, k, m, uses):
        self.name, self.n, self.k, self.m, self.uses = name, n, k, m, uses


def plan():
    st, use, order = {}, {}, []

    def one(*keys):
        for key in keys:
            use[key] = one.g
            one.g += 1
    one.g = 0

    def stage(name, n, k, m, uses):
        s = Stage(name, n, k, m, uses)
        s.c0, s.g0 = stage.c, one.g
        stage.c += n
        one.g += n * uses
        st[name] = s
        order.append(s)
    stage.c = 0

    one("tc", "tb")
    stage("ada0", 24, 8, 256, 2)
    one(*[("tx", i) for i in range(4)], "ra", "to")
    stage("ein", 12, 8, 256, 2)
    stage("gate", 1, 8, 128, 1)
    one("lam")
    stage("ada1", 24, 8, 256, 0)

    def mod(c):
        one(("mod", c))
        if c >= 1:
            one(("sel", c - 1))
    for i in range(4):
        one(("kv", i))
        mod(i)
    for i in range(4):
        one(("bkv", i))
        if i < ADA_EARLY - 4:
            mod(4 + i)
    one("acol", "gs", ("S", 0))
    for s in range(STEPS):
        h, quarter = s // 4, s % 4
        if quarter == 0 and 1 <= h <= H:
            one(("mN", h - 1), ("mC", h - 1))
        if s < 16:
            if quarter == 0:
                one(("bc", h))
            one(("mS", h, quarter))
        if s >= 2:
            one(("PV", s - 2))
        one(("mod", ADA_EARLY + s))
        if s < 15:
            one(("S", s + 1))
        if 1 <= s < 17:
            one(("T", s - 1))
        one(("sel", ADA_EARLY + s - 1))
    one(("sel", 23), "stokA", "stokB")
    for b in range(NS):
        one(("qb", b))
    one("rms", "st", "wT", "pvs", "pk", "rmsS")
    for t in range(8):
        one(("rb", t))
    stage("eout", 4, 8, 256, 2)
    one(("lnm", 0), ("lnq", 0))

    def ffn(l):
        for hf in range(2):
            stage(f"fi{l}{hf}", 11, 8, 256, 2)
            stage(f"fo{l}{hf}", 8, 11, 128, 1)
        one(("lnm", 2 * l + 1), ("lnq", 2 * l + 1))
    ffn(0)
    stage("oinx", 5, 8, 256, 2)
    stage("wax", 5, 4, 256, 4)
    stage("oing", 5, 8, 256, 2)
    one("osA", "osB")
    stage("oout", 8, 10, 128, 1)
    one(("lnm", 2), ("lnq", 2))
    ffn(1)
    one(*[("ty", i) for i in range(4)], "tys")
    return st, use, order


def trunk(nc, a, o):
    st, use, order = plan()

    def mod_use(s, c):
        return use[("mod", c)] if s.name == "ada1" else s.g0 + (2 * c - 1 if c else 0)

    def sel_use(s, c):
        if s.name == "ada1":
            return use[("sel", c)]
        return s.g0 + (2 * c + 2 if c < s.n - 1 else 2 * c + 1)
    chunk_stage = {}
    for s in order:
        for c in range(s.c0, s.c0 + s.n):
            chunk_stage[c] = s
    n_chunks = len(chunk_stage)

    def chunk_last_use(c):
        s = chunk_stage[c]
        if s.name[:3] == "ada":
            return mod_use(s, c - s.c0)
        return s.g0 + (c - s.c0 + 1) * s.uses - 1

    def chunk_floats(c):
        s = chunk_stage[c]
        return s.k * s.m

    with ExitStack() as ctx:
        def sb(name, shape, dt=F32):
            return ctx.enter_context(nc.sbuf_tensor(name, shape, dt))

        def sem(name):
            return ctx.enter_context(nc.semaphore(name))

        raw = [sb(f"raw{i}", [P, SLOT]) for i in range(NRAW)]
        whi = [sb(f"whi{i}", [P, SLOT], F32R) for i in range(NSPLIT)]
        wlo = [sb(f"wlo{i}", [P, SLOT], F32R) for i in range(NSPLIT)]
        xT = sb("xT", [P, KD, 2, HT])
        cn = sb("cn", [P, C_END])
        modT = [sb(f"modT{l}", [P, 48, 9]) for l in range(2)]
        G9 = sb("G9", [P, 4, KD, 9])
        B9 = sb("B9", [P, 4, KD, 9])
        lnT = sb("lnT", [P, KD, 8])
        lnA = sb("lnA", [P, KD, 8])
        OT = sb("OT", [P, KR, 40])
        sp8 = sb("sp8", [P, 4, KR])
        bT = sb("bT", [P, 101])
        gA = sb("gA", [P, 1])
        neglam = sb("neglam", [P, 1])
        neglr = sb("neglr", [P, 1])
        ones = sb("ones", [P, P])
        onesD = sb("onesD", [P, P])
        epsc = sb("epsc", [P, 1])
        stmp = sb("stmp", [P, 2, HS])
        sml = sb("sml", [P, 64])
        psig = sb("psig", [P, 1])
        xrS = sb("xrS", [P, KR, NS])
        pgt = sb("pgt", [P, 16], I32)
        mpv = sb("mpv", [P, H])
        bgi = sb("bgi", [P, 2])
        ident = cn[:, C_ID:C_ID + P]

        base = (nc.sbuf_base + 31) // 32 * 32 if not callable(nc.sbuf_base) else None
        HTB = 2 * HT * 4
        cH = nc.alloc_sbuf_tensor_at("cH", [P, KD, 18], F32R, offset=base)
        OS = nc.alloc_sbuf_tensor_at("OS", [P, KR, 20], F32, offset=base)
        base += KR * 20 * 4
        smp = nc.alloc_sbuf_tensor_at("smp", [P, 20, NS], F32, offset=base)
        tS = nc.alloc_sbuf_tensor_at("tS", [P, 2, KR, NS], F32, offset=base)
        base += 20 * NS * 4

        def at(name, shape, off, dt=F32):
            return nc.alloc_sbuf_tensor_at(name, shape, dt, offset=base + off)

        O_U = 24 * HTB
        O_L = 40 * HTB
        accS, accQ = at("accS", [P, 2, HT], O_L), at("accQ", [P, 2, HT], O_L + HTB)
        sqb = [at(f"sqb{i}", [P, 2, HT], O_L + (2 + i) * HTB) for i in range(2)]
        mu, rstd, tv = (at(n, [P, 2, HT], O_L + (2 + i) * HTB) for i, n in enumerate(["mu", "rstd", "tv"]))
        db = [at(f"db{i}", [P, 2, HT], O_L + (5 + i) * HTB) for i in range(2)]
        nb = [at(f"nb{i}", [P, 2, HT], O_L + (7 + i) * HTB) for i in range(2)]
        ub = [at(f"ub{i}", [P, 2, HT], O_L + (9 + i) * HTB) for i in range(2)]
        UH, UL = at("UH", [P, KD, 2, HT], O_U, F32R), at("UL", [P, KD, 2, HT], O_U + 8 * HTB, F32R)
        xtok = at("xtok", [P, 4, D], 0)
        RA, CR = at("RA", [P, D], 16384), at("CR", [P, D], 20480)
        RO = at("RO", [P, DR], 24576)
        BR, NR = at("BR", [P, P], 29696), at("NR", [P, P], 30208)
        lamr = at("lamr", [P, 272], 43 * HTB)
        proj = at("proj", [P, 24, 2, HT], 0)
        O_M = O_U
        def am(name, shape, off, dt=F32):
            n = 4
            for x in shape[1:]:
                n *= x
            assert O_M + off + n <= O_L + 12 * HTB, name
            return at(name, shape, O_M + off, dt)

        vtok = am("vtok", [P, 4, 512], 0)
        bkv = am("bkv", [P, 4, 768], 8192)
        stok = am("stok", [P, 2048], 8192)
        rowc = am("rowc", [P, 2, SEQ], 29440)
        acol = am("acol", [P, 4, H], 33536)
        gst = sml[:, 16:24]
        ncT = am("ncT", [P, 1], 33632)
        wl = am("wl", [P, 4], 33664)
        kw = am("kw", [P, 4, DK], 33696)
        Cst = am("Cst", [P, H, DK], 53152)
        nst = am("nst", [P, H, DK], 54176)
        cmB = [am(f"cmB{i}", [P, 2, 512], 36768 + i * 4096) for i in range(2)]
        PTall = am("PT", [P, 1280], 20480)
        Ex = [am("Ex0", [P, 512], 25600), am("Ex1", [P, 512], 34720)]
        pt_off = [0, 512, 896, 1152]
        PT = [PTall[:, pt_off[i]:pt_off[i] + 512 - i * P] for i in range(4)]
        rows = am("rows", [P, 6, 2, HT], 36768)
        ktok = am("ktok", [P, 4, 512], 20480)
        Sb = [at(f"Sb{i}", [P, 2, 512], 8 * HTB + i * 4096) for i in range(2)]
        Wb = [am(f"Wb{i}", [P, 512], 44960 + i * 2048) for i in range(2)]
        wTb = [am(f"wTb{i}", [P, 512], 49056 + i * 2048) for i in range(2)]
        st8 = [am(f"st8{i}", [P, 8], 55200 + i * 32) for i in range(2)]
        modrow = am("modrow", [P, 2, 256], 56192)
        rsq = [at(f"rsq{i}", [P, 2, HT], (4 + i) * HTB) for i in range(2)]
        selr = at("selr", [P, NS * P], 6 * HTB + 4 * 4096, F32R)
        Kp = [am(f"Kp{i}", [P, NPG, 512], i * 4096) for i in range(2)]
        stoks = am("stok_split", [P, 2, 1024], 16384, F32R)
        Vp = [at(f"Vp{i}", [P, NPG, 512], 6 * HTB + i * 4096) for i in range(4)]
        Vp += [am(f"Vp{4 + i}", [P, NPG, 512], i * 4096) for i in range(2)]
        Vp += [am(f"Vp{6 + i}", [P, NPG, 512], 16384 + i * 4096) for i in range(2)]
        qbc = am("qbc", [P, NS, 256], 24576)
        rmb = [am(f"rmb{i}", [P, 2, HT], 24576 + i * HTB) for i in range(2)]
        kbc = am("kbc", [P, NS, 256], 33280)
        Cs = am("Cs", [P, NS, 256], 41472)
        O_S = 49664
        Sc = am("Sc", [P, NPG, 64], O_S)
        Pq = am("Pq", [P, 257], O_S + 512)
        s8 = am("s8", [P, 64], O_S + 1568)
        CqS = am("CqS", [P, NS, H], O_S + 1824)
        wTs = am("wTs", [P, 3, 32], O_S + 1952)
        pks = am("pks", [P, NS, 16], O_S + 2336)
        Comb = am("Comb", [P, 32], O_S + 2848)
        sm8 = am("sm8", [P, 96], O_S + 2976)
        np8 = am("np8", [P, 512], O_S + 3360)
        t32 = am("t32", [P, 2, 32], O_S + 5408)
        cfac = am("cfac", [P, 2, 32], O_S + 5664)
        rsS = am("rsS", [P, 8, 2, HS], O_S + 5920)
        MH, ML = at("MH", [P, 8, 2, HT], O_U, F32R), at("ML", [P, 8, 2, HT], O_U + 8 * HTB, F32R)
        rrh, rrl = at("rrh", [P, 2, HT], 6 * HTB, F32R), at("rrl", [P, 2, HT], 7 * HTB, F32R)
        mxb = [at(f"mxb{i}", [P, 2, HT], (8 + i) * HTB) for i in range(2)]
        HH, HL = at("HH", [P, KH, 2, HT], 0, F32R), at("HL", [P, KH, 2, HT], 11 * HTB, F32R)
        silb = [at(f"silb{i}", [P, 2, HT], O_L + (5 + i) * HTB) for i in range(2)]
        hb = [at(f"hb{i}", [P, 2, HT], O_L + (7 + i) * HTB) for i in range(2)]
        xr = at("xr", [P, KR, 2 * HT], 0)
        rT, qT = at("rT", [P, KR, 2, HT], 0), at("qT", [P, KR, 2, HT], 0)
        YH = at("YH", [P, KR, 2, HT], 0, F32R)
        xc = at("xc", [P, KR, 2, HT], 10 * HTB)
        XL, YL = at("XL", [P, KR, 2, HT], 10 * HTB, F32R), at("YL", [P, KR, 2, HT], 10 * HTB, F32R)
        isb = [at(f"isb{i}", [P, 2, HT], (20 + i) * HTB) for i in range(2)]
        asq = [at(f"asq{i}", [P, 2, HT], (22 + i) * HTB) for i in range(2)]
        OST = at("OST", [P, DR], 20 * HTB)
        XH, aT = at("XH", [P, KR, 2, HT], 40 * HTB, F32R), at("aT", [P, KR, 2, HT], 40 * HTB)
        gb = [at(f"gb{i}", [P, 2, HT], (50 + i) * HTB) for i in range(2)]
        NG_RAW = 4

        def gate_buf(t):
            return isb[t - 2] if t in (2, 3) else gb[t % 2]
        ytok = [at(f"ytok{i}", [P, D], i * 4096) for i in range(4)]
        ysamp = at("ysamp", [P, D], 16384)
        xsm = at("xsm", [P, KD, NS], 20480)

        psum = [ctx.enter_context(nc.psum_tensor(f"ps{i}", [P, 2, 512], F32)) for i in range(NGRP)]

        raw_loaded = [sem(f"raw_loaded{i}") for i in range(NRAW)]
        hi_done, lo_done = sem("hi_done"), sem("lo_done")
        filled = sem("psum_filled")
        freed = [sem(f"psum_freed{i}") for i in range(NGRP)]
        consts_loaded, x_loaded, small_loaded = sem("consts_loaded"), sem("x_loaded"), sem("small_loaded")
        memset_done = sem("memset_done")
        silu_c, c_hi, c_lo = sem("silu_c"), sem("c_hi"), sem("c_lo")
        dve_step, act_step, pool_step = sem("dve_step"), sem("act_step"), sem("pool_step")
        d_ready, n_ready, u_ready, ut_ready = sem("d_ready"), sem("n_ready"), sem("u_ready"), sem("u_tokens_ready")
        uhi_ready, ulo_ready, x_ready = sem("uhi_ready"), sem("ulo_ready"), sem("x_ready")
        z_ready, sq_ready, acc_step = sem("z_ready"), sem("sq_ready"), sem("acc_step")
        mu_ready, var_ready, sd_ready = sem("mu_ready"), sem("var_ready"), sem("sd_ready")
        h_ready, hhi_ready, hlo_ready = sem("h_ready"), sem("hhi_ready"), sem("hlo_ready")
        evac = sem("proj_evacuated")
        act_q, dve_q = sem("act_answer"), sem("dve_ask")
        exq, pxq = sem("score_arg_ready"), sem("score_exp_ready")
        pt_ready, cm_ready = sem("pt_ready"), sem("cm_ready")
        for_pe = sem("dve_for_pe")
        pb_ready, w_ready = sem("p_ready"), sem("w_ready")
        smax_ready = sem("smax_ready")
        past_k = [sem(f"past_k{i}") for i in range(2)]
        past_v = [sem(f"past_v{i}") for i in range(NS)]
        k_used = sem("past_k_used")
        tok_hi, tok_lo, kq_ready, cq_ready = sem("tokens_hi"), sem("tokens_lo"), sem("kq_ready"), sem("cq_ready")
        rr_hi, tokens_stored = sem("rr_hi"), sem("tokens_stored")
        state_loaded, region_q = sem("state_loaded"), sem("region_free")
        state_n_loaded = sem("state_n_loaded")
        region_p = sem("prompt_states_stored")
        for_store = sem("dve_for_store")
        stored = sem("stored")
        rm_sq, mix_hi, mix_lo = sem("rms_sq"), sem("mix_hi"), sem("mix_lo")
        mx_ready = sem("mixed_ready")
        cv0, cv_ready, xch, xcl = sem("conv_first"), sem("conv_ready"), sem("xc_hi"), sem("xc_lo")
        hs_ready, gelu_ready = sem("h_states_ready"), sem("gelu_ready")
        ix_ready, a_ready, q_ready, sqrt_ready = sem("ix_ready"), sem("a_ready"), sem("q_ready"), sem("sqrt_ready")
        y_ready, yhi_ready, ylo_ready = sem("y_ready"), sem("yhi_ready"), sem("ylo_ready")
        y_stored, c_loaded, rsq_used, rr_ready = sem("y_stored"), sem("c_loaded"), sem("rsq_used"), sem("rr_ready")
        out_ready = sem("out_ready")
        zero_ready = sem("history_zero")

        block = ctx.enter_context(nc.Block())

        def ps(g):
            return psum[g % NGRP]

        def wait_filled(eng, g):
            eng.wait_ge(filled, g + 1)

        def free(ins, g):
            ins.then_inc(freed[g % NGRP], 1)

        def chain(eng, s):
            n = [0]

            def link(ins):
                n[0] += 1
                ins.then_inc(s, 1)
                eng.wait_ge(s, n[0])
            return link

        landed = {}

        def settled(eng, s, n=1):
            landed[s] = landed.get(s, 0) + n
            eng.wait_ge(s, landed[s])

        def tok(t):
            return t[:, :, 0:HALF]

        def smpl(t):
            return t[:, :, HALF:HT]

        def pT(g):
            return ps(g)[:, :, 0:HT]

        def weight_view(s):
            n = s.name
            if n[:3] == "ada":
                return a["w_ada"][int(n[3])].rearrange("(k p) (c m) -> c p k m", p=P, m=256)
            if n == "ein":
                return a["w_in_even"][0][:, 0:E_COLS].rearrange("(k p) (c m) -> c p k m", p=P, m=256)
            if n == "eout":
                return a["w_out_even"][0].rearrange("(k p) (c m) -> c p k m", p=P, m=256)
            if n[:2] == "fi":
                l, hf = int(n[2]), int(n[3])
                v = a["w_ffn_in"][l].rearrange("(k p) (g c m) -> c p k g m", p=P, g=2, m=P)
                return v[hf * KH:(hf + 1) * KH]
            if n[:2] == "fo":
                l, hf = int(n[2]), int(n[3])
                return a["w_ffn_out"][l][hf * KH * P:(hf + 1) * KH * P].rearrange("(k p) (c m) -> c p k m", p=P, m=P)
            if n in ("oinx", "oing"):
                c0 = 0 if n == "oing" else DR
                return a["w_in_odd"][0][:, c0:c0 + DR].rearrange("(k p) (c m) -> c p k m", p=P, m=256)
            return a["w_out_odd"][0].rearrange("(k p) (c m) -> c p k m", p=P, m=P)

        def past(sp):
            sp.wait_ge(small_loaded, 16 * N_SMALL)
            sp.wait_ge(region_q, 1)

            def page(b, g):
                return sp.value_load(pgt[0:1, 2 * b + g:2 * b + g + 1], min_val=0, max_val=NPOOL - 1)

            def load_k(b):
                if b >= 2:
                    sp.wait_ge(k_used, b - 1)
                for g in range(NPG):
                    pg = page(b, g)
                    src = a["cache_k"][0][bass.ds(pg, 1)].rearrange("a p h j d -> (a p) (h j d)")
                    sp.dma_start(Kp[b % 2][:, g], src).then_inc(past_k[b % 2], 16)

            def load_v(b):
                if b >= 4:
                    sp.wait_ge(k_used, 7 if b == 4 else 8)
                for g in range(NPG):
                    pg = page(b, g)
                    src = a["cache_v"][0][bass.ds(pg, 1)].rearrange("a p h d -> (a p) (h d)")
                    sp.dma_start(Vp[b][:, g], src).then_inc(past_v[b], 16)
            load_k(0)
            load_k(1)
            sp.dma_start(Cs[:], a["state_C"][0].rearrange("b h v k -> v (b h) k")).then_inc(state_loaded, 16)
            for b in range(2, NS):
                load_k(b)
                if b < 6:
                    load_v(b - 2)
            for b in range(4, NS):
                load_v(b)

        N_SMALL = 15
        count = {}

        @block.sync
        def _(sp):
            def load(s, c, it=None):
                gc = s.c0 + c
                slot = gc % NRAW
                if gc >= NRAW:
                    sp.wait_ge(lo_done, gc - NRAW + 1 + (0 if it is None else it * NRAW))
                v = weight_view(s)
                if s.name[:2] == "fi":
                    src = v[bass.ds(c + it * NRAW, 1)].rearrange("a p k g m -> (a p) k g m") if it is not None else v[c]
                    dst = raw[slot][:].rearrange("p (k g m) -> p k g m", k=8, g=2)
                    for g in range(2):
                        sp.dma_start(dst[:, :, g], src[:, :, g]).then_inc(raw_loaded[slot], 16)
                else:
                    src = v[bass.ds(c + it * NRAW, 1)].rearrange("a p k m -> (a p) k m") if it is not None else v[c]
                    dst = raw[slot][:, 0:s.k * s.m].rearrange("p (k m) -> p k m", m=s.m)
                    kh = s.k // 2
                    sp.dma_start(dst[:, 0:kh], src[:, 0:kh]).then_inc(raw_loaded[slot], 16)
                    sp.dma_start(dst[:, kh:], src[:, kh:]).then_inc(raw_loaded[slot], 16)

            sp.dma_start(cn[:], a["consts"]).then_inc(consts_loaded, 16)
            for s in order:
                if s.name == "gate":
                    gc = s.c0
                    sp.wait_ge(lo_done, gc - NRAW + 1)
                    dst = raw[gc % NRAW][:, 0:64].rearrange("p (k g m) -> p k g m", k=8, g=2)
                    src = a["w_in_even"][0][:, E_COLS:E_COLS + 8].rearrange("(k p) (g m) -> p k g m", p=P, g=2)
                    for g in range(2):
                        sp.dma_start(dst[:, :, g], src[:, :, g]).then_inc(raw_loaded[gc % NRAW], 16)
                    continue
                if s.name == "wax":
                    for b in range(s.n):
                        gc = s.c0 + b
                        sp.wait_ge(lo_done, gc - NRAW + 1)
                        dst = raw[gc % NRAW][:, 0:1024].rearrange("p (g k m) -> p g k m", g=2, m=256)
                        for g, w in enumerate(("w_a", "w_x")):
                            sp.dma_start(dst[:, g], a[w][0, b].rearrange("(k p) m -> p k m", p=P)).then_inc(raw_loaded[gc % NRAW], 16)
                    continue
                peel = NRAW if s.c0 == 0 else 0
                for c in range(peel):
                    load(s, c)
                if s.c0 == 0:
                    sp.dma_start(xtok[:], a["x_prompt"][0].rearrange("(b p) d -> p b d", p=P)).then_inc(x_loaded, 16)
                bodies = (s.n - peel) // NRAW
                if bodies > 1:
                    with sp.Fori(0, bodies) as it:
                        for c in range(NRAW):
                            load(s, peel + c, it=it)
                    peel += bodies * NRAW
                for c in range(peel, s.n):
                    load(s, c)
                if s.name == "eout":
                    past(sp)
            for tb in range(4):
                sp.wait_ge(out_ready, 3 + tb)
                sp.dma_start(o["y_prompt"][0][tb * P:(tb + 1) * P], ytok[tb][:]).then_inc(y_stored, 16)
            sp.wait_ge(out_ready, 7)
            sp.dma_start(o["y_sample"].rearrange("b t d -> (b t) d"), ysamp[0:NS]).then_inc(y_stored, 16)
            sp.wait_ge(y_stored, 16 * 5)

        @block.gpsimd
        def _(pool):
            link = chain(pool, pool_step)

            pool.memset(ones[:], 1.0).then_inc(memset_done, 1)
            settled(pool, memset_done)
            pool.memset(onesD[:], 1.0 / D).then_inc(memset_done, 1)
            settled(pool, memset_done)
            pool.memset(epsc[:], EPS).then_inc(memset_done, 1)
            settled(pool, memset_done)

            n = [0]

            def small(dst, src):
                pool.dma_start(dst, src).then_inc(small_loaded, 16)
                n[0] += 1
            small(RA[0:8], a["x_sample"].rearrange("b t d -> (b t) d"))
            small(RA[8:12], a["ln_g"].rearrange("l j d -> (l j) d"))
            small(RA[12:16], a["ln_b"].rearrange("l j d -> (l j) d"))
            small(RO[0:24], a["state_conv"][0].rearrange("b j d -> (b j) d"))
            small(RO[24:32], a["state_h"][0])
            small(RO[32:36], a["conv_w"][0])
            small(RO[36:37], a["conv_b"])
            small(RO[37:38], a["b_a"])
            small(RO[38:39], a["b_x"])
            small(RO[39:40], a["lru_lambda"])
            small(lamr[0:1, 0:256], a["lam"].rearrange("e r d -> e (r d)"))
            small(pgt[0:1, :], a["page_table"].rearrange("(e b) g -> e (b g)", e=1))
            small(mpv[0:NS], a["state_m"][0])
            small(bgi[0:4, 0:1], a["b_i"].rearrange("e h -> h e"))
            small(bgi[32:36, 1:2], a["b_f"].rearrange("e h -> h e"))
            assert n[0] == N_SMALL

            stores = [0]

            def store(dst, src):
                pool.dma_start(dst, src).then_inc(stored, 16)
                stores[0] += 1

            store(o["conv_sample"][0][:, 0:2, :], a["state_conv"][0][:, 1:3, :])

            for tb in range(4):
                g = use[("kv", tb)]
                pool.wait_ge(freed[g % NGRP], g // NGRP + 1)
                store(o["k_prompt"][0, 0, tb].rearrange("t h j d -> t (h j d)"), ktok[:, tb])
                store(o["v_prompt"][0, 0, tb].rearrange("t h d -> t (h d)"), vtok[:, tb])
            pool.wait_ge(for_store, 1)
            store(o["m_prompt"][0, 0].rearrange("(h e) -> h e", e=1), rowc[0:4, 1, SEQ - 1:SEQ])
            pool.wait_ge(stored, 16 * stores[0])
            def decay_argument(k):
                h, quarter = k // 4, k % 4
                n = SEQ - quarter * P
                g = use[("bc", h)]
                pool.wait_ge(freed[g % NGRP], g // NGRP + 1)
                if k >= 2:
                    g = use[("mS", (k - 2) // 4, (k - 2) % 4)]
                    pool.wait_ge(freed[g % NGRP], g // NGRP + 1)
                pool.tensor_tensor(Ex[k % 2][:, 0:n], cmB[h % 2][:, 0, quarter * P:SEQ], cn[:, C_MASK:C_MASK + n],
                                   ALU.add).then_inc(exq, 1)
                settled(pool, exq)

            def lo(c):
                pool.wait_ge(hi_done, c + 1)
                pool.wait_ge(lo_done, c)
                pool.tensor_tensor(wlo[c % 2][:], raw[c % NRAW][:], whi[c % 2][:].bitcast(F32), ALU.subtract).then_inc(lo_done, 1)
                pool.wait_ge(lo_done, c + 1)
            decay_argument(0)
            for s_ in range(STEPS):
                if s_ < 15:
                    decay_argument(s_ + 1)
                if s_ >= 1:
                    lo(st["ada1"].c0 + ADA_EARLY + s_ + 1)
            pool.wait_ge(for_store, 2)
            store(o["C_prompt"][0, 0].rearrange("h v k -> v h k"), Cst[:])
            store(o["n_prompt"][0].rearrange("a h k -> a (h k)"), nst[0:1].rearrange("p h k -> p (h k)"))
            pool.wait_ge(stored, 16 * stores[0])
            pool.wait_ge(for_store, 3)
            pool.memset(np8[:], 0.0).then_inc(region_p, 1)
            settled(pool, region_p)
            pool.dma_start(np8[0:NS, 0:256], a["state_n"][0].rearrange("b h k -> b (h k)")).then_inc(state_n_loaded, 16)
            pool.wait_ge(for_store, 5)
            pool.dma_start(o["k_sample"][0].rearrange("b t h j d -> (b t) (h j d)"), stok[0:NS, 512:1024]).then_inc(tokens_stored, 16)
            pool.dma_start(o["v_sample"][0].rearrange("b t h d -> (b t) (h d)"), stok[0:NS, 1024:1536]).then_inc(tokens_stored, 16)
            pool.wait_ge(state_loaded, 16)
            for b in range(NS):
                pool.wait_ge(kq_ready, 2 * b + 1)
                pool.tensor_tensor(qbc[:, b], qbc[:, b], Cs[:, b], ALU.mult).then_inc(cq_ready, 1)
                settled(pool, cq_ready)
            pool.wait_ge(for_store, 6)
            store(o["m_sample"][0], sm8[0:NS, 0:4])
            store(o["n_sample"][0].rearrange("b h k -> b (h k)"), np8[0:NS, 256:512])
            pool.wait_ge(for_store, 7)
            C4 = Cs[:].rearrange("p b (h k) -> p (b h) k", h=H)
            K4 = kbc[:].rearrange("p b (h k) -> p (b h) k", h=H)
            pool.wait_ge(kq_ready, 2 * NS)
            link(pool.tensor_tensor(K4, K4, cfac[:, 0].unsqueeze(2).broadcast_to([P, 32, DK]), ALU.mult))
            link(pool.tensor_tensor(C4, C4, cfac[:, 1].unsqueeze(2).broadcast_to([P, 32, DK]), ALU.mult))
            link(pool.tensor_tensor(C4, C4, K4, ALU.add))
            store(o["C_sample"][0].rearrange("b h v k -> v (b h) k"), Cs[:].rearrange("p b (h k) -> p (b h) k", h=H))
            mid_stores = count["middle"] = stores[0]

            def ln_sums(r):
                if r == 0:
                    pool.wait_ge(stored, 16 * mid_stores)
                for t in range(KD - 1):
                    pool.wait_ge(z_ready, 8 * r + t + 1)
                    k = 14 * r + 2 * t
                    if t == 0:
                        pool.tensor_copy(accS[:], xT[:, t]).then_inc(acc_step, 1)
                        settled(pool, acc_step)
                    else:
                        pool.wait_ge(acc_step, k)
                        pool.tensor_tensor(accS[:], accS[:], xT[:, t], ALU.add).then_inc(acc_step, 1)
                        settled(pool, acc_step)
                    pool.wait_ge(sq_ready, 8 * r + t + 1)
                    if t == 0:
                        pool.tensor_copy(accQ[:], sqb[t % 2][:]).then_inc(acc_step, 1)
                        settled(pool, acc_step)
                    else:
                        pool.tensor_tensor(accQ[:], accQ[:], sqb[t % 2][:], ALU.add).then_inc(acc_step, 1)
                        settled(pool, acc_step)

            def ln_center(r):
                pool.wait_ge(mu_ready, r + 1)
                for t in range(KD):
                    if t >= 2:
                        pool.wait_ge(n_ready, 8 * r + t - 1)
                    pool.tensor_tensor(db[t % 2][:], xT[:, t], mu[:], ALU.subtract).then_inc(d_ready, 1)
                    settled(pool, d_ready)

            for r in range(4):
                ln_sums(r)
                ln_center(r)
                if r == 1:
                    pool.wait_ge(ulo_ready, 8 * 3)
                    pool.memset(xr[:, :, 0:3], 0.0).then_inc(zero_ready, 1)
                    settled(pool, zero_ready)
                    for t in range(KR):
                        pool.wait_ge(xch, t + 1)
                        pool.tensor_tensor(XL[:, t], xc[:, t], XH[:, t].bitcast(F32), ALU.subtract).then_inc(xcl, 1)
                        settled(pool, xcl)
                    s = st["wax"]
                    for t in range(KR):
                        g = s.g0 + 2 * (t - t % 2) + 3
                        wait_filled(pool, g)
                        link(pool.tensor_tensor(xc[:, t], XH[:, t].bitcast(F32), XL[:, t].bitcast(F32), ALU.add))
                        pool.wait_ge(freed[(g - 1 + t % 2) % NGRP], (g - 1 + t % 2) // NGRP + 1)
                        pool.tensor_tensor(xc[:, t], xc[:, t], isb[t % 2][:], ALU.mult).then_inc(ix_ready, 1)
                        settled(pool, ix_ready)
                    s = st["oing"]
                    for t in range(KR):
                        pool.wait_ge(hs_ready, t + 1)
                        if t < NG_RAW:
                            pool.wait_ge(gelu_ready, t + 1)
                        else:
                            pool.wait_ge(freed[(s.g0 + t) % NGRP], (s.g0 + t) // NGRP + 1)
                        pool.tensor_tensor(xc[:, t], xc[:, t], gate_buf(t)[:], ALU.mult).then_inc(y_ready, 1)
                        settled(pool, y_ready)
                    pool.wait_ge(out_ready, 2)
                    store(o["conv_prompt"][0, 0], OST[0:3])
                    store(o["conv_sample"][0][:, 2, :], OST[3:11])
                    store(o["h_prompt"][0], OST[11:12])
                    store(o["h_sample"][0], OST[12:20])
                    count["rows_stored"] = stores[0]
            pool.wait_ge(stored, 16 * stores[0])

        def middle_act(act, link, hi):
            act.wait_ge(evac, 24)
            nc.scalar.activation(proj[:, 20:24], proj[:, 20:24], ACT.Sigmoid).then_inc(act_q, 1)
            settled(act, act_q)
            act.wait_ge(act_q, 4)
            g = use_gate
            wait_filled(act, g)
            act.wait_ge(dve_q, 3)
            nc.scalar.activation(rows[0:4, 0], ps(g)[0:4, :, 0:HT], ACT.Tanh, scale=1.0 / 15.0,
                                 bias=sml[0:4, 8:9]).then_inc(act_q, 1)
            settled(act, act_q)
            act.wait_ge(dve_q, 4)
            nc.scalar.activation(rows[0:4, 2], rows[0:4, 2], ACT.Exp, scale=-1.0).then_inc(act_q, 1)
            settled(act, act_q)
            act.wait_ge(act_q, 6)
            nc.scalar.activation(rows[0:4, 2], rows[0:4, 2], ACT.Ln, bias=1.0).then_inc(act_q, 1)
            settled(act, act_q)
            ada = st["ada1"]
            for tb in range(4):
                g = use[("kv", tb)]
                wait_filled(act, g)
                link(nc.scalar.activation(ktok[:, tb], ps(g)[:, 0], ACT.Identity))
                free(nc.scalar.activation(vtok[:, tb], ps(g)[:, 1], ACT.Identity), g)
                act.wait_ge(freed[g % NGRP], g // NGRP + 1)
                hi(ada.c0 + tb + 2)
            for tb in range(4):
                g = use[("bkv", tb)]
                wait_filled(act, g)
                free(nc.scalar.activation(bkv[:, tb], ps(g)[:].rearrange("p a b -> p (a b)")[:, 0:768], ACT.Identity), g)
                act.wait_ge(freed[g % NGRP], g // NGRP + 1)
                if tb < ADA_EARLY - 4:
                    hi(ada.c0 + 4 + tb + 2)

            def unit_exp(u):
                n = (u % 4 + 1) * P
                act.wait_ge(pb_ready, u + 1)
                for j in range(2):
                    ins = nc.scalar.activation(Sb[u % 2][:, j, 0:n], Sb[u % 2][:, j, 0:n], ACT.Exp,
                                               bias=st8[u % 2][:, j:j + 1], accum_out=st8[u % 2][:, 2 + j:3 + j])
                    ins.then_inc(smax_ready, 1)
                    settled(act, smax_ready)

            def head_rows(h):
                g = use[("bc", h)]
                wait_filled(act, g)
                cm = cmB[h % 2]
                if h >= 2:
                    act.wait_ge(for_pe, h + 2)
                link(nc.scalar.activation(cm[:, 0], ps(g)[:, 0], ACT.Identity))
                free(nc.scalar.activation(cm[:, 1], ps(g)[:, 1], ACT.Exp, scale=-1.0), g)
                act.wait_ge(freed[g % NGRP], g // NGRP + 1)

            def head_state_weights(h):
                nc.scalar.activation(ncT[:], cmB[h % 2][:, 0, SEQ - 1:SEQ], ACT.Copy, scale=-1.0).then_inc(cm_ready, 1)
                settled(act, cm_ready)
                if h >= 1:
                    act.wait_ge(for_pe, h + 3)
                nc.scalar.activation(wl[:], acol[:, :, h], ACT.Exp, bias=ncT[:]).then_inc(cm_ready, 1)
                settled(act, cm_ready)

            def decay(k):
                h, quarter = k // 4, k % 4
                n = SEQ - quarter * P
                act.wait_ge(exq, k + 1)
                nc.scalar.activation(Ex[k % 2][:, 0:n], Ex[k % 2][:, 0:n], ACT.Exp, scale=-1.0,
                                     bias=acol[:, quarter, h:h + 1]).then_inc(pxq, 1)
                settled(act, pxq)

            def unit_wT(u):
                n = (u % 4 + 1) * P
                g = use[("T", u)]
                wait_filled(act, g)
                if u >= 2:
                    wait_filled(act, use[("PV", u - 2)])
                free(nc.scalar.activation(wTb[u % 2][:, 0:n], ps(g)[:, 0, 0:n], ACT.Identity), g)
                act.wait_ge(freed[g % NGRP], g // NGRP + 1)
            act.wait_ge(for_store, 1)
            for s_ in range(STEPS):
                h, quarter = s_ // 4, s_ % 4
                if s_ >= 1:
                    hi(ada.c0 + ADA_EARLY + s_ + 1)
                if s_ < 16:
                    if quarter == 0:
                        head_rows(h)
                    unit_exp(s_)
                    decay(s_)
                if 1 <= s_ < 17:
                    unit_wT(s_ - 1)
                if s_ < 16 and quarter == 0:
                    head_state_weights(h)
            hi(ada.c0 + ada.n + 1)
            act.wait_ge(for_store, 5)
            nc.scalar.activation(stoks[0:NS, 0].rearrange("p (a c) -> p a c", a=2),
                                 stok[0:NS].rearrange("p (a c) -> p a c", c=512)[:, 0:4:3], ACT.Identity).then_inc(tok_hi, 1)
            settled(act, tok_hi)
            nc.scalar.activation(selr[0:NS], cn[0:NS, C_SEL:C_SEL + NS * P], ACT.Identity).then_inc(tok_hi, 1)
            settled(act, tok_hi)
            for b in range(NS):
                g = use[("qb", b)]
                wait_filled(act, g)
                for i, dst in enumerate((qbc, kbc)):
                    nc.scalar.activation(dst[:, b], ps(g)[:, 1, i * 256:(i + 1) * 256], ACT.Identity).then_inc(kq_ready, 1)
                    settled(act, kq_ready)
            for t in range(8):
                src = proj[:, t] if t < 4 else proj[:, 12 + t]
                if t >= 2:
                    act.wait_ge(rsq_used, t - 1)
                nc.scalar.activation(tok(rsq[t % 2]), tok(src), ACT.Square).then_inc(rm_sq, 1)
                settled(act, rm_sq)
            act.wait_ge(dve_q, 5)
            nc.scalar.activation(Pq[0:64], Pq[0:64], ACT.Exp, bias=t32[0:64, 0, 0:1],
                                 accum_out=t32[0:64, 0, 1:2]).then_inc(act_q, 1)
            settled(act, act_q)
            act.wait_ge(dve_q, 6)
            nc.scalar.activation(sm8[0:NS, 16:24], sm8[0:NS, 16:24], ACT.Exp).then_inc(act_q, 1)
            settled(act, act_q)
            nc.scalar.activation(sm8[0:NS, 24:28], sm8[0:NS, 0:4], ACT.Exp, scale=-1.0).then_inc(act_q, 1)
            settled(act, act_q)
            g = use["rms"]
            wait_filled(act, g)
            free(nc.scalar.activation(tok(rmb[0][0:8]), ps(g)[0:8, :, 0:HALF], ACT.Sqrt, bias=epsc[0:8]), g)
            act.wait_ge(freed[g % NGRP], g // NGRP + 1)
            act.wait_ge(for_pe, 12)
            nc.scalar.activation(rsS[:, 0:4], proj[:, 0:4, :, HALF:HT], ACT.Square)
            nc.scalar.activation(rsS[:, 4:8], proj[:, 16:20, :, HALF:HT], ACT.Square).then_inc(rm_sq, 1)
            settled(act, rm_sq)
            g = use["rmsS"]
            wait_filled(act, g)
            free(nc.scalar.activation(smpl(rmb[0][0:8]), ps(g)[0:8, :, 0:HS], ACT.Sqrt, bias=epsc[0:8]), g)
            act.wait_ge(freed[g % NGRP], g // NGRP + 1)
            act.wait_ge(rr_ready, 1)
            nc.scalar.activation(rrh[0:8], rmb[1][0:8], ACT.Identity).then_inc(rr_hi, 1)
            settled(act, rr_hi)
            act.wait_ge(tokens_stored, 32)
            for t in range(8):
                g = use[("rb", t)]
                if t < 4:
                    act.wait_ge(freed[g % NGRP], g // NGRP + 1)
                else:
                    act.wait_ge(mx_ready, t - 3)
                nc.scalar.activation(MH[:, t], mxb[t % 2][:], ACT.Identity).then_inc(mix_hi, 1)
                settled(act, mix_hi)

        def cm_sem(ins):
            ins.then_inc(cm_ready, 1)
            settled(nc.scalar, cm_ready)

        use_gate = st["gate"].g0

        @block.scalar
        def _(act):
            link = chain(act, act_step)

            def hi(c):
                if c >= n_chunks:
                    return
                s = chunk_stage[c]
                act.wait_ge(raw_loaded[c % NRAW], 32 * (c // NRAW + 1))
                if c >= NSPLIT:
                    wait_filled(act, chunk_last_use(c - NSPLIT))
                if s.name == "gate":
                    src = raw[c % NRAW][:, 0:64].rearrange("p (k g m) -> p k g m", k=8, g=2)
                    dst = whi[c % 2][:, 0:1024].rearrange("p (k g m) -> p k g m", k=8, m=32)[:, :, 0:2, 0:4]
                    ins = nc.scalar.activation(dst, src, ACT.Identity)
                else:
                    f = chunk_floats(c)
                    ins = nc.scalar.activation(whi[c % 2][:, 0:f], raw[c % NRAW][:, 0:f], ACT.Identity)
                ins.then_inc(hi_done, 1)
                settled(act, hi_done)

            act.dma_start(CR[0:1], a["c_prompt"]).then_inc(c_loaded, 16)
            act.dma_start(CR[1:9], a["c_sample"]).then_inc(c_loaded, 16)
            act.dma_start(BR[0:96], a["b_ada"].rearrange("l (r m) -> (l r) m", m=P)).then_inc(c_loaded, 16)
            act.dma_start(NR[0:1], a["attn_norm_g"]).then_inc(c_loaded, 16)
            act.dma_start(NR[1:5], a["mlstm_norm_g"][0]).then_inc(c_loaded, 16)
            act.wait_ge(c_loaded, 80)
            nc.scalar.activation(CR[0:9], CR[0:9], ACT.Silu).then_inc(silu_c, 1)
            settled(act, silu_c)
            hi(0)
            hi(1)
            act.wait_ge(memset_done, 3)
            wait_filled(act, use["tc"])
            nc.scalar.activation(cH[:, :, 0:9], ps(use["tc"])[:, 0, 0:72].rearrange("p (k c) -> p k c", c=9),
                                 ACT.Identity).then_inc(c_hi, 1)
            settled(act, c_hi)
            for c in range(24):
                hi(c + 2)
            def split_u(q):
                r = q - 1
                for t in range(KD):
                    if r >= 0 and q < 4 and t % 2:
                        act.wait_ge(n_ready, 8 * r + t + 1)
                        if t >= 2:
                            act.wait_ge(ulo_ready, 8 * q + t - 1)
                        nc.scalar.activation(tok(ub[t % 2]), tok(nb[t % 2]), ACT.Identity, scale=G9[:, q, t, 0:1],
                                             bias=B9[:, q, t, 0:1]).then_inc(ut_ready, 1)
                        settled(act, ut_ready)
                    if q < 4:
                        act.wait_ge(u_ready, 8 * q + t + 1)
                        nc.scalar.activation(UH[:, t], ub[t % 2][:], ACT.Identity).then_inc(uhi_ready, 1)
                        settled(act, uhi_ready)
                    if r >= 0:
                        act.wait_ge(n_ready, 8 * r + t + 1)
                        lt = lnT if r == 3 else lnA
                        nc.scalar.activation(xT[:, t], nb[t % 2][:], ACT.Identity, scale=lt[:, t, r:r + 1],
                                             bias=lt[:, t, 4 + r:5 + r]).then_inc(x_ready, 1)
                        settled(act, x_ready)

            def squares(r, t):
                act.wait_ge(z_ready, 8 * r + t + 1)
                if t >= 2:
                    act.wait_ge(acc_step, 14 * r + 2 * (t - 2) + 2)
                nc.scalar.activation(sqb[t % 2][:], xT[:, t], ACT.Square).then_inc(sq_ready, 1)
                settled(act, sq_ready)

            def ln_sqrt(r):
                link(nc.scalar.activation(sml[:, 12:13], epsc[:], ACT.Sqrt))
                act.wait_ge(var_ready, r + 1)
                nc.scalar.activation(tv[:], tv[:], ACT.Sqrt).then_inc(sd_ready, 1)
                settled(act, sd_ready)

            def ffn(l):
                for hf in range(2):
                    s = st[f"fi{l}{hf}"]
                    for c in range(s.n):
                        k = (2 * l + hf) * KH + c
                        g = s.g0 + 2 * c
                        wait_filled(act, g)
                        if k >= 2:
                            act.wait_ge(h_ready, k - 1)
                        ins = nc.scalar.activation(silb[c % 2][:], pT(g), ACT.Silu)
                        free(ins, g)
                        act.wait_ge(freed[g % NGRP], g // NGRP + 1)
                        if c < s.n - 1:
                            hi(s.c0 + c + 2)
                        act.wait_ge(h_ready, k + 1)
                        if l == 1 and hf == 0 and c == 0:
                            act.wait_ge(stored, 16 * count["rows_stored"])
                        nc.scalar.activation(HH[:, c], hb[c % 2][:], ACT.Identity).then_inc(hhi_ready, 1)
                        settled(act, hhi_ready)
                    hi(s.c0 + s.n + 1)
                    s = st[f"fo{l}{hf}"]
                    for c in range(s.n):
                        if hf == 1 and c >= 1:
                            squares(2 * l + 1, c - 1)
                        hi(s.c0 + c + 2)
                squares(2 * l + 1, KD - 1)
                ln_sqrt(2 * l + 1)

            split_u(0)
            act.wait_ge(dve_q, 1)
            nc.scalar.activation(sp8[:, 1], sp8[:, 1], ACT.Exp, scale=-1.0).then_inc(act_q, 1)
            settled(act, act_q)
            act.wait_ge(dve_q, 2)
            nc.scalar.activation(lamr[0:1, 258:260], lamr[0:1, 256:258], ACT.Exp).then_inc(act_q, 1)
            settled(act, act_q)
            act.wait_ge(act_q, 2)
            nc.scalar.activation(sp8[:, 1], sp8[:, 1], ACT.Ln, bias=1.0).then_inc(act_q, 1)
            settled(act, act_q)
            for c in range(12):
                hi(st["ein"].c0 + c + 2)
            hi(st["gate"].c0 + 2)
            middle_act(act, link, hi)
            act.wait_ge(stored, 16 * count["middle"])
            for c in range(4):
                if c >= 1:
                    squares(0, 2 * c - 2)
                    squares(0, 2 * c - 1)
                if c == 3:
                    squares(0, 6)
                hi(st["eout"].c0 + c + 2)
            squares(0, 7)
            ln_sqrt(0)
            split_u(1)
            ffn(0)
            split_u(2)
            def high_xc(t):
                act.wait_ge(cv_ready, t + 1)
                nc.scalar.activation(XH[:, t], xc[:, t], ACT.Identity).then_inc(xch, 1)
                settled(act, xch)
            s = st["oinx"]
            for c in range(s.n):
                hi(s.c0 + c + 2)
                for m in range(2):
                    t = 2 * c + m
                    g = s.g0 + t
                    wait_filled(act, g)
                    if t == 0:
                        act.wait_ge(zero_ready, 1)
                    nc.scalar.activation(xr[:, t, 3:3 + SEQ].rearrange("p (a b) -> p a b", a=2), ps(g)[:, :, 0:HALF], ACT.Identity)
                    nc.scalar.activation(xc[:, t], pT(g), ACT.Identity, scale=OT[:, t, 35:36],
                                         bias=OT[:, t, 36:37]).then_inc(cv0, 1)
                    settled(act, cv0)
                    if t >= 1:
                        high_xc(t - 1)
            high_xc(KR - 1)
            s = st["wax"]
            for b in range(s.n):
                for m in range(2):
                    t, g = 2 * b + m, s.g0 + 4 * b + m
                    wait_filled(act, g)
                    if t == 0:
                        act.wait_ge(for_store, 8)
                    free(nc.scalar.activation(rT[:, t], pT(g), ACT.Sigmoid, bias=OT[:, t, 37:38]), g)
                    act.wait_ge(freed[g % NGRP], g // NGRP + 1)
                for m in range(2):
                    t, g = 2 * b + m, s.g0 + 4 * b + 2 + m
                    wait_filled(act, g)
                    if t >= 2:
                        act.wait_ge(ix_ready, t - 1)
                    free(nc.scalar.activation(isb[m][:], pT(g), ACT.Sigmoid, bias=OT[:, t, 38:39]), g)
                    act.wait_ge(freed[g % NGRP], g // NGRP + 1)
                hi(s.c0 + b + 2)
            s = st["oing"]
            for t in range(KR):
                act.wait_ge(ix_ready, t + 1)
                link(nc.scalar.activation(aT[:, t], rT[:, t], ACT.Exp, scale=sp8[:, 3, t:t + 1]))
                nc.scalar.activation(qT[:, t], rT[:, t], ACT.Tanh, scale=sp8[:, 2, t:t + 1])
                if t >= 2:
                    act.wait_ge(q_ready, t - 1)
                nc.scalar.activation(asq[t % 2][:], aT[:, t], ACT.Square).then_inc(a_ready, 1)
                settled(act, a_ready)
                if t == 5:
                    hi(s.c0 + 2)
            for t in range(KR):
                act.wait_ge(q_ready, t + 1)
                nc.scalar.activation(qT[:, t], qT[:, t], ACT.Sqrt).then_inc(sqrt_ready, 1)
                settled(act, sqrt_ready)

            def high_y(t):
                act.wait_ge(y_ready, t + 1)
                nc.scalar.activation(YH[:, t], xc[:, t], ACT.Identity).then_inc(yhi_ready, 1)
                settled(act, yhi_ready)
            hi(s.c0 + 3)
            for t in range(KR):
                if t >= 4 and t % 2 == 0:
                    hi(s.c0 + t // 2 + 2)
                g = s.g0 + t
                b = gate_buf(t)
                if t < NG_RAW:
                    act.wait_ge(freed[g % NGRP], g // NGRP + 1)
                    nc.scalar.activation(b[:], b[:], ACT.Gelu_apprx_tanh).then_inc(gelu_ready, 1)
                    settled(act, gelu_ready)
                else:
                    wait_filled(act, g)
                    act.wait_ge(y_ready, t - 3 if t < 6 else t - 1)
                    free(nc.scalar.activation(b[:], pT(g), ACT.Gelu_apprx_tanh), g)
                    act.wait_ge(freed[g % NGRP], g // NGRP + 1)
                if t >= 1:
                    high_y(t - 1)
            high_y(KR - 1)
            s = st["oout"]
            for c in range(s.n):
                if c >= 1:
                    squares(2, c - 1)
                hi(s.c0 + c + 2)
            squares(2, KD - 1)
            ln_sqrt(2)
            split_u(3)
            ffn(1)
            split_u(4)

        def middle_dve(dve, link, lo, modulation_rows, select, modulation_sums):
            v = nc.vector
            v.tensor_copy(smp[:, 0:20].rearrange("p t (a b) -> p t a b", a=2), proj[:, 0:20, :, HALF:HT]).then_inc(for_pe, 1)
            settled(dve, for_pe)
            v.tensor_scalar(sml[0:4, 8:9], bgi[0:4, 0:1], 1.0 / 15.0, None, ALU.mult).then_inc(dve_q, 1)
            settled(dve, dve_q)
            g = use_gate
            wait_filled(dve, g)
            x_f = rows[0:4, 1]
            link(v.tensor_scalar(x_f, ps(g)[32:36, :, 0:HT], bgi[32:36, 1:2], None, ALU.add))
            link(v.tensor_scalar(rows[0:4, 2], x_f, -1.0, None, ALU.mult))
            v.tensor_tensor(rows[0:4, 2], rows[0:4, 2], x_f, ALU.max).then_inc(dve_q, 1)
            settled(dve, dve_q)
            dve.wait_ge(dve_q, 4)
            link(v.tensor_scalar(x_f, x_f, 0.0, None, ALU.min))
            dve.wait_ge(act_q, 7)
            free(v.tensor_scalar(rows[0:4, 0], rows[0:4, 0], 15.0, None, ALU.mult), g)
            dve.wait_ge(freed[g % NGRP], g // NGRP + 1)
            link(v.tensor_tensor(x_f, x_f, rows[0:4, 2], ALU.subtract))
            one_row = ones[0:4, 0:1].broadcast_to([4, HALF])
            for hf in range(2):
                ini = 0.0 if hf == 0 else rows[0:4, 3, 0, HALF - 1:HALF]
                link(v.tensor_tensor_scan(rows[0:4, 3, hf, 0:HALF], one_row, x_f[:, hf, 0:HALF], ini, ALU.mult, ALU.add))
            link(v.tensor_tensor(tok(rows[0:4, 4]), tok(rows[0:4, 0]), tok(rows[0:4, 3]), ALU.subtract))
            for hf in range(2):
                ini = 0.0 if hf == 0 else rowc[0:4, 0, HALF - 1:HALF]
                link(v.tensor_tensor_scan(rowc[0:4, 0, hf * HALF:(hf + 1) * HALF], one_row, rows[0:4, 4, hf, 0:HALF], ini,
                                          ALU.mult, ALU.max))
            link(v.tensor_tensor(rowc[0:4, 1].rearrange("p (a b) -> p a b", a=2), tok(rows[0:4, 3]),
                                 rowc[0:4, 0].rearrange("p (a b) -> p a b", a=2), ALU.add))
            link(v.tensor_copy(rows[0:4, 5, 0, 0:8].rearrange("p (a b) -> p a b", a=2), smpl(rows[0:4, 0])))
            v.tensor_copy(rows[0:4, 5, 0, 8:16].rearrange("p (a b) -> p a b", a=2), smpl(x_f)).then_inc(for_pe, 1)
            settled(dve, for_pe)
            ada = st["ada1"]
            for c in range(ADA_EARLY):
                modulation_rows(ada, c)
                lo(ada.c0 + c + 2)
                if c >= 1:
                    select(ada, c - 1)
            g = use["acol"]
            wait_filled(dve, g)
            free(v.tensor_copy(acol[:], ps(g)[:, 0, 0:16].rearrange("p (a b) -> p a b", a=4)), g)
            dve.wait_ge(freed[g % NGRP], g // NGRP + 1)
            g = use["gs"]
            wait_filled(dve, g)
            free(v.tensor_copy(gst[0:NS], ps(g)[0:NS, 0, 0:8]), g)
            dve.wait_ge(freed[g % NGRP], g // NGRP + 1)
            v.memset(sml[:, 10:11], 0.0).then_inc(for_store, 1)
            settled(dve, for_store)

            def scores(u):
                h, i = u // 4, u % 4
                n = (i + 1) * P
                g = use[("S", u)]
                S, s8_ = Sb[u % 2], st8[u % 2]
                wait_filled(dve, g)
                dist = cn[:, C_DIST + 512 - n:C_DIST + 512].unsqueeze(1).broadcast_to([P, 2, n])
                free(v.scalar_tensor_tensor(S[:, :, 0:n], dist, -(2.0 ** (-2.0 * (h + 1))), ps(g)[:, :, 0:n], ALU.mult, ALU.add), g)
                dve.wait_ge(freed[g % NGRP], g // NGRP + 1)
                link(v.tensor_reduce(s8_[:, 4:6], S[:, :, 0:n], AX.X, ALU.max))
                v.tensor_scalar(s8_[:, 0:2], s8_[:, 4:6], -1.0, None, ALU.mult).then_inc(pb_ready, 1)
                settled(dve, pb_ready)

            def weights(u):
                n = (u % 4 + 1) * P
                S, s8_ = Sb[u % 2], st8[u % 2]
                dve.wait_ge(smax_ready, 2 * u + 2)
                link(v.reciprocal(s8_[:, 2:4], s8_[:, 2:4]))
                link(v.tensor_scalar(s8_[:, 3:4], s8_[:, 3:4], neglam[:, 0:1], None, ALU.mult))
                link(v.tensor_scalar(S[:, 1, 0:n], S[:, 1, 0:n], s8_[:, 3:4], None, ALU.mult))
                if u >= 2:
                    wait_filled(dve, use[("T", u - 2)])
                v.scalar_tensor_tensor(Wb[u % 2][:, 0:n], S[:, 0, 0:n], s8_[:, 2:3], S[:, 1, 0:n], ALU.mult, ALU.add).then_inc(w_ready, 1)
                settled(dve, w_ready)

            def outputs(u):
                h, i = u // 4, u % 4
                g = use[("PV", u)]
                wait_filled(dve, g)
                free(v.tensor_copy(proj[:, h, i // 2, (i % 2) * P:(i % 2 + 1) * P], ps(g)[:, 0, 0:P]), g)
                dve.wait_ge(freed[g % NGRP], g // NGRP + 1)

            def decayed(k):
                h, quarter = k // 4, k % 4
                n = SEQ - quarter * P
                g = use[("mS", h, quarter)]
                dve.wait_ge(pxq, k + 1)
                wait_filled(dve, g)
                if h >= 1 and quarter == 0:
                    wait_filled(dve, use[("mN", h - 1)])
                free(v.tensor_tensor(PT[quarter][:, 0:n], ps(g)[:, 0, 0:n], Ex[k % 2][:, 0:n], ALU.mult), g)
                dve.wait_ge(freed[g % NGRP], g // NGRP + 1)

            def state_keys(h):
                dve.wait_ge(cm_ready, 2 * h + 2)
                if h >= 1:
                    wait_filled(dve, use[("mC", h - 1)])
                v.tensor_tensor(kw[:], bkv[:, :, 512 + h * DK:512 + (h + 1) * DK],
                                wl[:].unsqueeze(2).broadcast_to([P, 4, DK]), ALU.mult).then_inc(pt_ready, 1)
                settled(dve, pt_ready)

            def head_end(h):
                cm = cmB[h % 2]
                g = use[("mN", h)]
                wait_filled(dve, g)
                link(v.scalar_tensor_tensor(cm[:, 1], ps(g)[:, 1], -1.0, cm[:, 1], ALU.mult, ALU.max))
                link(v.tensor_tensor(cm[:, 1], ps(g)[:, 1], cm[:, 1], ALU.max))
                link(v.reciprocal(cm[:, 1], cm[:, 1]))
                free(v.tensor_tensor(tok(proj[:, 16 + h]), ps(g)[:, 0].rearrange("p (a b) -> p a b", a=2),
                                     cm[:, 1].rearrange("p (a b) -> p a b", a=2), ALU.mult), g)
                dve.wait_ge(freed[g % NGRP], g // NGRP + 1)
                g = use[("mC", h)]
                wait_filled(dve, g)
                link(v.tensor_copy(nst[0:1, h], ps(g)[0:1, 1, 0:DK]))
                free(v.tensor_copy(Cst[:, h], ps(g)[:, 0, 0:DK]), g)
                dve.wait_ge(freed[g % NGRP], g // NGRP + 1)
                v.memset(sml[:, 10:11], 0.0).then_inc(for_pe, 1)
                settled(dve, for_pe)
            for s_ in range(STEPS):
                h, quarter = s_ // 4, s_ % 4
                c = ADA_EARLY + s_
                if s_ < 16:
                    scores(s_)
                if s_ >= 1:
                    select(ada, c - 2)
                if 1 <= s_ < 17:
                    weights(s_ - 1)
                if quarter == 0 and 1 <= h <= H:
                    head_end(h - 1)
                if s_ >= 2:
                    outputs(s_ - 2)
                if s_ < 16:
                    decayed(s_)
                    if quarter == 3:
                        state_keys(h)
                modulation_rows(ada, c)
            lo(ada.c0 + ada.n + 1)
            v.memset(sml[:, 10:11], 0.0).then_inc(for_store, 1)
            settled(dve, for_store)
            v.memset(sml[:, 10:11], 0.0).then_inc(region_q, 1)
            settled(dve, region_q)
            v.memset(sml[:, 10:11], 0.0).then_inc(for_store, 1)
            settled(dve, for_store)
            select(ada, 22)
            select(ada, 23)
            for i, key in enumerate(("stokA", "stokB")):
                g = use[key]
                wait_filled(dve, g)
                free(v.tensor_copy(stok[0:NS, i * 1024:(i + 1) * 1024], ps(g)[0:NS].rearrange("p a b -> p (a b)")), g)
                dve.wait_ge(freed[g % NGRP], g // NGRP + 1)
                v.memset(sml[:, 10:11], 0.0).then_inc(for_store, 1)
                settled(dve, for_store)
            modulation_sums(1)
            dve.wait_ge(tok_hi, 2)
            v.tensor_tensor(stoks[0:NS, 1].rearrange("p (a c) -> p a c", a=2),
                            stok[0:NS].rearrange("p (a c) -> p a c", c=512)[:, 0:4:3],
                            stoks[0:NS, 0].bitcast(F32).rearrange("p (a c) -> p a c", a=2), ALU.subtract).then_inc(tok_lo, 1)
            settled(dve, tok_lo)
            for b in range(NS):
                g = use[("qb", b)]
                wait_filled(dve, g)
                dve.wait_ge(past_k[b % 2], 32 * (b // 2 + 1))
                dve.wait_ge(kq_ready, 2 * b + 2)
                free(v.tensor_tensor(Kp[b % 2][:], Kp[b % 2][:], ps(g)[:, 0:1, :].broadcast_to([P, NPG, 512]), ALU.mult), g)
                dve.wait_ge(freed[g % NGRP], g // NGRP + 1)
                v.tensor_reduce(Sc[:, :, b * 8:(b + 1) * 8], Kp[b % 2][:].rearrange("p g (r d) -> p g r d", d=DK), AX.X,
                                ALU.add).then_inc(k_used, 1)
                settled(dve, k_used)
            dve.wait_ge(region_p, 1)
            dve.wait_ge(state_n_loaded, 16)
            link(v.tensor_tensor(np8[0:NS, 256:512], stok[0:NS, 0:256], stok[0:NS, 512:768], ALU.mult))
            link(v.tensor_reduce(sm8[0:NS, 40:44], np8[0:NS, 256:512].rearrange("p (r d) -> p r d", d=DK), AX.X, ALU.add))
            link(v.tensor_tensor(np8[0:NS, 256:512], stok[0:NS, 256:512], stok[0:NS, 768:1024], ALU.mult))
            link(v.tensor_reduce(sm8[0:NS, 44:48], np8[0:NS, 256:512].rearrange("p (r d) -> p r d", d=DK), AX.X, ALU.add))
            sel8 = cn[0:NS, C_SEL:C_SEL + 1024].rearrange("p (b m) -> p b m", b=8)
            link(v.tensor_tensor(s8[0:NS, 0:64].rearrange("p (b r) -> p b r", b=8), sel8[:, :, 0:8],
                                 sm8[0:NS, 40:48].unsqueeze(1).broadcast_to([NS, 8, 8]), ALU.mult))
            v.scalar_tensor_tensor(Comb[0:64], cn[0:64, C_COMB + 32:C_COMB + 64], neglam[0:64, 0:1],
                                   cn[0:64, C_COMB:C_COMB + 32], ALU.mult, ALU.add).then_inc(for_pe, 1)
            settled(dve, for_pe)
            g = use["st"]
            wait_filled(dve, g)
            link(v.tensor_copy(Pq[0:64, 256:257], ps(g)[0:64, 1, 0:1]))
            free(v.scalar_tensor_tensor(Pq[0:64, 0:256], cn[0:64, C_DROW:C_DROW + 256], cn[0:64, C_SLOPE:C_SLOPE + 1],
                                        ps(g)[0:64, 0, 0:256], ALU.mult, ALU.add), g)
            dve.wait_ge(freed[g % NGRP], g // NGRP + 1)
            dve.wait_ge(freed[g % NGRP], g // NGRP + 1)
            link(v.tensor_reduce(t32[0:64, 0, 2:3], Pq[0:64], AX.X, ALU.max))
            v.tensor_scalar(t32[0:64, 0, 0:1], t32[0:64, 0, 2:3], -1.0, None, ALU.mult).then_inc(dve_q, 1)
            settled(dve, dve_q)
            dve.wait_ge(act_q, 8)
            link(v.reciprocal(t32[0:64, 0, 3:4], t32[0:64, 0, 1:2]))
            v.tensor_scalar(Pq[0:64], Pq[0:64], t32[0:64, 0, 3:4], None, ALU.mult).then_inc(for_pe, 1)
            settled(dve, for_pe)
            g = use["wT"]
            wait_filled(dve, g)
            v.tensor_copy(wTs[:], ps(g)[:, 0, 0:96].rearrange("p (a b) -> p a b", a=3)).then_inc(for_pe, 1)
            settled(dve, for_pe)
            dve.wait_ge(for_pe, 10)
            free(v.tensor_copy(sml[0:1, 11:12], ps(g)[0:1, 0, 0:1]), g)
            dve.wait_ge(freed[g % NGRP], g // NGRP + 1)
            dve.wait_ge(cq_ready, NS)
            link(v.tensor_reduce(CqS[:], qbc[:].rearrange("p b (h k) -> p b h k", h=H), AX.X, ALU.add))
            ig, lf = gst[0:NS, 0:4], gst[0:NS, 4:8]
            link(v.tensor_tensor(sm8[0:NS, 4:8], lf, mpv[0:NS], ALU.add))
            link(v.tensor_tensor(sm8[0:NS, 0:4], sm8[0:NS, 4:8], ig, ALU.max))
            link(v.tensor_tensor(sm8[0:NS, 16:20], ig, sm8[0:NS, 0:4], ALU.subtract))
            v.tensor_tensor(sm8[0:NS, 20:24], sm8[0:NS, 4:8], sm8[0:NS, 0:4], ALU.subtract).then_inc(dve_q, 1)
            settled(dve, dve_q)
            q_, k_ = stok[0:NS, 1536:1792], stok[0:NS, 1792:2048]
            link(v.tensor_tensor(np8[0:NS, 256:512], q_, k_, ALU.mult))
            link(v.tensor_reduce(sm8[0:NS, 28:32], np8[0:NS, 256:512].rearrange("p (h k) -> p h k", h=H), AX.X, ALU.add))
            link(v.tensor_tensor(np8[0:NS, 256:512], q_, np8[0:NS, 0:256], ALU.mult))
            link(v.tensor_reduce(sm8[0:NS, 32:36], np8[0:NS, 256:512].rearrange("p (h k) -> p h k", h=H), AX.X, ALU.add))
            dve.wait_ge(act_q, 10)
            w8, g8 = sm8[0:NS, 16:20], sm8[0:NS, 20:24]
            link(v.tensor_tensor(sm8[0:NS, 48:52], sm8[0:NS, 28:32], w8, ALU.mult))
            link(v.tensor_tensor(sm8[0:NS, 52:56], sm8[0:NS, 32:36], g8, ALU.mult))
            link(v.tensor_tensor(sm8[0:NS, 56:60], sm8[0:NS, 48:52], sm8[0:NS, 52:56], ALU.add))
            link(v.scalar_tensor_tensor(sm8[0:NS, 60:64], sm8[0:NS, 56:60], -1.0, sm8[0:NS, 24:28], ALU.mult, ALU.max))
            link(v.tensor_tensor(sm8[0:NS, 56:60], sm8[0:NS, 56:60], sm8[0:NS, 60:64], ALU.max))
            link(v.reciprocal(sm8[0:NS, 56:60], sm8[0:NS, 56:60]))
            pack = sm8[0:NS, 64:80]
            link(v.tensor_copy(pack[:, 0:4], g8))
            link(v.tensor_copy(pack[:, 4:8], w8))
            link(v.tensor_tensor(pack[:, 8:12], sm8[0:NS, 48:52], sm8[0:NS, 56:60], ALU.mult))
            link(v.tensor_tensor(pack[:, 12:16], g8, sm8[0:NS, 56:60], ALU.mult))
            bc = lambda x: x.unsqueeze(2).broadcast_to([NS, H, DK])
            hk = lambda x: x.rearrange("p (h k) -> p h k", h=H)
            link(v.tensor_tensor(hk(np8[0:NS, 256:512]), hk(np8[0:NS, 0:256]), bc(g8), ALU.mult))
            link(v.tensor_tensor(hk(np8[0:NS, 0:256]), hk(k_), bc(w8), ALU.mult))
            link(v.tensor_tensor(np8[0:NS, 256:512], np8[0:NS, 256:512], np8[0:NS, 0:256], ALU.add))
            v.memset(sml[:, 10:11], 0.0).then_inc(for_store, 1)
            settled(dve, for_store)
            v.memset(sml[:, 10:11], 0.0).then_inc(for_pe, 1)
            settled(dve, for_pe)
            def hb_view(x):
                return x.rearrange("p (b h) -> p h b", h=H)
            vnew = smp[:, 8:12]
            link(v.tensor_tensor(t32[:, 0].rearrange("p (h b) -> p h b", h=H), vnew, hb_view(wTs[:, 2]), ALU.mult))
            g = use["rms"]
            dve.wait_ge(freed[g % NGRP], g // NGRP + 1)
            link(v.reciprocal(tok(rmb[1][0:8]), tok(rmb[0][0:8])))
            g = use["pvs"]
            wait_filled(dve, g)
            link(v.tensor_tensor(t32[:, 1].rearrange("p (h b) -> p h b", h=H), hb_view(ps(g)[:, 0, 0:32]),
                                 t32[:, 0].rearrange("p (h b) -> p h b", h=H), ALU.add))
            free(v.tensor_copy(sml[0:1, 11:12], ps(g)[0:1, 0, 0:1]), g)
            dve.wait_ge(freed[g % NGRP], g // NGRP + 1)
            link(v.tensor_copy(proj[:, 0:4, :, HALF:HT], t32[:, 1].rearrange("p (h a b) -> p h a b", h=H, a=2)))
            g = use["pk"]
            wait_filled(dve, g)
            free(v.tensor_copy(pks[:], ps(g)[:, 0, 0:128].rearrange("p (b r) -> p b r", b=NS)), g)
            dve.wait_ge(freed[g % NGRP], g // NGRP + 1)
            dve.wait_ge(freed[g % NGRP], g // NGRP + 1)
            bv = smp[:, 16:20].rearrange("p h b -> p b h")
            tt = t32[:].rearrange("p a (b h) -> p a b h", h=H)
            link(v.tensor_tensor(tt[:, 0], bv, pks[:, :, 8:12], ALU.mult))
            link(v.tensor_tensor(tt[:, 1], CqS[:], pks[:, :, 12:16], ALU.mult))
            link(v.tensor_tensor(tt[:, 0], tt[:, 0], tt[:, 1], ALU.add))
            for hf in range(2):
                link(v.tensor_copy(proj[:, 16:20, hf, HALF:HT], tt[:, 0, hf * HS:(hf + 1) * HS].rearrange("p b h -> p h b")))
            v.memset(sml[:, 10:11], 0.0).then_inc(for_pe, 1)
            settled(dve, for_pe)
            link(v.tensor_tensor(cfac[:, 0].rearrange("p (b h) -> p b h", h=H), bv, pks[:, :, 4:8], ALU.mult))
            v.tensor_copy(cfac[:, 1].rearrange("p (b h) -> p b h", h=H), pks[:, :, 0:4]).then_inc(for_store, 1)
            settled(dve, for_store)
            g = use["rmsS"]
            dve.wait_ge(freed[g % NGRP], g // NGRP + 1)
            v.reciprocal(smpl(rmb[1][0:8]), smpl(rmb[0][0:8])).then_inc(rr_ready, 1)
            settled(dve, rr_ready)
            dve.wait_ge(rr_hi, 1)
            v.tensor_tensor(rrl[0:8], rmb[1][0:8], rrh[0:8].bitcast(F32), ALU.subtract).then_inc(rr_ready, 1)
            settled(dve, rr_ready)

            def low_mixed(t):
                dve.wait_ge(mix_hi, t + 1)
                v.tensor_tensor(ML[:, t], mxb[t % 2][:], MH[:, t].bitcast(F32), ALU.subtract).then_inc(mix_lo, 1)
                settled(dve, mix_lo)
            for t in range(8):
                g = use[("rb", t)]
                wait_filled(dve, g)
                src = proj[:, t] if t < 4 else proj[:, 12 + t]
                gain = gA[:, 0:1] if t < 4 else bT[:, 97 + t - 4:98 + t - 4]
                free(v.scalar_tensor_tensor(mxb[t % 2][:], src, gain, pT(g), ALU.mult, ALU.mult), g)
                dve.wait_ge(freed[g % NGRP], g // NGRP + 1)
                if t >= 4:
                    v.tensor_tensor(mxb[t % 2][:], mxb[t % 2][:], proj[:, 16 + t], ALU.mult).then_inc(mx_ready, 1)
                    settled(dve, mx_ready)
                if t >= 1:
                    low_mixed(t - 1)
            low_mixed(7)

        @block.vector
        def _(dve):
            link = chain(dve, dve_step)
            v = nc.vector

            def lo(c):
                if c >= n_chunks:
                    return
                s = chunk_stage[c]
                dve.wait_ge(hi_done, c + 1)
                if c == st["ada1"].c0 + st["ada1"].n + 1:
                    dve.wait_ge(lo_done, c)
                if s.name == "gate":
                    src = raw[c % NRAW][:, 0:64].rearrange("p (k g m) -> p k g m", k=8, g=2)
                    vh = whi[c % 2][:, 0:1024].rearrange("p (k g m) -> p k g m", k=8, m=32)[:, :, 0:2, 0:4]
                    vl = wlo[c % 2][:, 0:1024].rearrange("p (k g m) -> p k g m", k=8, m=32)[:, :, 0:2, 0:4]
                    ins = v.tensor_tensor(vl, src, vh.bitcast(F32), ALU.subtract)
                else:
                    f = chunk_floats(c)
                    ins = v.tensor_tensor(wlo[c % 2][:, 0:f], raw[c % NRAW][:, 0:f], whi[c % 2][:, 0:f].bitcast(F32),
                                          ALU.subtract)
                ins.then_inc(lo_done, 1)
                dve.wait_ge(lo_done, c + 1)

            g = use["tc"]
            wait_filled(dve, g)
            dve.wait_ge(c_hi, 1)
            link(v.tensor_tensor(cH[:, :, 9:18], ps(g)[:, 0, 0:72].rearrange("p (k c) -> p k c", c=9),
                                 cH[:, :, 0:9].bitcast(F32), ALU.subtract))
            free(v.tensor_copy(sml[0:1, 0:1], ps(g)[0:1, 0, 0:1]), g)
            dve.wait_ge(freed[g % NGRP], g // NGRP + 1)
            dve.wait_ge(freed[g % NGRP], g // NGRP + 1)
            v.memset(sml[:, 1:2], 0.0).then_inc(c_lo, 1)
            settled(dve, c_lo)
            g = use["tb"]
            wait_filled(dve, g)
            link(v.tensor_copy(bT[:], ps(g)[:, 0, 0:101]))
            free(v.tensor_scalar(gA[:], ps(g)[:, 0, 96:97], 1.0 - LAM_INIT, None, ALU.mult), g)
            dve.wait_ge(freed[g % NGRP], g // NGRP + 1)
            lo(0)
            lo(1)
            dve.wait_ge(memset_done, 3)

            def setup_dve():
                for tb in range(4):
                    g = use[("tx", tb)]
                    wait_filled(dve, g)
                    off = (tb % 2) * P
                    free(v.tensor_copy(xT[:, :, tb // 2, off:off + P], ps(g)[:].rearrange("p a (b c) -> p (a b) c", c=P)), g)
                    dve.wait_ge(freed[g % NGRP], g // NGRP + 1)
                g = use["ra"]
                wait_filled(dve, g)
                rv = ps(g)[:, 0, 0:128].rearrange("p (k r) -> p k r", r=16)
                for hf in range(2):
                    v.tensor_copy(xT[:, :, hf, HALF:HT], rv[:, :, hf * HS:(hf + 1) * HS])
                link(v.tensor_copy(lnT[:], rv[:, :, 8:16]))
                free(v.tensor_scalar(lnA[:], rv[:, :, 8:16], ALPHA, None, ALU.mult), g)
                dve.wait_ge(freed[g % NGRP], g // NGRP + 1)
                g = use["to"]
                wait_filled(dve, g)
                free(v.tensor_copy(OT[:], ps(g)[:, 0, 0:400].rearrange("p (k r) -> p k r", r=40)), g)
                dve.wait_ge(freed[g % NGRP], g // NGRP + 1)
                dve.wait_ge(freed[g % NGRP], g // NGRP + 1)

            def decay_and_lambda():
                lam_ = OT[:, :, 39]
                link(v.tensor_scalar(sp8[:, 0], lam_, -1.0, None, ALU.mult))
                v.tensor_tensor(sp8[:, 1], sp8[:, 0], lam_, ALU.max).then_inc(dve_q, 1)
                settled(dve, dve_q)
                dve.wait_ge(dve_q, 1)
                link(v.tensor_scalar(sp8[:, 0], sp8[:, 0], 0.0, None, ALU.max))
                link(v.tensor_tensor(lamr[0:1, 0:64], lamr[0:1, 0:64], lamr[0:1, 64:128], ALU.mult))
                link(v.tensor_tensor(lamr[0:1, 64:128], lamr[0:1, 128:192], lamr[0:1, 192:256], ALU.mult))
                v.tensor_reduce(lamr[0:1, 256:258], lamr[0:1, 0:128].rearrange("p (a b) -> p a b", a=2), AX.X,
                                ALU.add).then_inc(dve_q, 1)
                settled(dve, dve_q)
                dve.wait_ge(act_q, 3)
                link(v.tensor_tensor(sp8[:, 0], sp8[:, 0], sp8[:, 1], ALU.add))
                v.tensor_scalar(sp8[:, 2], sp8[:, 0], 8.0, None, ALU.mult)
                link(v.tensor_scalar(sp8[:, 3], sp8[:, 0], -8.0, None, ALU.mult))
                link(v.tensor_tensor(lamr[0:1, 260:261], lamr[0:1, 259:260], lamr[0:1, 258:259], ALU.subtract))
                v.tensor_scalar(neglr[0:1], lamr[0:1, 260:261], -LAM_INIT, None, ALU.add).then_inc(for_pe, 1)
                settled(dve, for_pe)

            def select(s, c):
                g = sel_use(s, c)
                l = int(s.name[3])
                wait_filled(dve, g)
                b = bT[:, l * 48 + 2 * c:l * 48 + 2 * c + 2].unsqueeze(2).broadcast_to([P, 2, 9])
                free(v.tensor_tensor(modT[l][:, 2 * c:2 * c + 2], ps(g)[:, 0, 0:18].rearrange("p (r c) -> p r c", c=9),
                                     b, ALU.add), g)
                dve.wait_ge(freed[g % NGRP], g // NGRP + 1)

            def modulation_rows(s, c):
                g = mod_use(s, c)
                wait_filled(dve, g)
                free(v.tensor_copy(modrow[0:18, c % 2], ps(g)[0:18, 0, 0:256]), g)
                dve.wait_ge(freed[g % NGRP], g // NGRP + 1)

            def modulation_sums(l):
                for j in range(2):
                    q = 2 * l + j
                    r = q - 1
                    sc, sh, gt = (modT[l][:, (3 * j + i) * 8:(3 * j + i + 1) * 8] for i in (1, 0, 2))
                    link(v.tensor_scalar(G9[:, q], sc, 1.0, None, ALU.add))
                    link(v.tensor_scalar(gt, gt, 1.0, None, ALU.add))
                    if r < 0:
                        link(v.tensor_copy(B9[:, q], sh))
                    else:
                        lb = lnT[:, :, 4 + r:5 + r].broadcast_to([P, KD, 9])
                        lg = lnT[:, :, r:r + 1].broadcast_to([P, KD, 9])
                        link(v.tensor_tensor(B9[:, q], G9[:, q], lb, ALU.mult))
                        link(v.tensor_tensor(B9[:, q], B9[:, q], sh, ALU.add))
                        link(v.tensor_tensor(G9[:, q], G9[:, q], lg, ALU.mult))
            for c in range(24):
                modulation_rows(st["ada0"], c)
                lo(c + 2)
                if c >= 1:
                    select(st["ada0"], c - 1)
            select(st["ada0"], 23)
            setup_dve()
            modulation_sums(0)

            def make_u(q):
                r = q - 1

                def low(t):
                    dve.wait_ge(uhi_ready, 8 * q + t + 1)
                    v.tensor_tensor(UL[:, t], ub[t % 2][:], UH[:, t].bitcast(F32), ALU.subtract).then_inc(ulo_ready, 1)
                    settled(dve, ulo_ready)
                for t in range(KD):
                    if r >= 0:
                        dve.wait_ge(d_ready, 8 * r + t + 1)
                        if t >= 2:
                            dve.wait_ge(x_ready, 8 * r + t - 1)
                        v.tensor_tensor(nb[t % 2][:], db[t % 2][:], rstd[:], ALU.mult).then_inc(n_ready, 1)
                        settled(dve, n_ready)
                        dve.wait_ge(n_ready, 8 * r + t + 1)
                        n = nb[t % 2]
                    else:
                        n = xT[:, t]
                    if q == 4:
                        continue
                    link(v.tensor_tensor(stmp[:], smpl(n), G9[:, q, t, 1:9].rearrange("p (a b) -> p a b", a=2), ALU.mult))
                    if r < 0 or t % 2 == 0:
                        v.tensor_scalar(tok(ub[t % 2]), tok(n), G9[:, q, t, 0:1], B9[:, q, t, 0:1], ALU.mult, ALU.add)
                    v.tensor_tensor(smpl(ub[t % 2]), stmp[:], B9[:, q, t, 1:9].rearrange("p (a b) -> p a b", a=2),
                                    ALU.add).then_inc(u_ready, 1)
                    settled(dve, u_ready)
                    if t >= 1:
                        low(t - 1)
                if q < 4:
                    low(KD - 1)
                if r < 0:
                    link(v.tensor_scalar(xT[:], xT[:], ALPHA, None, ALU.mult))

            def residual(r, t, g, last):
                gt = modT[r // 2][:, (3 * (r % 2) + 2) * 8 + t]
                x = xT[:, t]
                wait_filled(dve, g)
                link(v.tensor_tensor(stmp[:], ps(g)[:, :, HALF:HT], gt[:, 1:9].rearrange("p (a b) -> p a b", a=2), ALU.mult))
                free(v.scalar_tensor_tensor(tok(x), ps(g)[:, :, 0:HALF], gt[:, 0:1], tok(x), ALU.mult, ALU.add), g)
                dve.wait_ge(freed[g % NGRP], g // NGRP + 1)
                ins = v.tensor_tensor(smpl(x), stmp[:], smpl(x), ALU.add)
                if last:
                    ins.then_inc(z_ready, 1)
                    settled(dve, z_ready)
                else:
                    link(ins)

            def ln_stats(r, c):
                g = use[("lnm", r)]
                wait_filled(dve, g)
                free(v.tensor_copy(mu[:], pT(g)), g)
                dve.wait_ge(freed[g % NGRP], g // NGRP + 1)
                dve.wait_ge(freed[g % NGRP], g // NGRP + 1)
                v.tensor_tensor(tv[:], mu[:], mu[:], ALU.mult).then_inc(mu_ready, 1)
                settled(dve, mu_ready)
                dve.wait_ge(mu_ready, r + 1)
                g = use[("lnq", r)]
                wait_filled(dve, g)
                free(v.tensor_tensor(tv[:], pT(g), tv[:], ALU.subtract), g)
                dve.wait_ge(freed[g % NGRP], g // NGRP + 1)
                dve.wait_ge(freed[g % NGRP], g // NGRP + 1)
                link(v.tensor_scalar(tv[:], tv[:], 0.0, EPS, ALU.max, ALU.add))
                v.memset(sml[:, 3:4], 0.0).then_inc(var_ready, 1)
                settled(dve, var_ready)
                lo(c)
                dve.wait_ge(sd_ready, r + 1)
                link(v.reciprocal(rstd[:], tv[:]))

            def ffn(l):
                for hf in range(2):
                    s = st[f"fi{l}{hf}"]
                    for c in range(s.n):
                        k = (2 * l + hf) * KH + c
                        g = s.g0 + 2 * c + 1
                        wait_filled(dve, g)
                        dve.wait_ge(freed[(g - 1) % NGRP], (g - 1) // NGRP + 1)
                        v.tensor_tensor(hb[c % 2][:], pT(g), silb[c % 2][:], ALU.mult).then_inc(h_ready, 1)
                        settled(dve, h_ready)
                        dve.wait_ge(h_ready, k + 1)
                        free(v.tensor_copy(sml[0:1, 4:5], ps(g)[0:1, 0, 0:1]), g)
                        dve.wait_ge(freed[g % NGRP], g // NGRP + 1)
                        if c < s.n - 1:
                            lo(s.c0 + c + 2)
                        dve.wait_ge(hhi_ready, k + 1)
                        v.tensor_tensor(HL[:, c], hb[c % 2][:], HH[:, c].bitcast(F32), ALU.subtract).then_inc(hlo_ready, 1)
                        settled(dve, hlo_ready)
                    lo(s.c0 + s.n + 1)
                    s = st[f"fo{l}{hf}"]
                    for c in range(s.n):
                        residual(2 * l + 1, c, s.g0 + c, hf == 1)
                        if hf == 0 or c < s.n - 1:
                            lo(s.c0 + c + 2)
                ln_stats(2 * l + 1, s.c0 + s.n + 1)

            make_u(0)
            decay_and_lambda()
            s = st["ein"]
            for c in range(s.n):
                for m in range(2):
                    t, g = 2 * c + m, s.g0 + 2 * c + m
                    wait_filled(dve, g)
                    scale = 0.125 if t < 4 or 12 <= t < 14 else 1.0
                    free(v.tensor_scalar(proj[:, t], pT(g), scale, None, ALU.mult), g)
                    dve.wait_ge(freed[g % NGRP], g // NGRP + 1)
                dve.wait_ge(freed[g % NGRP], g // NGRP + 1)
                v.memset(sml[:, 5:6], 0.0).then_inc(evac, 2)
                settled(dve, evac, 2)
                lo(s.c0 + c + 2)
            lo(st["gate"].c0 + 2)
            g = use["lam"]
            wait_filled(dve, g)
            free(v.tensor_copy(neglam[:], ps(g)[:, 0, 0:1]), g)
            dve.wait_ge(freed[g % NGRP], g // NGRP + 1)
            middle_dve(dve, link, lo, modulation_rows, select, modulation_sums)
            s = st["eout"]
            for c in range(s.n):
                for m in range(2):
                    residual(0, 2 * c + m, s.g0 + 2 * c + m, True)
                if c < s.n - 1:
                    lo(s.c0 + c + 2)
            ln_stats(0, s.c0 + s.n + 1)
            make_u(1)
            ffn(0)
            make_u(2)
            def per_tile(col, n=NS):
                return OT[:, :, col:col + 1].broadcast_to([P, KR, n])
            link(v.tensor_tensor(tS[:, 0], OT[:, :, 0:24:3], per_tile(32), ALU.mult))
            for j in range(1, 3):
                link(v.tensor_tensor(tS[:, 1], OT[:, :, j:24:3], per_tile(32 + j), ALU.mult))
                link(v.tensor_tensor(tS[:, 0], tS[:, 0], tS[:, 1], ALU.add))

            s = st["oinx"]
            for c in range(s.n):
                for m in range(2):
                    t = 2 * c + m
                    g = s.g0 + t
                    dve.wait_ge(cv0, t + 1)
                    free(v.tensor_copy(xrS[:, t].rearrange("p (a b) -> p a b", a=2), ps(g)[:, :, HALF:HT]), g)
                    dve.wait_ge(freed[g % NGRP], g // NGRP + 1)
                    link(v.tensor_tensor(smpl(xc[:, t]), smpl(xc[:, t]), tS[:, 0, t].rearrange("p (a b) -> p a b", a=2), ALU.add))
                    for j in range(3):
                        ins = v.scalar_tensor_tensor(tok(xc[:, t]), xr[:, t, j:j + SEQ].rearrange("p (a b) -> p a b", a=2),
                                                     OT[:, t, 32 + j:33 + j], tok(xc[:, t]), ALU.mult, ALU.add)
                        if j < 2:
                            link(ins)
                    ins.then_inc(cv_ready, 1)
                    settled(dve, cv_ready)
                lo(s.c0 + c + 2)
            link(v.tensor_copy(OS[:, :, 0:3], xr[:, :, SEQ:SEQ + 3]))
            v.tensor_copy(OS[:, :, 3:11], xrS[:]).then_inc(for_store, 1)
            settled(dve, for_store)
            for b in range(st["wax"].n):
                lo(st["wax"].c0 + b + 2)
            s = st["oing"]
            for t in range(KR):
                dve.wait_ge(a_ready, t + 1)
                v.scalar_tensor_tensor(qT[:, t], asq[t % 2][:], 1.0, qT[:, t], ALU.add, ALU.mult).then_inc(q_ready, 1)
                settled(dve, q_ready)
                if t in (0, 2, 5, 7):
                    tg = (0, 2, 5, 7).index(t)
                    g = s.g0 + tg
                    wait_filled(dve, g)
                    if tg == 2:
                        dve.wait_ge(ix_ready, KR)
                    free(v.tensor_copy(gate_buf(tg)[:], pT(g)), g)
                    dve.wait_ge(freed[g % NGRP], g // NGRP + 1)
                if t == 5:
                    lo(s.c0 + 2)
            for t in range(KR):
                dve.wait_ge(sqrt_ready, t + 1)
                link(v.tensor_tensor(qT[:, t], qT[:, t], xc[:, t], ALU.mult))
                link(v.tensor_tensor(stmp[:], smpl(aT[:, t]), OT[:, t, 24:32].rearrange("p (a b) -> p a b", a=2), ALU.mult))
                link(v.tensor_tensor_scan(xc[:, t, 0, 0:HALF], aT[:, t, 0, 0:HALF], qT[:, t, 0, 0:HALF], 0.0, ALU.mult, ALU.add))
                link(v.tensor_tensor_scan(xc[:, t, 1, 0:HALF], aT[:, t, 1, 0:HALF], qT[:, t, 1, 0:HALF],
                                          xc[:, t, 0, HALF - 1:HALF], ALU.mult, ALU.add))
                link(v.tensor_tensor(smpl(xc[:, t]), stmp[:], smpl(qT[:, t]), ALU.add))
                link(v.tensor_copy(OS[:, t, 11:12], xc[:, t, 1, HALF - 1:HALF]))
                v.tensor_copy(OS[:, t, 12:20].rearrange("p (a b) -> p a b", a=2), smpl(xc[:, t])).then_inc(hs_ready, 1)
                settled(dve, hs_ready)
                if t in (1, 5, 8):
                    lo(s.c0 + {1: 3, 5: 4, 8: 5}[t])
            for t in range(KR):
                if t == 7:
                    lo(s.c0 + 6)
                dve.wait_ge(yhi_ready, t + 1)
                v.tensor_tensor(YL[:, t], xc[:, t], YH[:, t].bitcast(F32), ALU.subtract).then_inc(ylo_ready, 1)
                settled(dve, ylo_ready)
            for i, key in enumerate(("osA", "osB")):
                g = use[key]
                wait_filled(dve, g)
                n = 1024 if i == 0 else 256
                ins = v.tensor_copy(OST[0:20, i * 1024:i * 1024 + n], ps(g)[0:20].rearrange("p a b -> p (a b)")[:, 0:n])
                free(ins, g)
                dve.wait_ge(freed[g % NGRP], g // NGRP + 1)
                dve.wait_ge(freed[g % NGRP], g // NGRP + 1)
                v.memset(sml[:, 7:8], 0.0).then_inc(out_ready, 1)
                settled(dve, out_ready)
            s = st["oout"]
            for c in range(s.n):
                residual(2, c, s.g0 + c, True)
                if c < s.n - 1:
                    lo(s.c0 + c + 2)
            ln_stats(2, s.c0 + s.n + 1)
            make_u(3)
            ffn(1)
            make_u(4)
            dve.wait_ge(x_ready, 32)
            v.tensor_copy(xsm[:].rearrange("p k (a b) -> p k a b", a=2), xT[:, :, :, HALF:HT]).then_inc(for_pe, 1)
            settled(dve, for_pe)
            for tb in range(4):
                g = use[("ty", tb)]
                wait_filled(dve, g)
                free(v.tensor_copy(ytok[tb][:], ps(g)[:].rearrange("p a b -> p (a b)")), g)
                dve.wait_ge(freed[g % NGRP], g // NGRP + 1)
                dve.wait_ge(freed[g % NGRP], g // NGRP + 1)
                v.memset(sml[:, 7:8], 0.0).then_inc(out_ready, 1)
                settled(dve, out_ready)
            g = use["tys"]
            wait_filled(dve, g)
            v.tensor_copy(ysamp[0:NS], ps(g)[0:NS].rearrange("p a b -> p (a b)")).then_inc(out_ready, 1)
            settled(dve, out_ready)

        def middle_pe(pe, begin, done, mod_products, mod_select):
            T = nc.tensor

            def blk(t, tb, lo_=0, hi_=P):
                return proj[lo_:hi_, t, tb // 2, (tb % 2) * P:(tb % 2 + 1) * P]
            begin(use["lam"])
            pe.wait_ge(for_pe, 1)
            done(T.matmul(ps(use["lam"])[:, 0, 0:1], ones[0:1, :], neglr[0:1], start=True, stop=True))
            pe.wait_ge(evac, 24)
            ada = st["ada1"]
            for tb in range(4):
                g = use[("kv", tb)]
                begin(g)
                for i in range(8):
                    ins = T.transpose(ps(g)[:, i // 4, (i % 4) * P:(i % 4 + 1) * P], blk(4 + i, tb), ident)
                done(ins)
                mod_products(ada, tb)
                if tb >= 1:
                    mod_select(ada, tb - 1)
            for tb in range(4):
                g = use[("bkv", tb)]
                begin(g)
                for i in range(4):
                    T.transpose(ps(g)[:, 0, i * P:(i + 1) * P], blk(16 + i, tb), ident)
                for i in range(2):
                    ins = T.transpose(ps(g)[:, 1, i * P:(i + 1) * P], blk(14 + i, tb), ident)
                done(ins)
                if tb < ADA_EARLY - 4:
                    mod_products(ada, 4 + tb)
                    mod_select(ada, 3 + tb)
            pe.wait_ge(for_pe, 3)
            g = use["acol"]
            begin(g)
            for tb in range(4):
                ins = T.transpose(ps(g)[:, 0, 4 * tb:4 * tb + 4], rows[0:4, 4, tb // 2, (tb % 2) * P:(tb % 2 + 1) * P], ident[0:4, 0:4])
            done(ins)
            g = use["gs"]
            begin(g)
            T.transpose(ps(g)[0:NS, 0, 0:4], rows[0:4, 5, 0, 0:8], ident[0:4, 0:4])
            done(T.transpose(ps(g)[0:NS, 0, 4:8], rows[0:4, 5, 0, 8:16], ident[0:4, 0:4]))

            def head_rows(h):
                g = use[("bc", h)]
                begin(g)
                sel = cn[0:4, C_SEL + h * P:C_SEL + (h + 1) * P]
                for j in range(2):
                    ins = T.matmul(ps(g)[:, j], sel, rowc[0:4, j], start=True, stop=True)
                done(ins)

            def head_scores(h, s_):
                p0 = 64 * (h % 2)
                g = use[("mS", h, s_)]
                begin(g)
                kT = blk(14 + h // 2, s_, p0, p0 + 64)
                n = 0
                for tb in range(s_, 4):
                    ins = T.matmul(ps(g)[:, 0, n:n + P], kT, blk(12 + h // 2, tb, p0, p0 + 64), start=True, stop=True)
                    n += P
                done(ins)

            def head_sums(h):
                g = use[("mN", h)]
                begin(g)
                for s_ in range(4):
                    gs = use[("mS", h, s_)]
                    pe.wait_ge(freed[gs % NGRP], gs // NGRP + 1)
                for s_ in range(4):
                    n = SEQ - s_ * P
                    T.matmul(ps(g)[:, 0, s_ * P:SEQ], bkv[:, s_, h * DV:(h + 1) * DV], PT[s_][:, 0:n], start=(s_ == 0),
                             stop=(s_ == 3), skip_group_check=True)
                for s_ in range(4):
                    n = SEQ - s_ * P
                    ins = T.matmul(ps(g)[:, 1, s_ * P:SEQ], ones[:], PT[s_][:, 0:n], start=(s_ == 0), stop=(s_ == 3),
                                   skip_group_check=True)
                done(ins)
                g = use[("mC", h)]
                begin(g)
                pe.wait_ge(pt_ready, h + 1)
                for s_ in range(4):
                    T.matmul(ps(g)[:, 0, 0:DK], bkv[:, s_, h * DV:(h + 1) * DV], kw[:, s_], start=(s_ == 0), stop=(s_ == 3))
                for s_ in range(4):
                    ins = T.matmul(ps(g)[0:1, 1, 0:DK], wl[:, s_:s_ + 1], bkv[:, s_, 512 + h * DK:512 + (h + 1) * DK],
                                   start=(s_ == 0), stop=(s_ == 3))
                done(ins)

            def scores(u):
                h, i = u // 4, u % 4
                g = use[("S", u)]
                begin(g)
                for j in range(2):
                    q = blk(h, i, 64 * j, 64 * j + 64)
                    for hf in range(i // 2 + 1):
                        n = HALF if hf < i // 2 or i % 2 else P
                        ins = T.matmul(ps(g)[:, j, hf * HALF:hf * HALF + n], q, proj[64 * j:64 * j + 64, 4 + h, hf, 0:n],
                                       start=True, stop=True)
                done(ins)

            def transposes(u):
                g = use[("T", u)]
                begin(g)
                pe.wait_ge(w_ready, u + 1)
                for kb in range(u % 4 + 1):
                    ins = T.transpose(ps(g)[:, 0, kb * P:(kb + 1) * P], Wb[u % 2][:, kb * P:(kb + 1) * P], ident)
                done(ins)

            def pv(u):
                h, i = u // 4, u % 4
                g = use[("PV", u)]
                begin(g)
                gt = use[("T", u)]
                pe.wait_ge(freed[gt % NGRP], gt // NGRP + 1)
                for kb in range(i + 1):
                    ins = T.matmul(ps(g)[:, 0, 0:P], vtok[:, kb, h * DV:(h + 1) * DV], wTb[u % 2][:, kb * P:(kb + 1) * P],
                                   start=(kb == 0), stop=(kb == i))
                done(ins)
            scores(0)
            for s_ in range(STEPS):
                h, quarter = s_ // 4, s_ % 4
                if quarter == 0 and 1 <= h <= H:
                    head_sums(h - 1)
                if s_ < 16:
                    if quarter == 0:
                        head_rows(h)
                    head_scores(h, quarter)
                if s_ >= 2:
                    pv(s_ - 2)
                mod_products(ada, ADA_EARLY + s_)
                if s_ < 15:
                    scores(s_ + 1)
                if 1 <= s_ < 17:
                    transposes(s_ - 1)
                mod_select(ada, ADA_EARLY + s_ - 1)
            mod_select(ada, 23)
            pe.wait_ge(for_store, 3)
            for key, tiles in (("stokA", list(range(8))), ("stokB", [8, 9, 10, 11, 12, 13, 14, 15])):
                g = use[key]
                begin(g)
                for i, t in enumerate(tiles):
                    ins = T.transpose(ps(g)[0:NS, i // 4, (i % 4) * P:(i % 4 + 1) * P], smp[:, t], ident)
                done(ins)
            pe.wait_ge(for_store, 5)
            pe.wait_ge(tok_lo, 1)
            for b in range(NS):
                g = use[("qb", b)]
                begin(g)
                for j in range(2):
                    for i in range(2):
                        ins = T.matmul(ps(g)[:, j], selr[0:NS, b * P:(b + 1) * P], stoks[0:NS, i, j * 512:(j + 1) * 512],
                                       start=(i == 0), stop=(i == 1))
                done(ins)
            g = use["rms"]
            begin(g)
            for t in range(8):
                pe.wait_ge(rm_sq, t + 1)
                for hf in range(2):
                    ins = T.matmul(ps(g)[0:8, hf, 0:HALF], cn[:, C_SELV + 8 * t:C_SELV + 8 * t + 8], rsq[t % 2][:, hf, 0:HALF],
                                   start=(t == 0), stop=(t == 7))
                if t < 7:
                    ins.then_inc(rsq_used, 1)
            done(ins)
            g = use["st"]
            begin(g)
            pe.wait_ge(for_pe, 8)
            for pg in range(NPG):
                T.transpose(ps(g)[0:64, 0, pg * P:(pg + 1) * P], Sc[:, pg], ident)
            done(T.matmul(ps(g)[0:64, 1, 0:1], s8[0:NS, 0:64], ones[0:NS, 0:1], start=True, stop=True))
            g = use["wT"]
            begin(g)
            pe.wait_ge(for_pe, 9)
            for pg in range(NPG):
                T.matmul(ps(g)[:, 0, pg * 32:(pg + 1) * 32], Pq[0:64, pg * P:(pg + 1) * P], Comb[0:64], start=True, stop=True)
            done(T.matmul(ps(g)[:, 0, 64:96], Pq[0:64, 256:257].broadcast_to([64, P]), Comb[0:64], start=True, stop=True))
            g = use["pvs"]
            begin(g)
            pe.wait_ge(for_pe, 10)
            for b in range(NS):
                pe.wait_ge(past_v[b], 32)
                for h in range(H):
                    for pg in range(NPG):
                        col = 4 * b + h
                        ins = T.matmul(ps(g)[:, 0, col:col + 1], Vp[b][:, pg, h * DV:(h + 1) * DV], wTs[:, pg, col:col + 1],
                                       start=(pg == 0), stop=(pg == NPG - 1))
            done(ins)
            g = use["pk"]
            begin(g)
            pe.wait_ge(for_pe, 11)
            for b in range(NS):
                ins = T.matmul(ps(g)[:, 0, 16 * b:16 * b + 16], cn[0:NS, C_SEL + b * P:C_SEL + (b + 1) * P], sm8[0:NS, 64:80],
                               start=True, stop=True)
            done(ins)
            g = use["rmsS"]
            begin(g)
            pe.wait_ge(rm_sq, 9)
            for t in range(8):
                for hf in range(2):
                    ins = T.matmul(ps(g)[0:8, hf, 0:HS], cn[:, C_SELV + 8 * t:C_SELV + 8 * t + 8], rsS[:, t, hf],
                                   start=(t == 0), stop=(t == 7))
            done(ins)
            pe.wait_ge(rr_ready, 2)
            for t in range(8):
                g = use[("rb", t)]
                begin(g)
                for hf in range(2):
                    for r in (rrh, rrl):
                        ins = T.matmul(ps(g)[:, hf, 0:HT], selr[0:8, t * P:(t + 1) * P], r[0:8, hf],
                                       start=(r is rrh), stop=(r is rrl))
                done(ins)

        @block.tensor
        def _(pe):
            T = nc.tensor

            def begin(g, it=None, per=0):
                if g >= NGRP:
                    pe.wait_ge(freed[g % NGRP], g // NGRP if it is None else g // NGRP + it * per)

            def done(ins):
                ins.then_inc(filled, 1)

            def products(s, c, xh, xl, it=None):
                gc = s.c0 + c
                pe.wait_ge(lo_done, gc + 1 if it is None else gc + 1 + it * NRAW)
                wh = whi[gc % 2][:, 0:s.k * s.m].rearrange("p (k m) -> p k m", m=s.m)
                wl_ = wlo[gc % 2][:, 0:s.k * s.m].rearrange("p (k m) -> p k m", m=s.m)
                for m in range(s.uses):
                    g = s.g0 + c * s.uses + m
                    begin(g, it, s.uses * NRAW // NGRP)
                    for k in range(s.k):
                        wc = slice(m * P, (m + 1) * P)
                        for w, x in ((wh, xh), (wh, xl), (wl_, xh)):
                            for hf in range(2):
                                ins = T.matmul(ps(g)[:, hf, 0:HT], w[:, k, wc], x[:, k, hf], start=(k == 0 and w is wh and x is xh),
                                               stop=(k == s.k - 1 and w is wl_))
                    done(ins)

            def gemm(name, xh, xl, ready, n_ready):
                s = st[name]
                slot = s.c0 % 2
                for m in range(s.uses):
                    begin(s.g0 + m)
                pe.wait_ge(lo_done, s.c0 + 1)
                for k in range(s.k):
                    pe.wait_ge(ready, n_ready + k + 1)
                    for m in range(s.uses):
                        g = s.g0 + m
                        wc = slice(k * s.m + m * P, k * s.m + (m + 1) * P)
                        for w, x in ((whi, xh), (whi, xl), (wlo, xh)):
                            for hf in range(2):
                                ins = T.matmul(ps(g)[:, hf, 0:HT], w[slot][:, wc], x[:, k, hf],
                                               start=(k == 0 and w is whi and x is xh), stop=(k == s.k - 1 and w is wlo))
                        if k == s.k - 1:
                            done(ins)
                bodies = (s.n - 1) // NRAW
                c0 = 1
                if bodies > 1:
                    with pe.Fori(0, bodies) as it:
                        for c in range(c0, c0 + NRAW):
                            products(s, c, xh, xl, it)
                    c0 += bodies * NRAW
                for c in range(c0, s.n):
                    products(s, c, xh, xl)

            pe.wait_ge(consts_loaded, 16)
            pe.wait_ge(memset_done, 3)

            def rows_to_cols(g, src, n, cols, off=0):
                for k in range(cols):
                    ins = T.transpose(ps(g)[:, 0, off + k * n:off + (k + 1) * n], src[0:n, k * P:(k + 1) * P], ident[0:n, 0:n])
                return ins
            pe.wait_ge(silu_c, 1)
            begin(use["tc"])
            done(rows_to_cols(use["tc"], CR, 9, KD))
            begin(use["tb"])
            rows_to_cols(use["tb"], BR, 96, 1)
            done(rows_to_cols(use["tb"], NR, 5, 1, 96))

            def setup_pe():
                pe.wait_ge(x_loaded, 16)
                for tb in range(4):
                    g = use[("tx", tb)]
                    begin(g)
                    for k in range(KD):
                        ins = T.transpose(ps(g)[:].rearrange("p a (b c) -> p (a b) c", c=P)[:, k],
                                          xtok[:, tb, k * P:(k + 1) * P], ident)
                    done(ins)
                pe.wait_ge(small_loaded, 16 * N_SMALL)
                begin(use["ra"])
                done(rows_to_cols(use["ra"], RA, 16, KD))
                begin(use["to"])
                done(rows_to_cols(use["to"], RO, 40, KR))

            def mod_products(s, c, it=None):
                gc = s.c0 + c
                pe.wait_ge(lo_done, gc + 1 if it is None else gc + 1 + it * NRAW)
                g = mod_use(s, c)
                begin(g, it, 2)
                for k in range(KD):
                    for w in (whi, wlo):
                        ins = T.matmul(ps(g)[0:18, 0, 0:256], cH[:, k], w[gc % 2][:, k * 256:(k + 1) * 256],
                                       start=(k == 0 and w is whi), stop=(k == KD - 1 and w is wlo))
                done(ins)

            def mod_select(s, c, it=None):
                g = sel_use(s, c)
                begin(g, it, 2)
                gm = mod_use(s, c)
                pe.wait_ge(freed[gm % NGRP], gm // NGRP + 1 if it is None else gm // NGRP + 1 + it * 2)
                for k in range(2):
                    ins = T.matmul(ps(g)[:, 0, k * 9:(k + 1) * 9], modrow[0:18, c % 2, k * P:(k + 1) * P],
                                   cn[0:18, C_ADA:C_ADA + 9], start=True, stop=True)
                done(ins)
            pe.wait_ge(c_lo, 1)
            s = st["ada0"]
            for c in range(NRAW):
                mod_products(s, c)
                if c >= 1:
                    mod_select(s, c - 1)
            with pe.Fori(0, s.n // NRAW - 1) as it:
                for c in range(NRAW, 2 * NRAW):
                    mod_products(s, c, it)
                    mod_select(s, c - 1, it)
            mod_select(s, s.n - 1)
            setup_pe()

            gemm("ein", UH, UL, ulo_ready, 0)
            products(st["gate"], 0, UH, UL)
            middle_pe(pe, begin, done, mod_products, mod_select)
            gemm("eout", MH, ML, mix_lo, 0)

            def ln_sums(r):
                both = (("lnm", accS, xT[:, KD - 1], z_ready, 13), ("lnq", accQ, sqb[(KD - 1) % 2], sq_ready, 14))
                for key, acc, _, _, n in both:
                    g = use[(key, r)]
                    begin(g)
                    pe.wait_ge(acc_step, 14 * r + n)
                    for hf in range(2):
                        T.matmul(ps(g)[:, hf, 0:HT], onesD[:], acc[:, hf], start=True, stop=False, skip_group_check=True)
                for key, _, last, ready, _ in both:
                    g = use[(key, r)]
                    pe.wait_ge(ready, 8 * r + 8)
                    for hf in range(2):
                        ins = T.matmul(ps(g)[:, hf, 0:HT], onesD[:], last[:, hf], start=False, stop=True, skip_group_check=True)
                    done(ins)

            def ffn(l):
                for hf in range(2):
                    gemm(f"fi{l}{hf}", UH, UL, ulo_ready, 8 * (2 * l + 1))
                    gemm(f"fo{l}{hf}", HH, HL, hlo_ready, (2 * l + hf) * KH)
                ln_sums(2 * l + 1)
            ln_sums(0)
            ffn(0)
            gemm("oinx", UH, UL, ulo_ready, 16)
            s = st["wax"]
            for b in range(s.n):
                gc = s.c0 + b
                pe.wait_ge(lo_done, gc + 1)
                pe.wait_ge(xcl, 2 * b + 2)
                for r in range(4):
                    g = s.g0 + 4 * b + r
                    begin(g)
                    for k in range(2):
                        w0 = (r // 2) * 512 + k * 256 + (r % 2) * P
                        wc = slice(w0, w0 + P)
                        for wt, x in ((whi, XH), (whi, XL), (wlo, XH)):
                            for hf in range(2):
                                ins = T.matmul(ps(g)[:, hf, 0:HT], wt[gc % 2][:, wc], x[:, 2 * b + k, hf],
                                               start=(k == 0 and wt is whi and x is XH), stop=(k == 1 and wt is wlo))
                    done(ins)
            for c in range(st["oing"].n):
                products(st["oing"], c, UH, UL)
            pe.wait_ge(hs_ready, KR)
            for i, key in enumerate(("osA", "osB")):
                g = use[key]
                begin(g)
                for k in range(8 if i == 0 else 2):
                    ins = T.transpose(ps(g)[0:20].rearrange("p a (b c) -> p (a b) c", c=P)[:, k], OS[:, 8 * i + k], ident)
                done(ins)
            gemm("oout", YH, YL, ylo_ready, 0)
            ln_sums(2)
            ffn(1)
            for tb in range(4):
                begin(use[("ty", tb)])
            for k in range(KD):
                pe.wait_ge(x_ready, 24 + k + 1)
                for tb in range(4):
                    g = use[("ty", tb)]
                    off = (tb % 2) * P
                    ins = T.transpose(ps(g)[:].rearrange("p a (b c) -> p (a b) c", c=P)[:, k], xT[:, k, tb // 2, off:off + P], ident)
                    if k == KD - 1:
                        done(ins)
            g = use["tys"]
            begin(g)
            pe.wait_ge(for_pe, 13)
            for k in range(KD):
                ins = T.transpose(ps(g)[0:NS].rearrange("p a (b c) -> p (a b) c", c=P)[:, k], xsm[:, k], ident)
            done(ins)


_OUTS = [
    ("y_prompt", (1, 512, 1024)), ("y_sample", (8, 1, 1024)), ("k_prompt", (1, 1, 4, 128, 4, 2, 64)),
    ("v_prompt", (1, 1, 4, 128, 4, 128)), ("k_sample", (1, 8, 1, 4, 2, 64)), ("v_sample", (1, 8, 1, 4, 128)),
    ("C_prompt", (1, 1, 4, 128, 64)), ("n_prompt", (1, 1, 4, 64)), ("m_prompt", (1, 1, 4)),
    ("C_sample", (1, 8, 4, 128, 64)), ("n_sample", (1, 8, 4, 64)), ("m_sample", (1, 8, 4)),
    ("h_prompt", (1, 1, 1280)), ("conv_prompt", (1, 1, 3, 1280)), ("h_sample", (1, 8, 1280)),
    ("conv_sample", (1, 8, 3, 1280)),
]


def kernel(**inputs):
    import concourse.bacc as _bacc
    from concourse.bass_utils import run_bass_kernel_spmd as _run

    nc = _bacc.Bacc("TRN2", target_bir_lowering=False, num_devices=1)
    arrays, ins = {}, {}
    for name, value in list(inputs.items()) + [("consts", constants())]:
        arr = np.ascontiguousarray(value)
        arrays[f"in_{name}"] = arr
        ins[name] = nc.dram_tensor(f"in_{name}", arr.shape, mybir.dt.from_np(arr.dtype), kind="ExternalInput").ap()
    outs = {n: nc.dram_tensor(f"out_{n}", shape, F32, kind="ExternalOutput").ap() for n, shape in _OUTS}
    trunk(nc, ins, outs)
    r = _run(nc, [arrays], core_ids=[0])
    return tuple(r.results[0][f"out_{n}"] for n, _ in _OUTS)
```
